# Optimizing a Trainium2 kernel written in Bass

```python
import jax, jax.numpy as jnp
from jax import lax
import numpy as np

D_MODEL = 1024
BATCH = 1
SEQ = 256
DEPTH = 2

GROUP_HEADS = 4
HEAD_DIM = 64
GROUP_WIDTH = GROUP_HEADS * HEAD_DIM
N_GROUPS = 4
D_MIX = N_GROUPS * GROUP_WIDTH
BLOCK = 128
RET_CHUNK = 128
MLA_Q_RANK = 256
MLA_KV_RANK = 128
MLA_NOPE = 64
MLA_ROPE = 32
MLA_V = 64
ROPE_BASE = 10000.0
FORGET_BIAS_INIT = 4.0
PEER_HEADS = 8
PEER_KEYS = 128
PEER_EXPERTS = PEER_KEYS * PEER_KEYS
PEER_HALF = 128
PEER_QDIM = 2 * PEER_HALF
PEER_TOPK = 16
PEER_CHUNK = 128
EPS = 1e-6
IN_SPLITS = (GROUP_WIDTH,) * 4 + (GROUP_WIDTH,) * 3 + (GROUP_HEADS,) + (GROUP_WIDTH,) * 3 + (MLA_Q_RANK, MLA_KV_RANK, MLA_ROPE)
D_IN = sum(IN_SPLITS)

kernel_name = 'hybrid_ret_fox_sb_mla_peer'

def rms_norm(x, g):
    xf = x.astype(jnp.float32)
    y = xf * lax.rsqrt(jnp.mean(xf * xf, axis=-1, keepdims=True) + EPS)
    return (y * g.astype(jnp.float32)).astype(x.dtype)

def rope_tables(seq, dim):
    pos = jnp.arange(seq, dtype=jnp.float32)
    inv = ROPE_BASE ** (-jnp.arange(0, dim, 2, dtype=jnp.float32) / dim)
    ang = pos[:, None] * inv[None, :]
    return jnp.cos(ang), jnp.sin(ang)

def apply_rope(t, cos, sin):
    t1, t2 = jnp.split(t.astype(jnp.float32), 2, axis=-1)
    return jnp.concatenate([t1 * cos - t2 * sin, t1 * sin + t2 * cos], axis=-1)

def split_heads(t, n):
    b, s, _ = t.shape
    return t.reshape(b, s, n, -1).transpose(0, 2, 1, 3)

def head_norm(o, g, center):
    o = o.astype(jnp.float32)
    if center:
        o = o - jnp.mean(o, axis=-1, keepdims=True)
    o = o * lax.rsqrt(jnp.mean(o * o, axis=-1, keepdims=True) + EPS)
    b, h, s, d = o.shape
    return o.transpose(0, 2, 1, 3).reshape(b, s, h * d) * g.astype(jnp.float32)

def retention_chunkwise(q, k, v):
    b, h, s, d = q.shape
    dv = v.shape[-1]
    n = s // RET_CHUNK
    log_gamma = jnp.log1p(-(2.0 ** (-5.0 - jnp.arange(h, dtype=jnp.float32))))
    i = jnp.arange(RET_CHUNK, dtype=jnp.float32)
    rel = i[:, None] - i[None, :]
    intra = jnp.where(rel >= 0, jnp.exp(log_gamma[:, None, None] * jnp.maximum(rel, 0.0)), 0.0)
    q_decay = jnp.exp(log_gamma[:, None] * (i + 1.0))[:, :, None]
    k_decay = jnp.exp(log_gamma[:, None] * (RET_CHUNK - 1.0 - i))[:, :, None]
    chunk_decay = jnp.exp(log_gamma * RET_CHUNK)[:, None, None]

    def chunks(t):
        return t.astype(jnp.float32).reshape(b, h, n, RET_CHUNK, -1).transpose(2, 0, 1, 3, 4)

    def step(state, inp):
        qi, ki, vi = inp
        inner = jnp.einsum('bhid,bhjd->bhij', qi, ki) * intra
        out = jnp.einsum('bhij,bhjv->bhiv', inner, vi) + jnp.einsum('bhid,bhdv->bhiv', qi * q_decay, state)
        state = state * chunk_decay + jnp.einsum('bhjd,bhjv->bhdv', ki * k_decay, vi)
        return state, out

    state0 = jnp.zeros((b, h, d, dv), jnp.float32)
    _, out = lax.scan(step, state0, (chunks(q), chunks(k), chunks(v)))
    return out.transpose(1, 2, 0, 3, 4).reshape(b, h, s, dv)

def block_softmax_attention(q, k, v, scale, fcum=None):
    b, h, s, dk = q.shape
    n = s // BLOCK
    kf = k.astype(jnp.float32)
    vf = v.astype(jnp.float32)
    key_pos = jnp.arange(s)
    q_blocks = q.astype(jnp.float32).reshape(b, h, n, BLOCK, dk).transpose(2, 0, 1, 3, 4)
    xs = (jnp.arange(n), q_blocks)
    if fcum is not None:
        xs = xs + (fcum.reshape(b, h, n, BLOCK).transpose(2, 0, 1, 3),)

    def one_block(args):
        blk, qi = args[0], args[1]
        logits = jnp.einsum('bhqd,bhkd->bhqk', qi, kf) * scale
        if fcum is not None:
            logits = logits + args[2][..., :, None] - fcum[..., None, :]
        q_pos = blk * BLOCK + jnp.arange(BLOCK)
        logits = jnp.where(key_pos[None, :] <= q_pos[:, None], logits, -jnp.inf)
        p = jax.nn.softmax(logits, axis=-1)
        return jnp.einsum('bhqk,bhkv->bhqv', p, vf)

    out = lax.map(one_block, xs)
    return out.transpose(1, 2, 0, 3, 4).reshape(b, h, s, -1)

def stick_breaking_attention(q, k, v, scale):
    b, h, s, dk = q.shape
    n = s // BLOCK
    kf = k.astype(jnp.float32)
    vf = v.astype(jnp.float32)
    key_pos = jnp.arange(s)
    q_blocks = q.astype(jnp.float32).reshape(b, h, n, BLOCK, dk).transpose(2, 0, 1, 3, 4)

    def one_block(args):
        blk, qi = args
        z = jnp.einsum('bhqd,bhkd->bhqk', qi, kf) * scale
        q_pos = blk * BLOCK + jnp.arange(BLOCK)
        strict = key_pos[None, :] < q_pos[:, None]
        log_rest = jnp.where(strict, jax.nn.log_sigmoid(-z), 0.0)
        after = lax.cumsum(log_rest, axis=3, reverse=True) - log_rest
        w = jnp.where(strict, jnp.exp(jax.nn.log_sigmoid(z) + after), 0.0)
        return jnp.einsum('bhqk,bhkv->bhqv', w, vf)

    out = lax.map(one_block, (jnp.arange(n), q_blocks))
    return out.transpose(1, 2, 0, 3, 4).reshape(b, h, s, -1)

def latent_attention(cq_raw, ckv_raw, kr_raw, norm_cq, norm_ckv, w_uq, w_ukv, cos, sin):
    c_q = rms_norm(cq_raw, norm_cq)
    q = split_heads(c_q @ w_uq, GROUP_HEADS)
    q_nope, q_rope = q[..., :MLA_NOPE], q[..., MLA_NOPE:]
    c_kv = rms_norm(ckv_raw, norm_ckv)
    kv = split_heads(c_kv @ w_ukv, GROUP_HEADS)
    k_nope, v = kv[..., :MLA_NOPE], kv[..., MLA_NOPE:]
    k_rope = apply_rope(kr_raw[:, None], cos, sin)
    q_full = jnp.concatenate([q_nope.astype(jnp.float32), apply_rope(q_rope, cos, sin)], axis=-1)
    k_full = jnp.concatenate([k_nope.astype(jnp.float32), jnp.broadcast_to(k_rope, k_nope.shape[:-1] + (MLA_ROPE,))], axis=-1)
    return block_softmax_attention(q_full, k_full, v, (MLA_NOPE + MLA_ROPE) ** -0.5)

def hybrid_mixer(h, w_in, b_forget, norm_cq, norm_ckv, w_uq, w_ukv, head_gain, w_out, rope64, rope32):
    proj = h @ w_in
    (rq, rk, rv, rg, fq, fk, fv, ff, sq, sk, sv, cq, ckv, kr) = jnp.split(proj, np.cumsum(IN_SPLITS)[:-1].tolist(), axis=-1)
    cos64, sin64 = rope64
    cos32, sin32 = rope32
    gw = GROUP_WIDTH
    q_a = apply_rope(split_heads(rq, GROUP_HEADS), cos64, sin64)
    k_a = apply_rope(split_heads(rk, GROUP_HEADS), cos64, sin64) * HEAD_DIM ** -0.5
    o_a = retention_chunkwise(q_a, k_a, split_heads(rv, GROUP_HEADS))
    y_a = head_norm(o_a, head_gain[0:gw], True) * jax.nn.silu(rg.astype(jnp.float32))
    log_f = jax.nn.log_sigmoid(ff.astype(jnp.float32) + b_forget.astype(jnp.float32))
    fcum = jnp.cumsum(log_f, axis=1).transpose(0, 2, 1)
    o_b = block_softmax_attention(split_heads(fq, GROUP_HEADS), split_heads(fk, GROUP_HEADS), split_heads(fv, GROUP_HEADS), HEAD_DIM ** -0.5, fcum)
    y_b = head_norm(o_b, head_gain[gw:2 * gw], False)
    o_c = stick_breaking_attention(split_heads(sq, GROUP_HEADS), split_heads(sk, GROUP_HEADS), split_heads(sv, GROUP_HEADS), HEAD_DIM ** -0.5)
    y_c = head_norm(o_c, head_gain[2 * gw:3 * gw], False)
    o_d = latent_attention(cq, ckv, kr, norm_cq, norm_ckv, w_uq, w_ukv, cos32, sin32)
    y_d = head_norm(o_d, head_gain[3 * gw:4 * gw], False)
    y = jnp.concatenate([y_a, y_b, y_c, y_d], axis=-1).astype(h.dtype)
    return y @ w_out

def peer_ffn(h, w_query, sub_keys, expert_u, expert_v):
    b, s, d = h.shape
    t = b * s
    ht = h.reshape(t, d)
    q = (ht @ w_query).astype(jnp.float32).reshape(t, PEER_HEADS, 2, PEER_HALF)
    scores = jnp.einsum('thpc,hpnc->thpn', q, sub_keys.astype(jnp.float32))
    top_s, top_i = lax.top_k(scores, PEER_TOPK)
    kk = PEER_TOPK * PEER_TOPK
    cand_s = (top_s[:, :, 0, :, None] + top_s[:, :, 1, None, :]).reshape(t, PEER_HEADS, kk)
    cand_e = (top_i[:, :, 0, :, None] * PEER_KEYS + top_i[:, :, 1, None, :]).reshape(t, PEER_HEADS, kk)
    best_s, best_pos = lax.top_k(cand_s, PEER_TOPK)
    experts = jnp.take_along_axis(cand_e, best_pos, axis=-1)
    gates = jax.nn.softmax(best_s, axis=-1)
    n = t // PEER_CHUNK
    xs = (ht.reshape(n, PEER_CHUNK, d),
          experts.reshape(n, PEER_CHUNK, PEER_HEADS * PEER_TOPK),
          gates.reshape(n, PEER_CHUNK, PEER_HEADS * PEER_TOPK))

    def one_chunk(args):
        xi, ei, gi = args
        act = jax.nn.gelu(jnp.einsum('cd,ckd->ck', xi, expert_u[ei]).astype(jnp.float32), approximate=False)
        return jnp.einsum('ck,ckd->cd', (gi * act).astype(xi.dtype), expert_v[ei])

    return lax.map(one_chunk, xs).reshape(b, s, d)

def setup_inputs(seed: int = 0) -> dict:
    key = jax.random.key(seed)
    ks = jax.random.split(key, 16)
    f32 = jnp.float32

    def normal(k, shape, scale):
        return jax.random.normal(k, shape, f32) * scale

    def gain(k, shape):
        return 1.0 + 0.02 * jax.random.normal(k, shape, f32)

    return {
        'x': normal(ks[0], (BATCH, SEQ, D_MODEL), 1.0),
        'norm_mix': gain(ks[1], (DEPTH, D_MODEL)),
        'w_in': normal(ks[2], (DEPTH, D_MODEL, D_IN), D_MODEL ** -0.5),
        'b_forget': FORGET_BIAS_INIT + 0.5 * jax.random.normal(ks[3], (DEPTH, GROUP_HEADS), f32),
        'norm_cq': gain(ks[4], (DEPTH, MLA_Q_RANK)),
        'norm_ckv': gain(ks[5], (DEPTH, MLA_KV_RANK)),
        'w_uq': normal(ks[6], (DEPTH, MLA_Q_RANK, GROUP_HEADS * (MLA_NOPE + MLA_ROPE)), MLA_Q_RANK ** -0.5),
        'w_ukv': normal(ks[7], (DEPTH, MLA_KV_RANK, GROUP_HEADS * (MLA_NOPE + MLA_V)), MLA_KV_RANK ** -0.5),
        'head_gain': gain(ks[8], (DEPTH, D_MIX)),
        'w_out': normal(ks[9], (DEPTH, D_MIX, D_MODEL), D_MIX ** -0.5),
        'norm_ffn': gain(ks[10], (DEPTH, D_MODEL)),
        'w_query': normal(ks[11], (DEPTH, D_MODEL, PEER_HEADS * PEER_QDIM), D_MODEL ** -0.5),
        'sub_keys': normal(ks[12], (DEPTH, PEER_HEADS, 2, PEER_KEYS, PEER_HALF), PEER_HALF ** -0.5),
        'expert_u': normal(ks[13], (DEPTH, PEER_EXPERTS, D_MODEL), D_MODEL ** -0.5),
        'expert_v': normal(ks[14], (DEPTH, PEER_EXPERTS, D_MODEL), PEER_HEADS ** -0.5),
        'norm_final': gain(ks[15], (D_MODEL,)),
    }

def reference(x, norm_mix, w_in, b_forget, norm_cq, norm_ckv, w_uq, w_ukv, head_gain, w_out,
              norm_ffn, w_query, sub_keys, expert_u, expert_v, norm_final):
    seq = x.shape[1]
    rope64 = rope_tables(seq, HEAD_DIM)
    rope32 = rope_tables(seq, MLA_ROPE)
    for l in range(DEPTH):
        h = rms_norm(x, norm_mix[l])
        x = x + hybrid_mixer(h, w_in[l], b_forget[l], norm_cq[l], norm_ckv[l], w_uq[l], w_ukv[l],
                             head_gain[l], w_out[l], rope64, rope32)
        h = rms_norm(x, norm_ffn[l])
        x = x + peer_ffn(h, w_query[l], sub_keys[l], expert_u[l], expert_v[l])
    return rms_norm(x, norm_final)


_drawn_inputs = setup_inputs


def setup_inputs(seed=0):
    import zlib

    import numpy as np

    out = dict(_drawn_inputs(seed))
    spreads = {}
    factors = {'norm_cq': 3.09, 'norm_final': 2.886}
    for name, (base, spread) in spreads.items():
        noise = np.random.default_rng([zlib.crc32(name.encode()), seed]).standard_normal(out[name].shape)
        drawn = base * np.exp(spread * noise) if base else spread * noise
        out[name] = __import__('jax').numpy.asarray(drawn.astype(out[name].dtype))
    for name, factor in factors.items():
        out[name] = (out[name] * factor).astype(out[name].dtype)
    return out
```

```python
from contextlib import ExitStack

import numpy as np

import concourse.bass as bass
from concourse import mybir

F32 = mybir.dt.float32
F32R = mybir.dt.float32r
U32 = mybir.dt.uint32
ACT = mybir.ActivationFunctionType
ALU = mybir.AluOpType
AX_X = mybir.AxisListType.X

P = 128
D_MODEL = 1024
SEQ = 256
DEPTH = 2
HEADS = 4
HEAD_DIM = 64
GROUP_WIDTH = HEADS * HEAD_DIM
MLA_Q_RANK = 256
MLA_KV_RANK = 128
MLA_ROPE = 32
MLA_QK = HEAD_DIM + MLA_ROPE
PEER_HEADS = 8
PEER_KEYS = 128
TOPK = 16
EPS = 1e-6
ROPE_BASE = 10000.0
SCALE = HEAD_DIM ** -0.5
SCALE_MLA = MLA_QK ** -0.5

T = SEQ // P
KT = D_MODEL // P
CHUNK = KT * P
E_TILES = PEER_KEYS
C_WIDE1, C_TALL, C_WIDE2, C_OUT, C_QUERY, C_U = 0, 8, 16, 24, 32, 48
C_V = C_U + E_TILES
CHUNKS = C_V + E_TILES
PAIRS = CHUNKS // 2

BLK = 3 * P

FV, SV, CQ, CKV, KR, FF = 0, 256, 512, 768, 896, 928
NEG_BIG = -1e30
NEG_OUT = -3.0e38

ACT_STEPS, DVE_STEPS, ROUTE_STEPS = 12, 43, 19

G_MIX, G_HEAD, G_FFN, G_CQ, G_CKV, G_BF, GAINS = 0, 8, 16, 24, 26, 27, 31
W_UQ, W_UKV, W_KEYS, SMALL = 0, 768, 1280, 1280 + 16 * PEER_KEYS


def constants():
    i = np.arange(P, dtype=np.float32)
    k, q = i[:, None], i[None, :]
    tri_ge = (k >= q).astype(np.float32)
    tri_le = (k <= q).astype(np.float32)
    ones = np.ones((P, P), np.float32)
    gamma = np.log1p(-(2.0 ** (-5.0 - np.arange(HEADS, dtype=np.float32))))
    decay = np.zeros((P, HEADS, BLK), np.float32)
    for h in range(HEADS):
        near = np.where(q >= k, np.exp(gamma[h] * np.maximum(q - k, 0.0)), 0.0)
        far = np.exp(gamma[h] * (q + P - k))
        decay[:, h] = np.concatenate([near, far, near], 1) * SCALE
    late = np.where(k >= q, 0.0, NEG_BIG)
    causal = np.concatenate([late, 0 * late, late], 1)
    strict = np.concatenate([(k < q), np.ones((P, P), bool), (k < q)], 1)
    pos = np.arange(SEQ, dtype=np.float32)

    def rope(dim):
        inv = ROPE_BASE ** (-np.arange(0, dim, 2, dtype=np.float32) / dim)
        ang = (pos[:, None] * inv[None, :]).astype(np.float32)
        cos, sin = np.cos(ang), np.sin(ang)
        table = np.stack([np.concatenate([cos, cos], 1), np.concatenate([-sin, sin], 1)])
        return table.reshape(2, T, P, dim).transpose(2, 0, 1, 3).reshape(P, -1)

    pick = np.zeros((P, HEADS), np.float32)
    for h in range(HEADS):
        pick[h, h] = pick[HEADS + h, h] = 1.0
    return {
        "tri_ge": tri_ge, "tri_le": tri_le, "ones": ones, "decay": decay.reshape(P, -1),
        "causal": causal, "strict": strict, "rope64": rope(HEAD_DIM), "rope32": rope(MLA_ROPE),
        "pick": pick,
    }


MIXER_CONSTS = [("tri_ge", P), ("tri_le", P), ("ones", P), ("decay", HEADS * BLK), ("causal", BLK),
                ("strict", BLK), ("rope64", 2 * T * HEAD_DIM), ("rope32", 2 * T * MLA_ROPE), ("pick", HEADS)]
MIXER_CONST_COLS = sum(n for _, n in MIXER_CONSTS)


def hybrid_ret_fox_sb_mla_peer(nc, x, stream, gains, small, mixer_consts, fixed_consts, gain_final, out):
    with ExitStack() as ctx:
        def sb(name, shape, dt=F32):
            return ctx.enter_context(nc.sbuf_tensor(name, shape, dt))

        class Count:
            def __init__(self, name, per, first=0):
                self.sem, self.per, self.first = ctx.enter_context(nc.semaphore(name)), per, first

            def at(self, l, n):
                return l * self.per + (self.first + n)

        raw = sb("raw", [P, 4, CHUNK])
        head = sb("head", [P, 2, CHUNK], F32R)
        rest = sb("rest", [P, 2, CHUNK], F32R)
        xs = sb("xs", [P, T, D_MODEL])
        arena = sb("arena", [P, (E_TILES + 1) * SEQ])
        gain = sb("gain", [P, GAINS])
        fixed = sb("fixed", [P, 2 * P])
        ident, iota = fixed[:, 0:P], fixed[:, P:2 * P]
        picked = sb("picked", [P, 3, T, PEER_HEADS * TOPK])
        ss = sb("ss", [P, 2, T])
        css = sb("css", [P, 2, 2, T])
        hss = sb("hss", [P, 2, 32])
        gs = sb("gs", [P, 2, T, PEER_HEADS])
        top_v = sb("top_v", [P, 2, TOPK])
        top_i = sb("top_i", [P, 2, TOPK], U32)
        top_f = sb("top_f", [P, 2, TOPK])
        left = sb("left", [P, TOPK * TOPK])
        cand = sb("cand", [P, TOPK * TOPK])
        best_v = sb("best_v", [P, TOPK])
        best_i = sb("best_i", [P, TOPK], U32)
        rank_i = sb("rank_i", [P, 2, TOPK], U32)
        rank_f = sb("rank_f", [P, 2, TOPK])
        match = sb("match", [P, 2, TOPK * TOPK])

        with nc.sbuf_tensor("act_head", [P, KT, SEQ], F32R) as act_head, \
                nc.sbuf_tensor("act_rest", [P, KT, SEQ], F32R) as act_rest:
            pass
        picked_t = sb("picked_t", [P, 3, SEQ])
        hot1 = sb("hot1", [P, 8, P])
        hot2 = sb("hot2", [P, 8, P])
        w_head = sb("w_head", [P, 2, SEQ], F32R)
        w_rest = sb("w_rest", [P, 2, SEQ], F32R)
        sb("rest_of_act", [P, 256])

        used = [0]

        def carve(n):
            used[0] += n
            assert used[0] <= E_TILES * SEQ, used[0]
            return arena[:, used[0] - n:used[0]]

        xn = carve(T * D_MODEL).rearrange("p (t d) -> p t d", t=T)
        wt = [carve(HEADS * BLK).rearrange("p (h n) -> p h n", h=HEADS) for _ in range(4)]
        consts = carve(MIXER_CONST_COLS)
        at, c = 0, {}
        for name, n in MIXER_CONSTS:
            c[name] = consts[:, at:at + n]
            at += n
        smalls = carve(SMALL)
        w_uq = smalls[:, W_UQ:W_UKV].rearrange("p (r n) -> p r n", r=2)
        w_ukv = smalls[:, W_UKV:W_KEYS]
        keys_t = smalls[:, W_KEYS:SMALL].rearrange("p (m n) -> p m n", n=PEER_KEYS)
        rot = carve(T * 512).rearrange("p (t n) -> p t n", t=T)
        ret_t = carve(4 * SEQ).rearrange("p (j s) -> p j s", s=SEQ)
        rv = carve(T * GROUP_WIDTH).rearrange("p (t n) -> p t n", t=T)
        rg = carve(T * GROUP_WIDTH).rearrange("p (t n) -> p t n", t=T)
        fs_t = carve(8 * SEQ).rearrange("p (j s) -> p j s", s=SEQ)
        g2 = carve(T * D_MODEL).rearrange("p (t n) -> p t n", t=T)
        lf = carve(2 * T * HEADS).rearrange("p (a t h) -> p a t h", a=2, t=T)
        fc = carve(T * 16).rearrange("p (t n) -> p t n", t=T)
        fc_t = carve(2 * SEQ)
        fc_h = carve(HEADS * SEQ).rearrange("p (h s) -> p h s", h=HEADS)
        cn = carve(T * 384).rearrange("p (t n) -> p t n", t=T)
        c_at = used[0]
        c_t = carve(3 * SEQ).rearrange("p (j s) -> p j s", s=SEQ)
        mla_q = carve(T * HEADS * MLA_QK).rearrange("p (t h n) -> p t h n", t=T, h=HEADS)
        mla_k = carve(T * HEADS * MLA_QK).rearrange("p (t h n) -> p t h n", t=T, h=HEADS)
        mla_v = carve(T * GROUP_WIDTH).rearrange("p (t h n) -> p t h n", t=T, h=HEADS)
        krot = carve(T * MLA_ROPE).rearrange("p (t n) -> p t n", t=T)
        spare = carve(2 * 512)
        zs = carve(HEADS * BLK).rearrange("p (h n) -> p h n", h=HEADS)
        za = carve(HEADS * BLK).rearrange("p (h n) -> p h n", h=HEADS)
        soft = carve(HEADS * BLK).rearrange("p (h n) -> p h n", h=HEADS)
        mx = carve(4 * HEADS * T).rearrange("p (a t h) -> p a t h", a=4, t=T)
        dn = carve(4 * HEADS * T).rearrange("p (a t h) -> p a t h", a=4, t=T)
        mean = carve(2 * HEADS * T).rearrange("p (a n) -> p a n", a=2)
        scratch = wt[1].rearrange("p h n -> p (h n)")[:, 0:D_MODEL]
        qd_t = rot.rearrange("p t n -> p (t n)").rearrange("p (h s) -> p h s", h=HEADS)
        kd_t = ret_t
        ya = arena[:, c_at:c_at + 4 * T * GROUP_WIDTH].rearrange("p (g n) -> p g n", g=4)
        ysq = fs_t.rearrange("p j s -> p (j s)").rearrange("p (g n) -> p g n", g=4)
        query_t = arena[:, T * D_MODEL:T * D_MODEL + 16 * SEQ].rearrange("p (m s) -> p m s", s=SEQ)
        assert 16 * SEQ <= 4 * HEADS * BLK

        acts = arena[:, 0:E_TILES * SEQ].rearrange("p (i s) -> p i s", s=SEQ)
        SCORE_SLOT = E_TILES + 1 - T * PEER_HEADS

        def scores(unit):
            return arena[:, bass.ds((unit + SCORE_SLOT) * SEQ, SEQ)]

        acc = [ctx.enter_context(nc.psum_tensor(f"acc{i}", [P, 512], F32)) for i in range(4)]
        work = [ctx.enter_context(nc.psum_tensor(f"work{i}", [P, 512], F32)) for i in range(4)]

        raw_in = [Count(f"raw_in{i}", 16 * PAIRS // 2) for i in range(2)]
        head_in = Count("head_in", CHUNKS)
        rest_in = Count("rest_in", CHUNKS, 2)
        head_free = Count("head_free", CHUNKS, 2)
        chunk_done = Count("chunk_done", CHUNKS, 2)
        TALLS = 4 + 8 + E_TILES // 2
        bank_free = Count("bank_free", TALLS, 4)
        fixed_in = Count("fixed_in", 0)
        x_in = Count("x_in", 0)
        small_in = Count("small_in", 48)
        x_ready = Count("x_ready", 1, 1)
        x_mid = Count("x_mid", 1)
        std_ready = Count("std_ready", 2)
        xn_ready = Count("xn_ready", 3)
        turned = Count("turned", 12)
        act_head_in = Count("act_head_in", 12)
        act_rest_in = Count("act_rest_in", 12)
        rot_ready = Count("rot_ready", 1)
        rv_ready = Count("rv_ready", 1)
        ret_turned = Count("ret_turned", 1)
        ret_t_ready = Count("ret_t_ready", 1)
        g2_act = Count("g2_act", 1)
        g2_dve = Count("g2_dve", 1)
        cstd_ready = Count("cstd_ready", 1)
        cn_ready = Count("cn_ready", 1)
        c_turned = Count("c_turned", 1)
        c_t_ready = Count("c_t_ready", 1)
        mla_out = Count("mla_out", 1)
        krot_ready = Count("krot_ready", 1)
        mla_q_ready = Count("mla_q_ready", 1)
        mla_kv_ready = Count("mla_kv_ready", 1)
        mla_turned = Count("mla_turned", 1)
        mla_t_ready = Count("mla_t_ready", 1)
        ff_ready = Count("ff_ready", 1)
        ffl_ready = Count("ffl_ready", 1)
        ls_ready = Count("ls_ready", 1)
        fcum_out = Count("fcum_out", 1)
        fc_ready = Count("fc_ready", 1)
        fc_turned = Count("fc_turned", 1)
        fc_t_ready = Count("fc_t_ready", 1)
        sa_out = Count("sa_out", HEADS)
        wa_ready = Count("wa_ready", HEADS)
        sc_out = Count("sc_out", HEADS)
        zs_ready = Count("zs_ready", HEADS)
        lc_ready = Count("lc_ready", 1)
        sp_ready = Count("sp_ready", 1)
        cum_out = Count("cum_out", HEADS)
        logw_ready = Count("logw_ready", HEADS)
        ew_ready = Count("ew_ready", 1)
        wc_ready = Count("wc_ready", 1)
        soft_out = Count("soft_out", 2 * HEADS)
        soft_max = Count("soft_max", 2 * HEADS)
        soft_exp = Count("soft_exp", 2 * HEADS)
        soft_turned = Count("soft_turned", 2 * HEADS)
        soft_t_ready = Count("soft_t_ready", 2 * HEADS)
        o_out = Count("o_out", 4)
        hss_ready = Count("hss_ready", 1)
        hstd_ready = Count("hstd_ready", 1)
        score_out = Count("score_out", 8)
        score_in = Count("score_in", 8)
        UNITS = T * PEER_HEADS
        unit_done = Count("unit_done", UNITS, 1)
        gate_ready = Count("gate_ready", 1)
        gate_exp = Count("gate_exp", 1)
        gates_done = Count("gates_done", 1)
        picked_turned = Count("picked_turned", 1)
        GROUPS = SEQ // 4
        hot_ready = Count("hot_ready", GROUPS)
        gate_out = Count("gate_out", GROUPS)
        gate_used = Count("gate_used", GROUPS, 2)
        w_head_in = Count("w_head_in", E_TILES)
        w_rest_in = Count("w_rest_in", E_TILES, 2)
        out_done = Count("out_done", 0)
        act_step = Count("act_step", ACT_STEPS)
        dve_step = Count("dve_step", DVE_STEPS)
        route_step = Count("route_step", UNITS * ROUTE_STEPS)

        class Steps:

            def __init__(self, eng, count, l):
                self.eng, self.count, self.l, self.n = eng, count, l, 0

            def __call__(self, ins):
                ins.then_inc(self.count.sem, 1)
                self.n += 1
                self.eng.wait_ge(self.count.sem, self.count.at(self.l, self.n))

        passed = ctx.enter_context(nc.semaphore("passed"))

        def after_register_wait(eng):
            eng.sem_inc(passed, 1)

        block = ctx.enter_context(nc.Block())

        @block.sync
        def _(sp):
            def load(pair, slot):
                sp.dma_start(raw[:, 2 * slot:2 * slot + 2, :], stream[pair]).then_inc(raw_in[slot].sem, 16)

            load(0, 0)
            load(1, 1)
            with sp.Fori(1, DEPTH * PAIRS // 2) as k:
                for slot in range(2):
                    sp.wait_ge(rest_in.sem, 4 * k + (2 * slot + rest_in.first - 2))
                    load(2 * k + slot, slot)
            for slot in range(2):
                sp.wait_ge(raw_in[slot].sem, 16 * DEPTH * PAIRS // 2)

        @block.gpsimd
        def _(pool):
            pool.dma_start(fixed[:], fixed_consts).then_inc(fixed_in.sem, 16)
            pool.dma_start(xs[:], x).then_inc(x_in.sem, 16)
            with pool.Fori(0, DEPTH) as l:
                pool.wait_ge(x_ready.sem, x_ready.at(l, 0))
                pool.dma_start(gain[:], gains[l]).then_inc(small_in.sem, 16)
                pool.dma_start(smalls, small[l]).then_inc(small_in.sem, 16)
                pool.dma_start(consts, mixer_consts).then_inc(small_in.sem, 16)
            pool.wait_ge(x_ready.sem, DEPTH + 1)
            pool.dma_start(arena[:, 0:D_MODEL], gain_final.to_broadcast([P, D_MODEL])).then_inc(fixed_in.sem, 16)

        @block.tensor
        def _(pe):
            mm = nc.tensor.matmul
            pe.sem_inc(head_free.sem, 2)
            pe.sem_inc(chunk_done.sem, 2)
            pe.wait_ge(fixed_in.sem, 16)

            def tall_block(l, c0, use0):
                for j in range(8):
                    s, bank = j % 2, work[j // 2]
                    o = bank[:, (j % 2) * SEQ:(j % 2 + 1) * SEQ]
                    if j % 2 == 0:
                        pe.wait_ge(bank_free.sem, bank_free.at(l, use0 + (j // 2 - 3)))
                    pe.wait_ge(head_in.sem, head_in.at(l, c0 + (j + 1)))
                    for kt in range(KT):
                        w = head[:, s, kt * P:(kt + 1) * P]
                        mm(o, w, act_head[:, kt, :], start=(kt == 0), stop=False)
                        ins = mm(o, w, act_rest[:, kt, :], start=False, stop=False)
                    ins.then_inc(head_free.sem, 1)
                    pe.wait_ge(rest_in.sem, rest_in.at(l, c0 + (j + 1)))
                    for kt in range(KT):
                        ins = mm(o, rest[:, s, kt * P:(kt + 1) * P], act_head[:, kt, :], start=False, stop=(kt == KT - 1))
                    ins.then_inc(chunk_done.sem, 1)

            def wide_chunk(l, cj, s, a_head, a_rest, first, last):
                pe.wait_ge(head_in.sem, head_in.at(l, cj + 1))
                for t in range(T):
                    for n in range(2):
                        mm(acc[2 * t + n][:], a_head(t), head[:, s, n * 512:(n + 1) * 512], start=first, stop=False)
                for t in range(T):
                    for n in range(2):
                        ins = mm(acc[2 * t + n][:], a_rest(t), head[:, s, n * 512:(n + 1) * 512], start=False, stop=False)
                ins.then_inc(head_free.sem, 1)
                pe.wait_ge(rest_in.sem, rest_in.at(l, cj + 1))
                for t in range(T):
                    for n in range(2):
                        ins = mm(acc[2 * t + n][:], a_head(t), rest[:, s, n * 512:(n + 1) * 512], start=False, stop=last)
                ins.then_inc(chunk_done.sem, 1)

            def wide(l, c0):
                for kt in range(KT):
                    wide_chunk(l, c0 + kt, kt % 2, lambda t: act_head[:, kt, t * P:(t + 1) * P],
                               lambda t: act_rest[:, kt, t * P:(t + 1) * P], kt == 0, kt == KT - 1)

            def turn(l, use):
                pe.wait_ge(xn_ready.sem, xn_ready.at(l, use + 1))
                for kt in range(KT):
                    for t in range(T):
                        ins = pe.transpose(work[kt // 2][:, (kt % 2) * SEQ + t * P:(kt % 2) * SEQ + (t + 1) * P],
                                           xn[:, t, kt * P:(kt + 1) * P], ident)
                    if kt % 2:
                        ins.then_inc(turned.sem, 1)
                pe.wait_ge(act_rest_in.sem, act_rest_in.at(l, 4 * use + 4))

            def keys_by_queries(o, k_t, q_t):
                mm(o[:, 0:SEQ], k_t[:, 0:P], q_t, start=True, stop=True)
                return mm(o[:, SEQ:BLK], k_t[:, P:SEQ], q_t[:, P:SEQ], start=True, stop=True)

            def weighted(g, w, v):
                for h in range(HEADS):
                    o = acc[g][:, h * HEAD_DIM:(h + 1) * HEAD_DIM]
                    mm(o, w[:, h, 0:P], v(0, h), start=True, stop=True)
                    o = acc[g][:, GROUP_WIDTH + h * HEAD_DIM:GROUP_WIDTH + (h + 1) * HEAD_DIM]
                    mm(o, w[:, h, P:SEQ], v(0, h), start=True, stop=False)
                    ins = mm(o, w[:, h, SEQ:BLK], v(1, h), start=False, stop=True)
                ins.then_inc(o_out.sem, 1)

            def rows(h):
                return slice((h % 2) * HEAD_DIM, (h % 2 + 1) * HEAD_DIM)

            with pe.Fori(0, DEPTH) as l:
                pe.wait_ge(x_ready.sem, x_ready.at(l, 0))
                turn(l, 0)
                wide(l, C_WIDE1)
                tall_block(l, C_TALL, 0)
                pe.wait_ge(rot_ready.sem, rot_ready.at(l, 1))
                pe.wait_ge(rv_ready.sem, rv_ready.at(l, 1))
                wide(l, C_WIDE2)

                pe.wait_ge(bank_free.sem, bank_free.at(l, 4))
                for j in range(4):
                    for t in range(T):
                        ins = pe.transpose(work[j // 2][:, (j % 2) * SEQ + t * P:(j % 2) * SEQ + (t + 1) * P],
                                           rot[:, t, j * P:(j + 1) * P], ident)
                ins.then_inc(ret_turned.sem, 1)
                pe.wait_ge(ret_t_ready.sem, ret_t_ready.at(l, 1))
                for h in range(HEADS):
                    keys_by_queries(work[h], ret_t[rows(h), 2 + h // 2, :], ret_t[rows(h), h // 2, :])\
                        .then_inc(sa_out.sem, 1)

                pe.wait_ge(g2_act.sem, g2_act.at(l, 1))
                pe.wait_ge(cn_ready.sem, cn_ready.at(l, 1))
                for j in range(3):
                    for t in range(T):
                        ins = pe.transpose(acc[2 + j // 2][:, (j % 2) * SEQ + t * P:(j % 2) * SEQ + (t + 1) * P],
                                           cn[:, t, j * P:(j + 1) * P], ident)
                ins.then_inc(c_turned.sem, 1)

                for h in range(HEADS):
                    pe.wait_ge(wa_ready.sem, wa_ready.at(l, h + 1))
                    keys_by_queries(work[h], fs_t[rows(h), 6 + h // 2, :], fs_t[rows(h), 4 + h // 2, :])\
                        .then_inc(sc_out.sem, 1)

                pe.wait_ge(ls_ready.sem, ls_ready.at(l, 1))
                pe.wait_ge(g2_dve.sem, g2_dve.at(l, 1))
                mm(acc[0][:, 0:HEADS], c["tri_le"], lf[:, 0, 0, :], start=True, stop=True)
                mm(acc[0][:, HEADS:2 * HEADS], c["tri_le"], lf[:, 0, 1, :], start=True, stop=False)
                mm(acc[0][:, HEADS:2 * HEADS], c["ones"], lf[:, 0, 0, :], start=False, stop=True).then_inc(fcum_out.sem, 1)
                pe.wait_ge(fc_ready.sem, fc_ready.at(l, 1))
                pe.wait_ge(zs_ready.sem, zs_ready.at(l, 1))
                for a in range(2):
                    for t in range(T):
                        ins = pe.transpose(work[0][0:8, a * SEQ + t * P:a * SEQ + (t + 1) * P],
                                           fc[:, t, 8 * a:8 * a + 8], ident)
                ins.then_inc(fc_turned.sem, 1)

                pe.wait_ge(c_t_ready.sem, c_t_ready.at(l, 1))
                for t in range(T):
                    mm(acc[t][:, 0:384], c_t[:, 0, t * P:(t + 1) * P], w_uq[:, 0, :], start=True, stop=False)
                    mm(acc[t][:, 0:384], c_t[:, 1, t * P:(t + 1) * P], w_uq[:, 1, :], start=False, stop=True)
                for t in range(T):
                    ins = mm(acc[2 + t][:], c_t[:, 2, t * P:(t + 1) * P], w_ukv, start=True, stop=True)
                ins.then_inc(mla_out.sem, 1)

                pe.wait_ge(sp_ready.sem, sp_ready.at(l, 1))
                pe.wait_ge(zs_ready.sem, zs_ready.at(l, HEADS))
                pe.wait_ge(fc_t_ready.sem, fc_t_ready.at(l, 1))
                for h in range(HEADS):
                    mm(work[h][:, 0:BLK], c["tri_ge"], za[:, h, :], start=True, stop=False)
                    mm(work[h][:, P:SEQ], c["ones"], za[:, h, SEQ:BLK], start=False, stop=True).then_inc(cum_out.sem, 1)

                pe.wait_ge(mla_q_ready.sem, mla_q_ready.at(l, 1))
                pe.wait_ge(mla_kv_ready.sem, mla_kv_ready.at(l, 1))
                for a, src in enumerate((mla_q, mla_k)):
                    for h in range(HEADS):
                        for t in range(T):
                            ins = pe.transpose(
                                acc[2 * a + h // 2][0:MLA_QK, (h % 2) * SEQ + t * P:(h % 2) * SEQ + (t + 1) * P],
                                src[:, t, h, :], ident)
                ins.then_inc(mla_turned.sem, 1)

                for h in range(HEADS):
                    q_t, k_t, o = fs_t[rows(h), h // 2, :], fs_t[rows(h), 2 + h // 2, :], work[h]
                    pe.wait_ge(logw_ready.sem, logw_ready.at(l, h + 1))
                    mm(o[:, 0:P], q_t[:, 0:P], k_t[:, 0:P], start=True, stop=False)
                    mm(o[:, 0:P], fc_h[0:8, h, 0:P], fc_t[0:8, SEQ:SEQ + P], start=False, stop=True)
                    mm(o[:, P:BLK], q_t[:, P:SEQ], k_t, start=True, stop=False)
                    mm(o[:, P:BLK], fc_h[0:8, h, P:SEQ], fc_t[0:8, SEQ:2 * SEQ], start=False, stop=True)\
                        .then_inc(soft_out.sem, 1)

                def turn_weights(base):
                    for h in range(HEADS):
                        pe.wait_ge(soft_exp.sem, soft_exp.at(l, base + h + 1))
                        for j in range(3):
                            ins = pe.transpose(work[h][:, j * P:(j + 1) * P], soft[:, h, j * P:(j + 1) * P], ident)
                        ins.then_inc(soft_turned.sem, 1)

                pe.wait_ge(mla_t_ready.sem, mla_t_ready.at(l, 1))
                weighted(0, wt[0], lambda t, h: rv[:, t, h * HEAD_DIM:(h + 1) * HEAD_DIM])
                turn_weights(0)
                pe.wait_ge(wc_ready.sem, wc_ready.at(l, 1))
                weighted(2, wt[2], lambda t, h: g2[:, t, SV + h * HEAD_DIM:SV + (h + 1) * HEAD_DIM])
                for h in range(HEADS):
                    pe.wait_ge(soft_t_ready.sem, soft_t_ready.at(l, h + 1))
                    mm(work[h][:, 0:P], qd_t[0:MLA_QK, h, 0:P], kd_t[0:MLA_QK, h, 0:P], start=True, stop=True)
                    mm(work[h][:, P:BLK], qd_t[0:MLA_QK, h, P:SEQ], kd_t[0:MLA_QK, h, :], start=True, stop=True)\
                        .then_inc(soft_out.sem, 1)
                weighted(1, wt[1], lambda t, h: g2[:, t, FV + h * HEAD_DIM:FV + (h + 1) * HEAD_DIM])
                turn_weights(HEADS)
                pe.wait_ge(soft_t_ready.sem, soft_t_ready.at(l, 2 * HEADS))
                weighted(3, wt[3], lambda t, h: mla_v[:, t, h, :])

                turn(l, 1)
                wide(l, C_OUT)

                turn(l, 2)
                after_register_wait(pe)
                with pe.Fori(0, 2) as half:
                    tall_block(l, C_QUERY + half * 8, 4 + half * 4)
                pe.wait_ge(bank_free.sem, bank_free.at(l, 4 + 8))
                for t in range(T):
                    for m4 in range(4):
                        if t:
                            pe.wait_ge(score_in.sem, score_in.at(l, m4 + 1))
                        for m in range(4):
                            ins = mm(work[m4][:, m * P:(m + 1) * P], query_t[:, 4 * m4 + m, t * P:(t + 1) * P],
                                     keys_t[:, 4 * m4 + m, :], start=True, stop=True)
                        ins.then_inc(score_out.sem, 1)
                pe.wait_ge(score_in.sem, score_in.at(l, 8))
                after_register_wait(pe)

                with pe.Fori(0, E_TILES // 8) as u:
                    tall_block(l, C_U + u * 8, 12 + u * 4)

                pe.wait_ge(bank_free.sem, bank_free.at(l, TALLS))
                pe.wait_ge(gates_done.sem, gates_done.at(l, 1))
                for a in range(3):
                    for t in range(T):
                        ins = pe.transpose(work[a // 2][:, (a % 2) * SEQ + t * P:(a % 2) * SEQ + (t + 1) * P],
                                           picked[:, a, t, :], ident)
                ins.then_inc(picked_turned.sem, 1)
                with pe.Fori(0, GROUPS // 2) as g:
                    for b in range(2):
                        pe.wait_ge(hot_ready.sem, hot_ready.at(l, 2 * g + (b + 1)))
                        pe.wait_ge(gate_used.sem, gate_used.at(l, 2 * g + (b - 1)))
                        for q in range(4):
                            ins = mm(work[2 + b][:, q * P:(q + 1) * P], hot2[:, 4 * b + q, :], hot1[:, 4 * b + q, :],
                                     start=True, stop=True)
                        ins.then_inc(gate_out.sem, 1)

                def v_block(i0, first, last):
                    for j in range(4):
                        pe.wait_ge(w_head_in.sem, w_head_in.at(l, i0 + (j + 1)))
                        pe.wait_ge(w_rest_in.sem, w_rest_in.at(l, i0 + (j + 1)))
                        wide_chunk(l, C_V + i0 + j, j % 2, lambda t: w_head[:, j % 2, t * P:(t + 1) * P],
                                   lambda t: w_rest[:, j % 2, t * P:(t + 1) * P], first and j == 0, last and j == 3)

                v_block(0, True, False)
                with pe.Fori(1, E_TILES // 4 - 1) as v:
                    v_block(4 * v, False, False)
                v_block(E_TILES - 4, False, True)

        @block.scalar
        def _(act):
            act.sem_inc(bank_free.sem, 4)

            def split_head(l, cj, slot, raw_slot):
                act.wait_ge(raw_in[raw_slot // 2].sem, raw_in[raw_slot // 2].at(l, 4 * (cj + (4 - raw_slot))))
                act.wait_ge(head_free.sem, head_free.at(l, cj - 1))
                act.wait_ge(rest_in.sem, rest_in.at(l, cj - 1))
                nc.scalar.copy(head[:, slot, :], raw[:, raw_slot, :]).then_inc(head_in.sem, 1)

            def ahead(l, c0, n, j0=0):
                for j in range(j0, j0 + n):
                    split_head(l, c0 + (j + 2), j % 2, (j + 2) % 4)

            def std(l, use, step):
                for t in range(T):
                    step(nc.scalar.activation(scratch, xs[:, t, :], ACT.Square, accum_out=ss[:, 0, t:t + 1]))
                nc.scalar.activation(ss[:, 1, :], ss[:, 0, :], ACT.Sqrt, scale=1.0 / D_MODEL, bias=eps)\
                    .then_inc(std_ready.sem, 1)

            def act_heads(l, use, g0):
                for b in range(4):
                    act.wait_ge(turned.sem, turned.at(l, 4 * use + b + 1))
                    for kt in (2 * b, 2 * b + 1):
                        ins = nc.scalar.activation(act_head[:, kt, :], work[b][:, (kt % 2) * SEQ:(kt % 2 + 1) * SEQ],
                                                   ACT.Copy, scale=gain[:, g0 + kt:g0 + kt + 1])
                    ins.then_inc(act_head_in.sem, 1)

            def weights_exp(l, base, n, scale):
                for h in range(HEADS):
                    act.wait_ge(soft_max.sem, soft_max.at(l, base + h + 1))
                    nc.scalar.activation(soft[:, h, 0:P], soft[:, h, 0:P], ACT.Exp, scale=scale,
                                         bias=mx[:, 2 * n + 1, 0, h:h + 1], accum_out=dn[:, 2 * n, 0, h:h + 1])
                    nc.scalar.activation(soft[:, h, P:BLK], soft[:, h, P:BLK], ACT.Exp, scale=scale,
                                         bias=mx[:, 2 * n + 1, 1, h:h + 1], accum_out=dn[:, 2 * n, 1, h:h + 1])\
                        .then_inc(soft_exp.sem, 1)

            def weights_t(l, base, dst):
                for h in range(HEADS):
                    act.wait_ge(soft_turned.sem, soft_turned.at(l, base + h + 1))
                    nc.scalar.copy(dst[:, h, :], work[h][:, 0:BLK]).then_inc(soft_t_ready.sem, 1)

            eps = EPS
            with act.Fori(0, DEPTH) as l:
                step = Steps(act, act_step, l)
                act.wait_ge(x_ready.sem, x_ready.at(l, 0))
                std(l, 0, step)
                for j in range(2):
                    split_head(l, j, j, j)
                act.wait_ge(small_in.sem, small_in.at(l, 48))
                act_heads(l, 0, G_MIX)
                ahead(l, C_WIDE1, 8)
                act.wait_ge(chunk_done.sem, chunk_done.at(l, C_TALL))
                for t in range(T):
                    nc.scalar.copy(rv[:, t, :], acc[2 * t + 1][:, 0:GROUP_WIDTH])
                for t in range(T):
                    ins = nc.scalar.activation(rg[:, t, :], acc[2 * t + 1][:, GROUP_WIDTH:512], ACT.Silu)
                ins.then_inc(rv_ready.sem, 1)
                for b in range(4):
                    ahead(l, C_TALL, 2, 2 * b)
                    act.wait_ge(chunk_done.sem, chunk_done.at(l, C_TALL + 2 * b + 2))
                    nc.scalar.copy(fs_t[:, 2 * b:2 * b + 2, :], work[b][:].rearrange("p (j s) -> p j s", s=SEQ))\
                        .then_inc(bank_free.sem, 1)
                ahead(l, C_WIDE2, 8)

                act.wait_ge(ret_turned.sem, ret_turned.at(l, 1))
                for b in range(2):
                    ins = nc.scalar.copy(ret_t[:, 2 * b:2 * b + 2, :], work[b][:].rearrange("p (j s) -> p j s", s=SEQ))
                ins.then_inc(ret_t_ready.sem, 1)
                act.wait_ge(chunk_done.sem, chunk_done.at(l, C_OUT))
                for n in range(2):
                    ins = nc.scalar.copy(g2[:, 0, n * 512:(n + 1) * 512], acc[n][:])
                ins.then_inc(g2_act.sem, 1)
                act.wait_ge(g2_dve.sem, g2_dve.at(l, 1))
                act.wait_ge(g2_act.sem, g2_act.at(l, 1))
                for a, (c0, n) in enumerate(((CQ, MLA_Q_RANK), (CKV, MLA_KV_RANK))):
                    for t in range(T):
                        step(nc.scalar.activation(scratch[:, 0:n], g2[:, t, c0:c0 + n], ACT.Square,
                                                  accum_out=css[:, 0, a, t:t + 1]))
                nc.scalar.activation(css[:, 1, 0, :], css[:, 0, 0, :], ACT.Sqrt, scale=1.0 / MLA_Q_RANK, bias=eps)
                nc.scalar.activation(css[:, 1, 1, :], css[:, 0, 1, :], ACT.Sqrt, scale=1.0 / MLA_KV_RANK, bias=eps)\
                    .then_inc(cstd_ready.sem, 1)
                for h in range(HEADS):
                    act.wait_ge(sc_out.sem, sc_out.at(l, h + 1))
                    nc.scalar.activation(zs[:, h, :], work[h][:, 0:BLK], ACT.Copy, scale=SCALE).then_inc(zs_ready.sem, 1)
                act.wait_ge(ff_ready.sem, ff_ready.at(l, 1))
                step(nc.scalar.activation(lf[:, 1, :, :], lf[:, 0, :, :], ACT.Abs))
                step(nc.scalar.activation(lf[:, 1, :, :], lf[:, 1, :, :], ACT.Exp, scale=-1.0))
                nc.scalar.activation(lf[:, 1, :, :], lf[:, 1, :, :], ACT.Ln, bias=1.0).then_inc(ffl_ready.sem, 1)
                act.wait_ge(c_turned.sem, c_turned.at(l, 1))
                for j in range(3):
                    ins = nc.scalar.activation(c_t[:, j, :], acc[2 + j // 2][:, (j % 2) * SEQ:(j % 2 + 1) * SEQ], ACT.Copy,
                                               scale=gain[:, G_CQ + j:G_CQ + j + 1])
                ins.then_inc(c_t_ready.sem, 1)
                act.wait_ge(zs_ready.sem, zs_ready.at(l, HEADS))
                step(nc.scalar.activation(za[:, :, :], zs[:, :, :], ACT.Abs))
                step(nc.scalar.activation(za[:, :, :], za[:, :, :], ACT.Exp, scale=-1.0))
                nc.scalar.activation(za[:, :, :], za[:, :, :], ACT.Ln, bias=1.0).then_inc(lc_ready.sem, 1)
                act.wait_ge(mla_out.sem, mla_out.at(l, 1))
                act.wait_ge(krot_ready.sem, krot_ready.at(l, 1))
                for t in range(T):
                    kv = acc[2 + t][:].rearrange("p (h n) -> p h n", h=HEADS)
                    nc.scalar.copy(mla_k[:, t, :, 0:HEAD_DIM], kv[:, :, 0:HEAD_DIM])
                    nc.scalar.copy(mla_v[:, t, :, :], kv[:, :, HEAD_DIM:])
                    ins = nc.scalar.copy(mla_k[:, t, :, HEAD_DIM:MLA_QK],
                                         krot[:, t:t + 1, :].to_broadcast([P, HEADS, MLA_ROPE]))
                ins.then_inc(mla_kv_ready.sem, 1)
                act.wait_ge(mla_turned.sem, mla_turned.at(l, 1))
                for a, dst in enumerate((qd_t, kd_t)):
                    for b in range(2):
                        ins = nc.scalar.copy(dst[0:MLA_QK, 2 * b:2 * b + 2, :],
                                             acc[2 * a + b][0:MLA_QK, :].rearrange("p (h s) -> p h s", s=SEQ))
                ins.then_inc(mla_t_ready.sem, 1)
                act.wait_ge(logw_ready.sem, logw_ready.at(l, HEADS))
                nc.scalar.activation(za[:, :, :], zs[:, :, :], ACT.Exp).then_inc(ew_ready.sem, 1)
                weights_exp(l, 0, 0, SCALE)
                weights_t(l, 0, wt[1])
                weights_exp(l, HEADS, 1, SCALE_MLA)
                weights_t(l, HEADS, wt[3])
                act.wait_ge(hss_ready.sem, hss_ready.at(l, 1))
                nc.scalar.activation(hss[:, 1, :], hss[:, 0, :], ACT.Sqrt, scale=1.0 / HEAD_DIM, bias=eps)\
                    .then_inc(hstd_ready.sem, 1)
                act_heads(l, 1, G_HEAD)
                ahead(l, C_OUT, 8)

                act.wait_ge(x_mid.sem, x_mid.at(l, 1))
                std(l, 1, step)
                act_heads(l, 2, G_FFN)
                with act.Fori(0, 2) as half:
                    for b in range(4):
                        ahead(l, C_QUERY + half * 8, 2, 2 * b)
                        act.wait_ge(chunk_done.sem, chunk_done.at(l, C_QUERY + half * 8 + (2 * b + 2)))
                        nc.scalar.copy(query_t[:, bass.ds(half * 8 + 2 * b, 2), :],
                                       work[b][:].rearrange("p (j s) -> p j s", s=SEQ)).then_inc(bank_free.sem, 1)
                for t in range(T):
                    for m4 in range(4):
                        act.wait_ge(score_out.sem, score_out.at(l, 4 * t + m4 + 1))
                        at = (SCORE_SLOT + t * PEER_HEADS + 2 * m4) * SEQ
                        nc.scalar.copy(arena[:, at:at + 512], work[m4][:]).then_inc(score_in.sem, 1)
                nc.scalar.preload_act_table(ACT.Gelu)
                with act.Fori(0, E_TILES // 8) as u:
                    act.wait_ge(unit_done.sem, unit_done.at(l, u))
                    for b in range(4):
                        ahead(l, C_U + u * 8, 2, 2 * b)
                        act.wait_ge(chunk_done.sem, chunk_done.at(l, C_U + u * 8 + (2 * b + 2)))
                        nc.scalar.activation(acts[:, bass.ds(u * 8 + 2 * b, 2), :],
                                             work[b][:].rearrange("p (j s) -> p j s", s=SEQ), ACT.Gelu)\
                            .then_inc(bank_free.sem, 1)
                act.wait_ge(gate_ready.sem, gate_ready.at(l, 1))
                nc.scalar.activation(picked[:, 2, :, :], picked[:, 2, :, :], ACT.Exp).then_inc(gate_exp.sem, 1)

                def weight_head(i, slot):
                    act.wait_ge(chunk_done.sem, chunk_done.at(l, C_V + i - 1))
                    act.wait_ge(w_rest_in.sem, w_rest_in.at(l, i - 1))
                    nc.scalar.copy(w_head[:, slot, :], acts[:, i, :]).then_inc(w_head_in.sem, 1)

                def v_block(i0, last):
                    for j in range(4):
                        if not (last and j == 3):
                            weight_head(i0 + (j + 1), (j + 1) % 2)
                        if not (last and j >= 2):
                            split_head(l, C_V + i0 + (j + 2), j % 2, (j + 2) % 4)

                act.wait_ge(gate_used.sem, gate_used.at(l, GROUPS))
                weight_head(0, 0)
                v_block(0, False)
                with act.Fori(1, E_TILES // 4 - 1) as v:
                    v_block(4 * v, False)
                v_block(E_TILES - 4, True)
                assert step.n == ACT_STEPS, step.n
            act.wait_ge(x_ready.sem, DEPTH + 1)
            for t in range(T):
                nc.scalar.activation(arena[:, (2 + t) * D_MODEL:(3 + t) * D_MODEL], xs[:, t, :], ACT.Square,
                                     accum_out=ss[:, 0, t:t + 1]).then_inc(act_step.sem, 1)
            act.wait_ge(act_step.sem, DEPTH * ACT_STEPS + 2)
            nc.scalar.activation(ss[:, 1, :], ss[:, 0, :], ACT.Sqrt, scale=1.0 / D_MODEL, bias=eps)\
                .then_inc(std_ready.sem, 1)
            act.wait_ge(rot_ready.sem, DEPTH + 1)
            act.dma_start(out, xs[:]).then_inc(out_done.sem, 16)
            act.wait_ge(out_done.sem, 16)

        @block.vector
        def _(dve):
            tt, ts = nc.vector.tensor_tensor, nc.vector.tensor_scalar
            dve.sem_inc(rest_in.sem, 2)
            dve.sem_inc(unit_done.sem, 1)
            dve.sem_inc(gate_used.sem, 2)
            dve.sem_inc(w_rest_in.sem, 2)
            dve.wait_ge(x_in.sem, 16)
            dve.sem_inc(x_ready.sem, 1)

            def split_rest(l, cj, slot, raw_slot):
                dve.wait_ge(head_in.sem, head_in.at(l, cj + 1))
                dve.wait_ge(chunk_done.sem, chunk_done.at(l, cj - 1))
                tt(rest[:, slot, :], raw[:, raw_slot, :], head[:, slot, :].bitcast(F32), ALU.subtract)\
                    .then_inc(rest_in.sem, 1)

            def ahead(l, c0, n, j0=0):
                for j in range(j0, j0 + n):
                    split_rest(l, c0 + (j + 2), j % 2, (j + 2) % 4)

            def norm_tokens(l, use, step):
                dve.wait_ge(std_ready.sem, std_ready.at(l, use + 1))
                step(nc.vector.reciprocal(ss[:, 1, :], ss[:, 1, :]))
                for t in range(T):
                    ins = ts(xn[:, t, :], xs[:, t, :], ss[:, 1, t:t + 1], None, ALU.mult)
                ins.then_inc(xn_ready.sem, 1)

            def act_rests(l, use, g0):
                for b in range(4):
                    dve.wait_ge(act_head_in.sem, act_head_in.at(l, 4 * use + b + 1))
                    for kt in (2 * b, 2 * b + 1):
                        ins = nc.vector.scalar_tensor_tensor(
                            out=act_rest[:, kt, :], in0=work[b][:, (kt % 2) * SEQ:(kt % 2 + 1) * SEQ],
                            scalar=gain[:, g0 + kt:g0 + kt + 1], in1=act_head[:, kt, :].bitcast(F32),
                            op0=ALU.mult, op1=ALU.subtract)
                    ins.then_inc(act_rest_in.sem, 1)

            def rope(dst, src, table, heads, half, tmp, step):
                n = 2 * half
                cos, sin = table
                a = tmp[:, 0:heads * n].rearrange("p (h n) -> p h n", h=heads)
                b = tmp[:, 512:512 + heads * n].rearrange("p (h n) -> p h n", h=heads)
                tt(a, src, cos[:, None, :].to_broadcast([P, heads, n]), ALU.mult)
                tt(b[:, :, 0:half], src[:, :, half:n], sin[:, None, 0:half].to_broadcast([P, heads, half]), ALU.mult)
                step(tt(b[:, :, half:n], src[:, :, 0:half], sin[:, None, half:n].to_broadcast([P, heads, half]), ALU.mult))
                ins = tt(dst, a, b, ALU.add)
                return ins

            def table(name, dim, t):
                v = c[name].rearrange("p (a t n) -> p a t n", a=2, t=T)
                return v[:, 0, t, :], v[:, 1, t, :]

            def weights_max(l, base, n, scale, step):
                for h in range(HEADS):
                    dve.wait_ge(soft_out.sem, soft_out.at(l, base + h + 1))
                    if base:
                        dve.wait_ge(soft_turned.sem, soft_turned.at(l, h + 1))
                    step(tt(soft[:, h, :], work[h][:, 0:BLK], c["causal"], ALU.add))
                    nc.vector.reduce_max(mx[:, 2 * n, 0, h:h + 1], soft[:, h, 0:P], AX_X)
                    step(nc.vector.reduce_max(mx[:, 2 * n, 1, h:h + 1], soft[:, h, P:BLK], AX_X))
                    ts(mx[:, 2 * n + 1, :, h], mx[:, 2 * n, :, h], -scale, None, ALU.mult).then_inc(soft_max.sem, 1)

            with dve.Fori(0, DEPTH) as l:
                step = Steps(dve, dve_step, l)
                norm_tokens(l, 0, step)
                for j in range(2):
                    split_rest(l, j, j, j)
                act_rests(l, 0, G_MIX)
                ahead(l, C_WIDE1, 8)
                dve.wait_ge(chunk_done.sem, chunk_done.at(l, C_TALL))
                dve.wait_ge(small_in.sem, small_in.at(l, 48))
                for t in range(T):
                    ahead(l, C_TALL, 2, 2 * t)
                    src = acc[2 * t][:].rearrange("p (h n) -> p h n", n=HEAD_DIM)
                    dst = rot[:, t, :].rearrange("p (h n) -> p h n", n=HEAD_DIM)
                    ins = rope(dst, src, table("rope64", HEAD_DIM, t), 8, HEAD_DIM // 2, spare, step)
                    if t == 0:
                        step(ins)
                ins.then_inc(rot_ready.sem, 1)
                ahead(l, C_TALL, 4, 4)
                ahead(l, C_WIDE2, 8)
                dve.wait_ge(chunk_done.sem, chunk_done.at(l, C_OUT))
                for n in range(2):
                    ins = nc.vector.tensor_copy(g2[:, 1, n * 512:(n + 1) * 512], acc[2 + n][:])
                ins.then_inc(g2_dve.sem, 1)
                dve.wait_ge(g2_dve.sem, g2_dve.at(l, 1))
                dve.wait_ge(g2_act.sem, g2_act.at(l, 1))
                tt(lf[:, 0, :, :], g2[:, :, FF:FF + HEADS],
                   gain[:, None, G_BF:G_BF + HEADS].to_broadcast([P, T, HEADS]), ALU.add).then_inc(ff_ready.sem, 1)
                for t in range(T):
                    src = g2[:, t, None, KR:KR + MLA_ROPE]
                    ins = rope(krot[:, t, None, :], src, table("rope32", MLA_ROPE, t), 1, MLA_ROPE // 2, spare, step)
                    if t == 0:
                        step(ins)
                ins.then_inc(krot_ready.sem, 1)
                decay = c["decay"].rearrange("p (h n) -> p h n", h=HEADS)
                for h in range(HEADS):
                    dve.wait_ge(sa_out.sem, sa_out.at(l, h + 1))
                    tt(wt[0][:, h, :], work[h][:, 0:BLK], decay[:, h, :], ALU.mult).then_inc(wa_ready.sem, 1)
                dve.wait_ge(cstd_ready.sem, cstd_ready.at(l, 1))
                step(nc.vector.reciprocal(css[:, 1, :, :], css[:, 1, :, :]))
                for t in range(T):
                    ts(cn[:, t, 0:256], g2[:, t, CQ:CKV], css[:, 1, 0, t:t + 1], None, ALU.mult)
                    ins = ts(cn[:, t, 256:384], g2[:, t, CKV:KR], css[:, 1, 1, t:t + 1], None, ALU.mult)
                ins.then_inc(cn_ready.sem, 1)
                dve.wait_ge(ffl_ready.sem, ffl_ready.at(l, 1))
                nc.vector.scalar_tensor_tensor(out=lf[:, 0, :, :], in0=lf[:, 0, :, :], scalar=0.0, in1=lf[:, 1, :, :],
                                               op0=ALU.min, op1=ALU.subtract).then_inc(ls_ready.sem, 1)
                step(nc.vector.memset(fc[:, :, :], 1.0))
                dve.wait_ge(fcum_out.sem, fcum_out.at(l, 1))
                cum = acc[0][:, 0:2 * HEADS].rearrange("p (t h) -> p t h", t=T)
                ts(fc[:, :, 0:HEADS], cum, 1.0 / SCALE, None, ALU.mult)
                ts(fc[:, :, 8 + HEADS:16], cum, -1.0 / SCALE, None, ALU.mult).then_inc(fc_ready.sem, 1)
                dve.wait_ge(fc_turned.sem, fc_turned.at(l, 1))
                step(nc.vector.tensor_copy(fc_t[0:8, :], work[0][0:8, :]))
                for h in range(HEADS):
                    ins = ts(fc_h[0:8, h, :], fc_t[0:8, 0:SEQ], c["pick"][0:8, h:h + 1], None, ALU.mult)
                ins.then_inc(fc_t_ready.sem, 1)
                dve.wait_ge(lc_ready.sem, lc_ready.at(l, 1))
                step(nc.vector.scalar_tensor_tensor(out=za[:, :, :], in0=zs[:, :, :], scalar=0.0, in1=za[:, :, :],
                                                    op0=ALU.max, op1=ALU.add))
                strict = c["strict"][:, None, :].to_broadcast([P, HEADS, BLK])
                tt(za[:, :, :], za[:, :, :], strict, ALU.mult).then_inc(sp_ready.sem, 1)
                dve.wait_ge(mla_out.sem, mla_out.at(l, 1))
                for t in range(T):
                    src = acc[t][:, 0:HEADS * MLA_QK].rearrange("p (h n) -> p h n", h=HEADS)
                    nc.vector.tensor_copy(mla_q[:, t, :, 0:HEAD_DIM], src[:, :, 0:HEAD_DIM])
                    ins = rope(mla_q[:, t, :, HEAD_DIM:MLA_QK], src[:, :, HEAD_DIM:MLA_QK],
                               table("rope32", MLA_ROPE, t), HEADS, MLA_ROPE // 2, spare, step)
                    if t == 0:
                        step(ins)
                ins.then_inc(mla_q_ready.sem, 1)
                for h in range(HEADS):
                    dve.wait_ge(cum_out.sem, cum_out.at(l, h + 1))
                    tt(zs[:, h, :], zs[:, h, :], work[h][:, 0:BLK], ALU.subtract).then_inc(logw_ready.sem, 1)
                weights_max(l, 0, 0, SCALE, step)
                dve.wait_ge(ew_ready.sem, ew_ready.at(l, 1))
                tt(wt[2][:, :, :], za[:, :, :], strict, ALU.mult).then_inc(wc_ready.sem, 1)
                weights_max(l, HEADS, 1, SCALE_MLA, step)

                def heads(v):
                    return v.rearrange("p (n d) -> p n d", d=HEAD_DIM)

                def each(v):
                    return v[:, :, None].to_broadcast([P, T * HEADS, HEAD_DIM])

                dve.wait_ge(o_out.sem, o_out.at(l, 1))
                step(nc.vector.reduce_sum(mean[:, 0, :], heads(acc[0][:]), AX_X))
                step(ts(mean[:, 1, :], mean[:, 0, :], 1.0 / HEAD_DIM, None, ALU.mult))
                tt(heads(ya[:, 0, :]), heads(acc[0][:]), each(mean[:, 1, :]), ALU.subtract)
                dve.wait_ge(o_out.sem, o_out.at(l, 2))
                nc.vector.tensor_copy(ya[:, 2, :], acc[2][:])
                for n, g in enumerate((1, 3)):
                    dve.wait_ge(o_out.sem, o_out.at(l, 3 + n))
                    step(nc.vector.reciprocal(dn[:, 2 * n + 1, :, :], dn[:, 2 * n, :, :]))
                    ins = tt(heads(ya[:, g, :]), heads(acc[g][:]),
                             each(dn[:, 2 * n + 1, :, :].rearrange("p t h -> p (t h)")), ALU.mult)
                step(ins)
                step(tt(ysq[:, :, :], ya[:, :, :], ya[:, :, :], ALU.mult))
                nc.vector.reduce_sum(hss[:, 0, :], heads(ysq.rearrange("p g n -> p (g n)")), AX_X)\
                    .then_inc(hss_ready.sem, 1)
                dve.wait_ge(hstd_ready.sem, hstd_ready.at(l, 1))
                step(nc.vector.reciprocal(hss[:, 1, :], hss[:, 1, :]))
                for g in range(4):
                    ins = tt(xn[:, :, g * GROUP_WIDTH:(g + 1) * GROUP_WIDTH].rearrange("p t (h d) -> p t h d", d=HEAD_DIM),
                             ya[:, g, :].rearrange("p (t h d) -> p t h d", t=T, d=HEAD_DIM),
                             hss[:, 1, 8 * g:8 * g + 8].rearrange("p (t h) -> p t h", t=T)[:, :, :, None]
                             .to_broadcast([P, T, HEADS, HEAD_DIM]), ALU.mult)
                step(ins)
                tt(xn[:, :, 0:GROUP_WIDTH], xn[:, :, 0:GROUP_WIDTH], rg[:, :, :], ALU.mult).then_inc(xn_ready.sem, 1)

                act_rests(l, 1, G_HEAD)
                ahead(l, C_OUT, 8)

                def add_residual(done):
                    dve.wait_ge(chunk_done.sem, chunk_done.at(l, done))
                    for t in range(T):
                        for n in range(2):
                            x_part = xs[:, t, n * 512:(n + 1) * 512]
                            ins = tt(x_part, x_part, acc[2 * t + n][:], ALU.add)
                    return ins

                add_residual(C_QUERY).then_inc(x_mid.sem, 1)

                dve.wait_ge(x_mid.sem, x_mid.at(l, 1))
                norm_tokens(l, 1, step)
                act_rests(l, 2, G_FFN)
                with dve.Fori(0, 2) as half:
                    ahead(l, C_QUERY + half * 8, 8)
                dve.wait_ge(score_in.sem, score_in.at(l, 8))
                after_register_wait(dve)
                with dve.Fori(0, UNITS) as u:
                    n_step = [0]

                    def rstep(ins):
                        ins.then_inc(route_step.sem, 1)
                        n_step[0] += 1
                        dve.wait_ge(route_step.sem, l * route_step.per + u * ROUTE_STEPS + n_step[0])
                        after_register_wait(dve)

                    def pass_chunk(j):
                        split_rest(l, C_U + u * 8 + (j + 2), j % 2, (j + 2) % 4)

                    s = scores(u)

                    def top16(part, values, index):
                        rstep(nc.vector.max(part[:, 0:8], values))
                        nc.vector.max_index(index[:, 0:8], part[:, 0:8], values)
                        work_v = left[:, 0:values.shape[1]]
                        rstep(nc.vector.match_replace(work_v, part[:, 0:8], values, NEG_OUT))
                        rstep(nc.vector.max(part[:, 8:16], work_v))
                        rstep(nc.vector.max_index(index[:, 8:16], part[:, 8:16], work_v))

                    pass_chunk(0)
                    rstep(nc.vector.tensor_copy(cand[:, :], s))
                    top16(top_v[:, 0, :], cand[:, 0:P], top_i[:, 0, :])
                    pass_chunk(1)
                    top16(top_v[:, 1, :], cand[:, P:2 * P], top_i[:, 1, :])
                    pass_chunk(2)
                    nc.vector.tensor_copy(top_f[:, :, :], top_i[:, :, :])
                    rstep(tt(cand[:, :].rearrange("p (a b) -> p a b", a=TOPK),
                             top_v[:, 0, :, None].to_broadcast([P, TOPK, TOPK]),
                             top_v[:, 1, None, :].to_broadcast([P, TOPK, TOPK]), ALU.add))
                    pass_chunk(3)
                    best = best_v
                    top16(best, cand[:, :], best_i)
                    pass_chunk(4)
                    ts(rank_i[:, 0, :], best_i[:, :], 4, None, ALU.logical_shift_right)
                    rstep(ts(rank_i[:, 1, :], best_i[:, :], 15, None, ALU.bitwise_and))
                    rstep(nc.vector.tensor_copy(rank_f[:, :, :], rank_i[:, :, :]))
                    for a in range(2):
                        ins = tt(match[:, a, :].rearrange("p (k r) -> p k r", k=TOPK),
                                 rank_f[:, a, :, None].to_broadcast([P, TOPK, TOPK]),
                                 iota[:, None, 0:TOPK].to_broadcast([P, TOPK, TOPK]), ALU.is_equal)
                    rstep(ins)
                    pass_chunk(5)
                    for a in range(2):
                        m = match[:, a, :].rearrange("p (k r) -> p k r", k=TOPK)
                        ins = tt(m, m, top_f[:, a, None, :].to_broadcast([P, TOPK, TOPK]), ALU.mult)
                    rstep(ins)
                    pass_chunk(6)
                    for a in range(2):
                        ins = nc.vector.reduce_sum(rank_f[:, a, :], match[:, a, :].rearrange("p (k r) -> p k r", k=TOPK), AX_X)
                    rstep(ins)
                    pass_chunk(7)
                    flat = picked[:, :, :, :].rearrange("p a t n -> p a (t n)")
                    nc.vector.tensor_copy(flat[:, 0:2, bass.ds(u * TOPK, TOPK)], rank_f[:, :, :])
                    nc.vector.tensor_copy(flat[:, 2, bass.ds(u * TOPK, TOPK)], best[:, :]).then_inc(unit_done.sem, 1)
                    assert n_step[0] == ROUTE_STEPS, n_step[0]
                dve.wait_ge(unit_done.sem, unit_done.at(l, UNITS))
                gate = picked[:, 2, :, :].rearrange("p t (h k) -> p (t h) k", k=TOPK)
                gsum = gs[:, :, :, :].rearrange("p a t h -> p a (t h)")
                step(nc.vector.tensor_copy(gsum[:, 0, :], gate[:, :, 0]))
                tt(gate, gate, gsum[:, 0, :, None].to_broadcast([P, UNITS, TOPK]), ALU.subtract).then_inc(gate_ready.sem, 1)
                dve.wait_ge(gate_exp.sem, gate_exp.at(l, 1))
                step(nc.vector.reduce_sum(gsum[:, 0, :], gate, AX_X))
                step(nc.vector.reciprocal(gsum[:, 1, :], gsum[:, 0, :]))
                tt(gate, gate, gsum[:, 1, :, None].to_broadcast([P, UNITS, TOPK]), ALU.mult).then_inc(gates_done.sem, 1)
                dve.wait_ge(picked_turned.sem, picked_turned.at(l, 1))
                nc.vector.tensor_copy(picked_t[:, 0:2, :], work[0][:].rearrange("p (a s) -> p a s", a=2))
                step(nc.vector.tensor_copy(picked_t[:, 2, :], work[1][:, 0:SEQ]))
                after_register_wait(dve)
                with dve.Fori(0, GROUPS // 2) as g:
                    for b in range(2):
                        for q in range(4):
                            tok = g * 8 + (4 * b + q)
                            ts(hot2[:, 4 * b + q, :], iota, picked_t[:, 1, bass.ds(tok, 1)],
                               picked_t[:, 2, bass.ds(tok, 1)], ALU.is_equal, ALU.mult)
                            ins = ts(hot1[:, 4 * b + q, :], iota, picked_t[:, 0, bass.ds(tok, 1)], None, ALU.is_equal)
                        ins.then_inc(hot_ready.sem, 1)
                    for b in range(2):
                        dve.wait_ge(gate_out.sem, gate_out.at(l, 2 * g + (b + 1)))
                        a = acts[:, :, bass.ds(g * 8 + 4 * b, 4)]
                        tt(a, a, work[2 + b][:].rearrange("p (q i) -> p i q", q=4), ALU.mult).then_inc(gate_used.sem, 1)

                def weight_rest(i, slot):
                    dve.wait_ge(w_head_in.sem, w_head_in.at(l, i + 1))
                    dve.wait_ge(chunk_done.sem, chunk_done.at(l, C_V + i - 1))
                    tt(w_rest[:, slot, :], acts[:, i, :], w_head[:, slot, :].bitcast(F32), ALU.subtract)\
                        .then_inc(w_rest_in.sem, 1)

                def v_block(i0, last):
                    for j in range(4):
                        if not (last and j == 3):
                            weight_rest(i0 + (j + 1), (j + 1) % 2)
                        if not (last and j >= 2):
                            split_rest(l, C_V + i0 + (j + 2), j % 2, (j + 2) % 4)

                dve.wait_ge(gate_used.sem, gate_used.at(l, GROUPS))
                weight_rest(0, 0)
                v_block(0, False)
                with dve.Fori(1, E_TILES // 4 - 1) as v:
                    v_block(4 * v, False)
                v_block(E_TILES - 4, True)
                add_residual(CHUNKS).then_inc(x_ready.sem, 1)
                assert step.n == DVE_STEPS, step.n
            dve.wait_ge(std_ready.sem, DEPTH * 2 + 1)
            nc.vector.reciprocal(ss[:, 1, :], ss[:, 1, :]).then_inc(dve_step.sem, 1)
            dve.wait_ge(dve_step.sem, DEPTH * DVE_STEPS + 1)
            dve.wait_ge(fixed_in.sem, 32)
            for t in range(T):
                ins = nc.vector.scalar_tensor_tensor(out=xs[:, t, :], in0=xs[:, t, :], scalar=ss[:, 1, t:t + 1],
                                                     in1=arena[:, 0:D_MODEL], op0=ALU.mult, op1=ALU.mult)
            ins.then_inc(rot_ready.sem, 1)


def stream_layout(w_in, w_out, w_query, expert_u, expert_v):
    w = GROUP_WIDTH
    cols = np.cumsum([0] + [w] * 7 + [HEADS] + [w] * 3 + [MLA_Q_RANK, MLA_KV_RANK, MLA_ROPE])
    rq, rk, rv, rg, fq, fk, fv, ff, sq, sk, sv, cq, ckv, kr = (
        w_in[:, a:b] for a, b in zip(cols[:-1], cols[1:]))

    def wide(m):
        return m.reshape(-1, P, CHUNK)

    def tall(m):
        return m.reshape(KT, P, -1, P).transpose(2, 1, 0, 3).reshape(-1, P, CHUNK)

    second = np.concatenate([fv, sv, cq, ckv, kr, ff], 1)
    second = np.pad(second, ((0, 0), (0, D_MODEL - second.shape[1])))
    experts = expert_u.reshape(E_TILES, P, KT, P).transpose(0, 3, 2, 1).reshape(-1, P, CHUNK)
    chunks = np.concatenate([
        wide(np.concatenate([rq, rk, rv, rg], 1)), tall(np.concatenate([fq, fk, sq, sk], 1)),
        wide(second), wide(w_out), tall(w_query), experts, wide(expert_v)])
    return chunks.reshape(PAIRS, 2, P, CHUNK).transpose(0, 2, 1, 3)


def kernel(x, norm_mix, w_in, b_forget, norm_cq, norm_ckv, w_uq, w_ukv, head_gain, w_out,
           norm_ffn, w_query, sub_keys, expert_u, expert_v, norm_final):
    import concourse.bacc as bacc
    from concourse.bass_utils import run_bass_kernel_spmd

    def a(v):
        return np.asarray(v)

    def per_partition(v):
        return a(v).reshape(DEPTH, -1, P).transpose(0, 2, 1)

    stream = np.concatenate([stream_layout(a(w_in)[l], a(w_out)[l], a(w_query)[l], a(expert_u)[l], a(expert_v)[l])
                             for l in range(DEPTH)])
    gains = np.concatenate([
        per_partition(norm_mix), per_partition(head_gain), per_partition(norm_ffn), per_partition(norm_cq),
        per_partition(norm_ckv), np.broadcast_to(a(b_forget)[:, None, :], (DEPTH, P, HEADS))], 2)
    small = np.concatenate([
        a(w_uq).reshape(DEPTH, 2, P, -1).transpose(0, 2, 1, 3).reshape(DEPTH, P, -1), a(w_ukv),
        a(sub_keys).transpose(0, 4, 1, 2, 3).reshape(DEPTH, P, -1)], 2)
    tables = constants()
    arrays = {
        "x": a(x).reshape(T, P, D_MODEL).transpose(1, 0, 2),
        "stream": stream,
        "gains": gains,
        "small": small,
        "mixer_consts": np.concatenate([tables[n] for n, _ in MIXER_CONSTS], 1),
        "fixed_consts": np.concatenate([np.eye(P), np.tile(np.arange(P), (P, 1))], 1),
        "gain_final": a(norm_final).reshape(1, D_MODEL),
    }
    arrays = {n: np.ascontiguousarray(v, dtype=np.float32) for n, v in arrays.items()}
    nc = bacc.Bacc("TRN2", target_bir_lowering=False, num_devices=1)
    args = {n: nc.dram_tensor(n, v.shape, F32, kind="ExternalInput").ap() for n, v in arrays.items()}
    out = nc.dram_tensor("out", (P, T, D_MODEL), F32, kind="ExternalOutput").ap()
    hybrid_ret_fox_sb_mla_peer(nc, **args, out=out)
    r = run_bass_kernel_spmd(nc, [arrays], core_ids=[0])
    return r.results[0]["out"].transpose(1, 0, 2).reshape(1, SEQ, D_MODEL)
```

```python
from contextlib import ExitStack

import numpy as np

import concourse.bass as bass
from concourse import mybir

F32 = mybir.dt.float32
F32R = mybir.dt.float32r
U32 = mybir.dt.uint32
ACT = mybir.ActivationFunctionType
ALU = mybir.AluOpType
AX_X = mybir.AxisListType.X

P = 128
D_MODEL = 1024
SEQ = 256
DEPTH = 2
HEADS = 4
HEAD_DIM = 64
GROUP_WIDTH = HEADS * HEAD_DIM
MLA_Q_RANK = 256
MLA_KV_RANK = 128
MLA_ROPE = 32
MLA_QK = HEAD_DIM + MLA_ROPE
PEER_HEADS = 8
PEER_KEYS = 128
TOPK = 16
EPS = 1e-6
ROPE_BASE = 10000.0
SCALE = HEAD_DIM ** -0.5
SCALE_MLA = MLA_QK ** -0.5

T = SEQ // P
KT = D_MODEL // P
CHUNK = KT * P
E_TILES = PEER_KEYS
HALF = E_TILES // 2
C_WIDE1, C_TALL, C_WIDE2, C_OUT, C_QUERY, C_U = 0, 8, 16, 24, 32, 48
C_V = C_U + E_TILES
CHUNKS = C_V + E_TILES
PAIRS = CHUNKS // 2

BLK = 3 * P

FV, SV, CQ, CKV, KR, FF = 0, 256, 512, 768, 896, 928
NEG_BIG = -1e30
NEG_OUT = -3.0e38

ACT_STEPS, DVE_STEPS, ROUTE_STEPS = 12, 41, 16

G_MIX, G_HEAD, G_FFN, G_CQ, G_CKV, G_BF, GAINS = 0, 8, 16, 24, 26, 27, 31
W_UQ, W_UKV, W_KEYS, SMALL = 0, 768, 1280, 1280 + 16 * PEER_KEYS


def constants():
    i = np.arange(P, dtype=np.float32)
    k, q = i[:, None], i[None, :]
    tri_ge = (k >= q).astype(np.float32)
    tri_le = (k <= q).astype(np.float32)
    ones = np.ones((P, P), np.float32)
    gamma = np.log1p(-(2.0 ** (-5.0 - np.arange(HEADS, dtype=np.float32))))
    decay = np.zeros((P, HEADS, BLK), np.float32)
    for h in range(HEADS):
        near = np.where(q >= k, np.exp(gamma[h] * np.maximum(q - k, 0.0)), 0.0)
        far = np.exp(gamma[h] * (q + P - k))
        decay[:, h] = np.concatenate([near, far, near], 1) * SCALE
    late = np.where(k >= q, 0.0, NEG_BIG)
    causal = np.concatenate([late, 0 * late, late], 1)
    strict = np.concatenate([(k < q), np.ones((P, P), bool), (k < q)], 1)
    pos = np.arange(SEQ, dtype=np.float32)

    def rope(dim):
        inv = ROPE_BASE ** (-np.arange(0, dim, 2, dtype=np.float32) / dim)
        ang = (pos[:, None] * inv[None, :]).astype(np.float32)
        cos, sin = np.cos(ang), np.sin(ang)
        table = np.stack([np.concatenate([cos, cos], 1), np.concatenate([-sin, sin], 1)])
        return table.reshape(2, T, P, dim).transpose(2, 0, 1, 3).reshape(P, -1)

    pick = np.zeros((P, HEADS), np.float32)
    for h in range(HEADS):
        pick[h, h] = pick[HEADS + h, h] = 1.0
    return {
        "tri_ge": tri_ge, "tri_le": tri_le, "ones": ones, "decay": decay.reshape(P, -1),
        "causal": causal, "strict": strict, "rope64": rope(HEAD_DIM), "rope32": rope(MLA_ROPE),
        "pick": pick,
    }


MIXER_CONSTS = [("tri_ge", P), ("tri_le", P), ("ones", P), ("decay", HEADS * BLK), ("causal", BLK),
                ("strict", BLK), ("rope64", 2 * T * HEAD_DIM), ("rope32", 2 * T * MLA_ROPE), ("pick", HEADS)]
MIXER_CONST_COLS = sum(n for _, n in MIXER_CONSTS)


def hybrid_ret_fox_sb_mla_peer(nc, x, stream, gains, small, mixer_consts, fixed_consts, gain_final, out):
    with ExitStack() as ctx:
        def sb(name, shape, dt=F32):
            return ctx.enter_context(nc.sbuf_tensor(name, shape, dt))

        class Count:
            def __init__(self, name, per, first=0):
                self.sem, self.per, self.first = ctx.enter_context(nc.semaphore(name)), per, first

            def at(self, l, n):
                return l * self.per + (self.first + n)

        raw = sb("raw", [P, 4, CHUNK])
        head = sb("head", [P, 2, CHUNK], F32R)
        rest = sb("rest", [P, 2, CHUNK], F32R)
        xs = sb("xs", [P, T, D_MODEL])
        arena = sb("arena", [P, E_TILES * SEQ])
        gain = sb("gain", [P, GAINS])
        fixed = sb("fixed", [P, 2 * P])
        ident, iota = fixed[:, 0:P], fixed[:, P:2 * P]
        picked = sb("picked", [P, 3, T, PEER_HEADS * TOPK])
        ss = sb("ss", [P, 2, T])
        css = sb("css", [P, 2, 2, T])
        hss = sb("hss", [P, 2, 32])
        gs = sb("gs", [P, 2, T, PEER_HEADS])
        picked_t = sb("picked_t", [P, 3, SEQ])
        hot1 = sb("hot1", [P, 2, 4, HALF])
        hot2 = sb("hot2", [P, 2, 4, P])
        top_v = sb("top_v", [P, 2, TOPK])
        top_i = sb("top_i", [P, 2, TOPK], U32)
        top_f = sb("top_f", [P, 2, TOPK])
        left = sb("left", [P, 2, P])
        cand = sb("cand", [P, TOPK * TOPK])
        stage = sb("stage", [P, 2, P])
        best_v = sb("best_v", [P, TOPK])
        best_i = sb("best_i", [P, TOPK], U32)
        rank_i = sb("rank_i", [P, 2, TOPK], U32)
        rank_f = sb("rank_f", [P, 2, TOPK])
        match = sb("match", [P, 2, TOPK * TOPK])

        with nc.sbuf_tensor("act_head", [P, KT, SEQ], F32R) as act_head, \
                nc.sbuf_tensor("act_rest", [P, KT, SEQ], F32R) as act_rest:
            pass
        w_head = sb("w_head", [P, 2, SEQ], F32R)
        w_rest = sb("w_rest", [P, 2, SEQ], F32R)

        used = [0]

        def carve(n):
            used[0] += n
            assert used[0] <= E_TILES * SEQ, used[0]
            return arena[:, used[0] - n:used[0]]

        xn = carve(T * D_MODEL).rearrange("p (t d) -> p t d", t=T)
        wt = [carve(HEADS * BLK).rearrange("p (h n) -> p h n", h=HEADS) for _ in range(4)]
        consts = carve(MIXER_CONST_COLS)
        at, c = 0, {}
        for name, n in MIXER_CONSTS:
            c[name] = consts[:, at:at + n]
            at += n
        smalls = carve(SMALL)
        w_uq = smalls[:, W_UQ:W_UKV].rearrange("p (r n) -> p r n", r=2)
        w_ukv = smalls[:, W_UKV:W_KEYS]
        keys_t = smalls[:, W_KEYS:SMALL].rearrange("p (m n) -> p m n", n=PEER_KEYS)
        rot = carve(T * 512).rearrange("p (t n) -> p t n", t=T)
        ret_t = carve(4 * SEQ).rearrange("p (j s) -> p j s", s=SEQ)
        rv = carve(T * GROUP_WIDTH).rearrange("p (t n) -> p t n", t=T)
        rg = carve(T * GROUP_WIDTH).rearrange("p (t n) -> p t n", t=T)
        fs_t = carve(8 * SEQ).rearrange("p (j s) -> p j s", s=SEQ)
        g2 = carve(T * D_MODEL).rearrange("p (t n) -> p t n", t=T)
        lf = carve(2 * T * HEADS).rearrange("p (a t h) -> p a t h", a=2, t=T)
        fc = carve(T * 16).rearrange("p (t n) -> p t n", t=T)
        fc_t = carve(2 * SEQ)
        fc_h = carve(HEADS * SEQ).rearrange("p (h s) -> p h s", h=HEADS)
        cn = carve(T * 384).rearrange("p (t n) -> p t n", t=T)
        c_at = used[0]
        c_t = carve(3 * SEQ).rearrange("p (j s) -> p j s", s=SEQ)
        mla_q = carve(T * HEADS * MLA_QK).rearrange("p (t h n) -> p t h n", t=T, h=HEADS)
        mla_k = carve(T * HEADS * MLA_QK).rearrange("p (t h n) -> p t h n", t=T, h=HEADS)
        mla_v = carve(T * GROUP_WIDTH).rearrange("p (t h n) -> p t h n", t=T, h=HEADS)
        krot = carve(T * MLA_ROPE).rearrange("p (t n) -> p t n", t=T)
        spare = carve(2 * 512)
        zs = carve(HEADS * BLK).rearrange("p (h n) -> p h n", h=HEADS)
        za = carve(HEADS * BLK).rearrange("p (h n) -> p h n", h=HEADS)
        soft = carve(HEADS * BLK).rearrange("p (h n) -> p h n", h=HEADS)
        mx = carve(4 * HEADS * T).rearrange("p (a t h) -> p a t h", a=4, t=T)
        dn = carve(4 * HEADS * T).rearrange("p (a t h) -> p a t h", a=4, t=T)
        mean = carve(2 * HEADS * T).rearrange("p (a n) -> p a n", a=2)
        scratch = wt[1].rearrange("p h n -> p (h n)")[:, 0:D_MODEL]
        qd_t = rot.rearrange("p t n -> p (t n)").rearrange("p (h s) -> p h s", h=HEADS)
        kd_t = ret_t
        ya = arena[:, c_at:c_at + 4 * T * GROUP_WIDTH].rearrange("p (g n) -> p g n", g=4)
        ysq = fs_t.rearrange("p j s -> p (j s)").rearrange("p (g n) -> p g n", g=4)
        query_t = arena[:, T * D_MODEL:T * D_MODEL + 16 * SEQ].rearrange("p (m s) -> p m s", s=SEQ)
        assert 16 * SEQ <= 4 * HEADS * BLK

        acts = arena[:, 0:E_TILES * SEQ].rearrange("p (i s) -> p i s", s=SEQ)
        SCORE_SLOT = E_TILES - T * PEER_HEADS

        def scores(unit):
            return arena[:, bass.ds((unit + SCORE_SLOT) * SEQ, SEQ)]

        acc = [ctx.enter_context(nc.psum_tensor(f"acc{i}", [P, 512], F32)) for i in range(4)]
        work = [ctx.enter_context(nc.psum_tensor(f"work{i}", [P, 512], F32)) for i in range(4)]

        raw_in = [Count(f"raw_in{i}", 16 * PAIRS // 2) for i in range(2)]
        head_in = Count("head_in", CHUNKS)
        rest_in = Count("rest_in", CHUNKS, 2)
        head_free = Count("head_free", CHUNKS, 2)
        chunk_done = Count("chunk_done", CHUNKS, 2)
        TALLS = 4 + 8 + E_TILES // 2
        bank_free = Count("bank_free", TALLS, 2)
        fixed_in = Count("fixed_in", 0)
        x_in = Count("x_in", 0)
        small_in = Count("small_in", 48)
        x_ready = Count("x_ready", 1, 1)
        x_mid = Count("x_mid", 1)
        std_ready = Count("std_ready", 2)
        xn_ready = Count("xn_ready", 3)
        turned = Count("turned", 12)
        act_head_in = Count("act_head_in", 12)
        act_rest_in = Count("act_rest_in", 12)
        rot_ready = Count("rot_ready", 1)
        rv_ready = Count("rv_ready", 1)
        ret_turned = Count("ret_turned", 1)
        ret_t_ready = Count("ret_t_ready", 1)
        g2_act = Count("g2_act", 1)
        g2_dve = Count("g2_dve", 1)
        cstd_ready = Count("cstd_ready", 1)
        cn_ready = Count("cn_ready", 1)
        c_turned = Count("c_turned", 1)
        c_t_ready = Count("c_t_ready", 1)
        mla_out = Count("mla_out", 1)
        krot_ready = Count("krot_ready", 1)
        mla_q_ready = Count("mla_q_ready", 1)
        mla_kv_ready = Count("mla_kv_ready", 1)
        mla_turned = Count("mla_turned", 1)
        mla_t_ready = Count("mla_t_ready", 1)
        ff_ready = Count("ff_ready", 1)
        ffl_ready = Count("ffl_ready", 1)
        ls_ready = Count("ls_ready", 1)
        fcum_out = Count("fcum_out", 1)
        fc_ready = Count("fc_ready", 1)
        fc_turned = Count("fc_turned", 1)
        fc_t_ready = Count("fc_t_ready", 1)
        sa_out = Count("sa_out", HEADS)
        wa_ready = Count("wa_ready", HEADS)
        sc_out = Count("sc_out", HEADS)
        zs_ready = Count("zs_ready", HEADS)
        lc_ready = Count("lc_ready", 1)
        sp_ready = Count("sp_ready", 1)
        cum_out = Count("cum_out", HEADS)
        logw_ready = Count("logw_ready", HEADS)
        ew_ready = Count("ew_ready", 1)
        wc_ready = Count("wc_ready", 1)
        soft_out = Count("soft_out", 2 * HEADS)
        soft_max = Count("soft_max", 2 * HEADS)
        soft_exp = Count("soft_exp", 2 * HEADS)
        soft_turned = Count("soft_turned", 2 * HEADS)
        soft_t_ready = Count("soft_t_ready", 2 * HEADS)
        o_out = Count("o_out", 4)
        hss_ready = Count("hss_ready", 1)
        hstd_ready = Count("hstd_ready", 1)
        score_out = Count("score_out", 8)
        score_in = Count("score_in", 8)
        UNITS = T * PEER_HEADS
        unit_done = Count("unit_done", UNITS, 1)
        gate_exp = Count("gate_exp", 1)
        gates_done = Count("gates_done", 1)
        picked_turned = Count("picked_turned", 1)
        picked_t_in = Count("picked_t_in", 1)
        staged = Count("staged", UNITS)
        GROUPS = 2 * SEQ // 4
        hot_ready = Count("hot_ready", GROUPS)
        gate_out = Count("gate_out", GROUPS)
        gate_used = Count("gate_used", GROUPS, 2)
        w_head_in = Count("w_head_in", E_TILES)
        w_rest_in = Count("w_rest_in", E_TILES, 2)
        out_done = Count("out_done", 0)
        act_step = Count("act_step", ACT_STEPS)
        dve_step = Count("dve_step", DVE_STEPS)
        route_step = Count("route_step", UNITS * ROUTE_STEPS)

        class Steps:

            def __init__(self, eng, count, l):
                self.eng, self.count, self.l, self.n = eng, count, l, 0

            def __call__(self, ins):
                ins.then_inc(self.count.sem, 1)
                self.n += 1
                self.eng.wait_ge(self.count.sem, self.count.at(self.l, self.n))

        passed = ctx.enter_context(nc.semaphore("passed"))

        def after_register_wait(eng):
            eng.sem_inc(passed, 1)

        block = ctx.enter_context(nc.Block())

        @block.sync
        def _(sp):
            def load(pair, slot):
                sp.dma_start(raw[:, 2 * slot:2 * slot + 2, :], stream[pair]).then_inc(raw_in[slot].sem, 16)

            load(0, 0)
            load(1, 1)
            with sp.Fori(1, DEPTH * PAIRS // 2) as k:
                for slot in range(2):
                    sp.wait_ge(rest_in.sem, 4 * k + (2 * slot + rest_in.first - 2))
                    load(2 * k + slot, slot)
            for slot in range(2):
                sp.wait_ge(raw_in[slot].sem, 16 * DEPTH * PAIRS // 2)

        @block.gpsimd
        def _(pool):
            pool.dma_start(fixed[:], fixed_consts).then_inc(fixed_in.sem, 16)
            pool.dma_start(xs[:], x).then_inc(x_in.sem, 16)
            with pool.Fori(0, DEPTH) as l:
                pool.wait_ge(x_ready.sem, x_ready.at(l, 0))
                pool.dma_start(gain[:], gains[l]).then_inc(small_in.sem, 16)
                pool.dma_start(smalls, small[l]).then_inc(small_in.sem, 16)
                pool.dma_start(consts, mixer_consts).then_inc(small_in.sem, 16)
            pool.wait_ge(x_ready.sem, DEPTH + 1)
            pool.dma_start(arena[:, 0:D_MODEL], gain_final.to_broadcast([P, D_MODEL])).then_inc(fixed_in.sem, 16)

        @block.tensor
        def _(pe):
            mm = nc.tensor.matmul
            pe.sem_inc(head_free.sem, 2)
            pe.sem_inc(chunk_done.sem, 2)
            pe.wait_ge(fixed_in.sem, 16)

            def tall_block(l, c0, pair0, between=None):
                for j in range(4):
                    s, bank = j % 2, work[j // 2]
                    o = bank[:, (j % 2) * SEQ:(j % 2 + 1) * SEQ]
                    if j % 2 == 0:
                        pe.wait_ge(bank_free.sem, bank_free.at(l, pair0 + (j // 2 - 1)))
                    pe.wait_ge(head_in.sem, head_in.at(l, c0 + (j + 1)))
                    for kt in range(KT):
                        w = head[:, s, kt * P:(kt + 1) * P]
                        mm(o, w, act_head[:, kt, :], start=(kt == 0), stop=False)
                        ins = mm(o, w, act_rest[:, kt, :], start=False, stop=False)
                    ins.then_inc(head_free.sem, 1)
                    if between:
                        between(j)
                    pe.wait_ge(rest_in.sem, rest_in.at(l, c0 + (j + 1)))
                    for kt in range(KT):
                        ins = mm(o, rest[:, s, kt * P:(kt + 1) * P], act_head[:, kt, :],
                                 start=False, stop=(kt == KT - 1))
                    ins.then_inc(chunk_done.sem, 1)

            def gates_of(l, n, b):
                pe.wait_ge(hot_ready.sem, hot_ready.at(l, n + 1))
                pe.wait_ge(gate_used.sem, gate_used.at(l, n - 1))
                for q in range(4):
                    ins = mm(work[2 + b][:, q * HALF:(q + 1) * HALF], hot2[:, b, q, :], hot1[:, b, q, :],
                             start=True, stop=True)
                ins.then_inc(gate_out.sem, 1)

            def wide_chunk(l, cj, s, a_head, a_rest, first, last, between=None):
                pe.wait_ge(head_in.sem, head_in.at(l, cj + 1))
                for t in range(T):
                    for n in range(2):
                        mm(acc[2 * t + n][:], a_head(t), head[:, s, n * 512:(n + 1) * 512], start=first, stop=False)
                for t in range(T):
                    for n in range(2):
                        ins = mm(acc[2 * t + n][:], a_rest(t), head[:, s, n * 512:(n + 1) * 512], start=False, stop=False)
                ins.then_inc(head_free.sem, 1)
                if between:
                    between()
                pe.wait_ge(rest_in.sem, rest_in.at(l, cj + 1))
                for t in range(T):
                    for n in range(2):
                        ins = mm(acc[2 * t + n][:], a_head(t), rest[:, s, n * 512:(n + 1) * 512], start=False, stop=last)
                ins.then_inc(chunk_done.sem, 1)

            def wide(l, c0):
                for kt in range(KT):
                    wide_chunk(l, c0 + kt, kt % 2, lambda t: act_head[:, kt, t * P:(t + 1) * P],
                               lambda t: act_rest[:, kt, t * P:(t + 1) * P], kt == 0, kt == KT - 1)

            def turn(l, use):
                pe.wait_ge(xn_ready.sem, xn_ready.at(l, use + 1))
                for kt in range(KT):
                    for t in range(T):
                        ins = pe.transpose(work[kt // 2][:, (kt % 2) * SEQ + t * P:(kt % 2) * SEQ + (t + 1) * P],
                                           xn[:, t, kt * P:(kt + 1) * P], ident)
                    if kt % 2:
                        ins.then_inc(turned.sem, 1)
                pe.wait_ge(act_rest_in.sem, act_rest_in.at(l, 4 * use + 4))

            def keys_by_queries(o, k_t, q_t):
                mm(o[:, 0:SEQ], k_t[:, 0:P], q_t, start=True, stop=True)
                return mm(o[:, SEQ:BLK], k_t[:, P:SEQ], q_t[:, P:SEQ], start=True, stop=True)

            def weighted(g, w, v):
                for h in range(HEADS):
                    o = acc[g][:, h * HEAD_DIM:(h + 1) * HEAD_DIM]
                    mm(o, w[:, h, 0:P], v(0, h), start=True, stop=True)
                    o = acc[g][:, GROUP_WIDTH + h * HEAD_DIM:GROUP_WIDTH + (h + 1) * HEAD_DIM]
                    mm(o, w[:, h, P:SEQ], v(0, h), start=True, stop=False)
                    ins = mm(o, w[:, h, SEQ:BLK], v(1, h), start=False, stop=True)
                ins.then_inc(o_out.sem, 1)

            def rows(h):
                return slice((h % 2) * HEAD_DIM, (h % 2 + 1) * HEAD_DIM)

            with pe.Fori(0, DEPTH) as l:
                pe.wait_ge(x_ready.sem, x_ready.at(l, 0))
                turn(l, 0)
                wide(l, C_WIDE1)
                tall_block(l, C_TALL, 0)
                tall_block(l, C_TALL + 4, 2)
                pe.wait_ge(rot_ready.sem, rot_ready.at(l, 1))
                pe.wait_ge(rv_ready.sem, rv_ready.at(l, 1))
                wide(l, C_WIDE2)

                pe.wait_ge(bank_free.sem, bank_free.at(l, 4))
                for j in range(4):
                    for t in range(T):
                        ins = pe.transpose(work[j // 2][:, (j % 2) * SEQ + t * P:(j % 2) * SEQ + (t + 1) * P],
                                           rot[:, t, j * P:(j + 1) * P], ident)
                ins.then_inc(ret_turned.sem, 1)
                pe.wait_ge(ret_t_ready.sem, ret_t_ready.at(l, 1))
                for h in range(HEADS):
                    keys_by_queries(work[h], ret_t[rows(h), 2 + h // 2, :], ret_t[rows(h), h // 2, :])\
                        .then_inc(sa_out.sem, 1)

                pe.wait_ge(g2_act.sem, g2_act.at(l, 1))
                pe.wait_ge(cn_ready.sem, cn_ready.at(l, 1))
                for j in range(3):
                    for t in range(T):
                        ins = pe.transpose(acc[2 + j // 2][:, (j % 2) * SEQ + t * P:(j % 2) * SEQ + (t + 1) * P],
                                           cn[:, t, j * P:(j + 1) * P], ident)
                ins.then_inc(c_turned.sem, 1)

                for h in range(HEADS):
                    pe.wait_ge(wa_ready.sem, wa_ready.at(l, h + 1))
                    keys_by_queries(work[h], fs_t[rows(h), 6 + h // 2, :], fs_t[rows(h), 4 + h // 2, :])\
                        .then_inc(sc_out.sem, 1)

                pe.wait_ge(ls_ready.sem, ls_ready.at(l, 1))
                pe.wait_ge(g2_dve.sem, g2_dve.at(l, 1))
                mm(acc[0][:, 0:HEADS], c["tri_le"], lf[:, 0, 0, :], start=True, stop=True)
                mm(acc[0][:, HEADS:2 * HEADS], c["tri_le"], lf[:, 0, 1, :], start=True, stop=False)
                mm(acc[0][:, HEADS:2 * HEADS], c["ones"], lf[:, 0, 0, :], start=False, stop=True).then_inc(fcum_out.sem, 1)
                pe.wait_ge(fc_ready.sem, fc_ready.at(l, 1))
                pe.wait_ge(zs_ready.sem, zs_ready.at(l, 1))
                for a in range(2):
                    for t in range(T):
                        ins = pe.transpose(work[0][0:8, a * SEQ + t * P:a * SEQ + (t + 1) * P],
                                           fc[:, t, 8 * a:8 * a + 8], ident)
                ins.then_inc(fc_turned.sem, 1)

                pe.wait_ge(c_t_ready.sem, c_t_ready.at(l, 1))
                for t in range(T):
                    mm(acc[t][:, 0:384], c_t[:, 0, t * P:(t + 1) * P], w_uq[:, 0, :], start=True, stop=False)
                    mm(acc[t][:, 0:384], c_t[:, 1, t * P:(t + 1) * P], w_uq[:, 1, :], start=False, stop=True)
                for t in range(T):
                    ins = mm(acc[2 + t][:], c_t[:, 2, t * P:(t + 1) * P], w_ukv, start=True, stop=True)
                ins.then_inc(mla_out.sem, 1)

                pe.wait_ge(sp_ready.sem, sp_ready.at(l, 1))
                pe.wait_ge(zs_ready.sem, zs_ready.at(l, HEADS))
                pe.wait_ge(fc_t_ready.sem, fc_t_ready.at(l, 1))
                for h in range(HEADS):
                    mm(work[h][:, 0:BLK], c["tri_ge"], za[:, h, :], start=True, stop=False)
                    mm(work[h][:, P:SEQ], c["ones"], za[:, h, SEQ:BLK], start=False, stop=True).then_inc(cum_out.sem, 1)

                pe.wait_ge(mla_q_ready.sem, mla_q_ready.at(l, 1))
                pe.wait_ge(mla_kv_ready.sem, mla_kv_ready.at(l, 1))
                for a, src in enumerate((mla_q, mla_k)):
                    for h in range(HEADS):
                        for t in range(T):
                            ins = pe.transpose(
                                acc[2 * a + h // 2][0:MLA_QK, (h % 2) * SEQ + t * P:(h % 2) * SEQ + (t + 1) * P],
                                src[:, t, h, :], ident)
                ins.then_inc(mla_turned.sem, 1)

                for h in range(HEADS):
                    q_t, k_t, o = fs_t[rows(h), h // 2, :], fs_t[rows(h), 2 + h // 2, :], work[h]
                    pe.wait_ge(logw_ready.sem, logw_ready.at(l, h + 1))
                    mm(o[:, 0:P], q_t[:, 0:P], k_t[:, 0:P], start=True, stop=False)
                    mm(o[:, 0:P], fc_h[0:8, h, 0:P], fc_t[0:8, SEQ:SEQ + P], start=False, stop=True)
                    mm(o[:, P:BLK], q_t[:, P:SEQ], k_t, start=True, stop=False)
                    mm(o[:, P:BLK], fc_h[0:8, h, P:SEQ], fc_t[0:8, SEQ:2 * SEQ], start=False, stop=True)\
                        .then_inc(soft_out.sem, 1)

                def turn_weights(base):
                    for h in range(HEADS):
                        pe.wait_ge(soft_exp.sem, soft_exp.at(l, base + h + 1))
                        for j in range(3):
                            ins = pe.transpose(work[h][:, j * P:(j + 1) * P], soft[:, h, j * P:(j + 1) * P], ident)
                        ins.then_inc(soft_turned.sem, 1)

                pe.wait_ge(mla_t_ready.sem, mla_t_ready.at(l, 1))
                weighted(0, wt[0], lambda t, h: rv[:, t, h * HEAD_DIM:(h + 1) * HEAD_DIM])
                turn_weights(0)
                pe.wait_ge(wc_ready.sem, wc_ready.at(l, 1))
                weighted(2, wt[2], lambda t, h: g2[:, t, SV + h * HEAD_DIM:SV + (h + 1) * HEAD_DIM])
                for h in range(HEADS):
                    pe.wait_ge(soft_t_ready.sem, soft_t_ready.at(l, h + 1))
                    mm(work[h][:, 0:P], qd_t[0:MLA_QK, h, 0:P], kd_t[0:MLA_QK, h, 0:P], start=True, stop=True)
                    mm(work[h][:, P:BLK], qd_t[0:MLA_QK, h, P:SEQ], kd_t[0:MLA_QK, h, :], start=True, stop=True)\
                        .then_inc(soft_out.sem, 1)
                weighted(1, wt[1], lambda t, h: g2[:, t, FV + h * HEAD_DIM:FV + (h + 1) * HEAD_DIM])
                turn_weights(HEADS)
                pe.wait_ge(soft_t_ready.sem, soft_t_ready.at(l, 2 * HEADS))
                weighted(3, wt[3], lambda t, h: mla_v[:, t, h, :])

                turn(l, 1)
                wide(l, C_OUT)

                turn(l, 2)
                after_register_wait(pe)
                with pe.Fori(0, 4) as k:
                    tall_block(l, C_QUERY + k * 4, 4 + k * 2)
                pe.wait_ge(bank_free.sem, bank_free.at(l, 4 + 8))
                for t in range(T):
                    for m4 in range(4):
                        if t:
                            pe.wait_ge(score_in.sem, score_in.at(l, m4 + 1))
                        for m in range(4):
                            ins = mm(work[m4][:, m * P:(m + 1) * P], query_t[:, 4 * m4 + m, t * P:(t + 1) * P],
                                     keys_t[:, 4 * m4 + m, :], start=True, stop=True)
                        ins.then_inc(score_out.sem, 1)
                pe.wait_ge(score_in.sem, score_in.at(l, 8))
                after_register_wait(pe)

                with pe.Fori(0, UNITS) as u:
                    tall_block(l, C_U + u * 4, 12 + u * 2)

                pe.wait_ge(gates_done.sem, gates_done.at(l, 1))
                for a in range(3):
                    for t in range(T):
                        ins = pe.transpose(work[2 + a // 2][:, (a % 2) * SEQ + t * P:(a % 2) * SEQ + (t + 1) * P],
                                           picked[:, a, t, :], ident)
                ins.then_inc(picked_turned.sem, 1)
                pe.wait_ge(picked_t_in.sem, picked_t_in.at(l, 1))
                after_register_wait(pe)

                with pe.Fori(0, HALF // 4) as u:
                    tall_block(l, C_U + HALF + u * 4, 12 + HALF // 2 + u * 2,
                               lambda j: gates_of(l, 4 * u + j, j % 2))

                def v_block(i0, first, last, with_gates):
                    for j in range(4):
                        pe.wait_ge(w_head_in.sem, w_head_in.at(l, i0 + (j + 1)))
                        pe.wait_ge(w_rest_in.sem, w_rest_in.at(l, i0 + (j + 1)))
                        wide_chunk(l, C_V + i0 + j, j % 2, lambda t: w_head[:, j % 2, t * P:(t + 1) * P],
                                   lambda t: w_rest[:, j % 2, t * P:(t + 1) * P], first and j == 0, last and j == 3,
                                   (lambda: gates_of(l, GROUPS // 2 + i0 + j, j % 2)) if with_gates else None)

                v_block(0, True, False, True)
                with pe.Fori(1, HALF // 4) as v:
                    v_block(4 * v, False, False, True)
                with pe.Fori(HALF // 4, E_TILES // 4 - 1) as v:
                    v_block(4 * v, False, False, False)
                v_block(E_TILES - 4, False, True, False)

        @block.scalar
        def _(act):
            act.sem_inc(bank_free.sem, 2)

            def split_head(l, cj, slot, raw_slot):
                act.wait_ge(raw_in[raw_slot // 2].sem, raw_in[raw_slot // 2].at(l, 4 * (cj + (4 - raw_slot))))
                act.wait_ge(head_free.sem, head_free.at(l, cj - 1))
                act.wait_ge(rest_in.sem, rest_in.at(l, cj - 1))
                nc.scalar.copy(head[:, slot, :], raw[:, raw_slot, :]).then_inc(head_in.sem, 1)

            def ahead(l, c0, n, j0=0):
                for j in range(j0, j0 + n):
                    split_head(l, c0 + (j + 2), j % 2, (j + 2) % 4)

            def std(l, use, step):
                for t in range(T):
                    step(nc.scalar.activation(scratch, xs[:, t, :], ACT.Square, accum_out=ss[:, 0, t:t + 1]))
                nc.scalar.activation(ss[:, 1, :], ss[:, 0, :], ACT.Sqrt, scale=1.0 / D_MODEL, bias=eps)\
                    .then_inc(std_ready.sem, 1)

            def act_heads(l, use, g0):
                for b in range(4):
                    act.wait_ge(turned.sem, turned.at(l, 4 * use + b + 1))
                    for kt in (2 * b, 2 * b + 1):
                        ins = nc.scalar.activation(act_head[:, kt, :], work[b][:, (kt % 2) * SEQ:(kt % 2 + 1) * SEQ],
                                                   ACT.Copy, scale=gain[:, g0 + kt:g0 + kt + 1])
                    ins.then_inc(act_head_in.sem, 1)

            def weights_exp(l, base, n, scale):
                for h in range(HEADS):
                    act.wait_ge(soft_max.sem, soft_max.at(l, base + h + 1))
                    nc.scalar.activation(soft[:, h, 0:P], soft[:, h, 0:P], ACT.Exp, scale=scale,
                                         bias=mx[:, 2 * n + 1, 0, h:h + 1], accum_out=dn[:, 2 * n, 0, h:h + 1])
                    nc.scalar.activation(soft[:, h, P:BLK], soft[:, h, P:BLK], ACT.Exp, scale=scale,
                                         bias=mx[:, 2 * n + 1, 1, h:h + 1], accum_out=dn[:, 2 * n, 1, h:h + 1])\
                        .then_inc(soft_exp.sem, 1)

            def weights_t(l, base, dst):
                for h in range(HEADS):
                    act.wait_ge(soft_turned.sem, soft_turned.at(l, base + h + 1))
                    nc.scalar.copy(dst[:, h, :], work[h][:, 0:BLK]).then_inc(soft_t_ready.sem, 1)

            eps = EPS
            with act.Fori(0, DEPTH) as l:
                step = Steps(act, act_step, l)
                act.wait_ge(x_ready.sem, x_ready.at(l, 0))
                std(l, 0, step)
                for j in range(2):
                    split_head(l, j, j, j)
                act.wait_ge(small_in.sem, small_in.at(l, 48))
                act_heads(l, 0, G_MIX)
                ahead(l, C_WIDE1, 8)
                act.wait_ge(chunk_done.sem, chunk_done.at(l, C_TALL))
                for t in range(T):
                    nc.scalar.copy(rv[:, t, :], acc[2 * t + 1][:, 0:GROUP_WIDTH])
                for t in range(T):
                    ins = nc.scalar.activation(rg[:, t, :], acc[2 * t + 1][:, GROUP_WIDTH:512], ACT.Silu)
                ins.then_inc(rv_ready.sem, 1)
                for b in range(4):
                    ahead(l, C_TALL, 2, 2 * b)
                    act.wait_ge(chunk_done.sem, chunk_done.at(l, C_TALL + 2 * b + 2))
                    nc.scalar.copy(fs_t[:, 2 * b:2 * b + 2, :], work[b % 2][:].rearrange("p (j s) -> p j s", s=SEQ))\
                        .then_inc(bank_free.sem, 1)
                ahead(l, C_WIDE2, 8)

                act.wait_ge(ret_turned.sem, ret_turned.at(l, 1))
                for b in range(2):
                    ins = nc.scalar.copy(ret_t[:, 2 * b:2 * b + 2, :], work[b][:].rearrange("p (j s) -> p j s", s=SEQ))
                ins.then_inc(ret_t_ready.sem, 1)
                act.wait_ge(chunk_done.sem, chunk_done.at(l, C_OUT))
                for n in range(2):
                    ins = nc.scalar.copy(g2[:, 0, n * 512:(n + 1) * 512], acc[n][:])
                ins.then_inc(g2_act.sem, 1)
                act.wait_ge(g2_dve.sem, g2_dve.at(l, 1))
                act.wait_ge(g2_act.sem, g2_act.at(l, 1))
                for a, (c0, n) in enumerate(((CQ, MLA_Q_RANK), (CKV, MLA_KV_RANK))):
                    for t in range(T):
                        step(nc.scalar.activation(scratch[:, 0:n], g2[:, t, c0:c0 + n], ACT.Square,
                                                  accum_out=css[:, 0, a, t:t + 1]))
                nc.scalar.activation(css[:, 1, 0, :], css[:, 0, 0, :], ACT.Sqrt, scale=1.0 / MLA_Q_RANK, bias=eps)
                nc.scalar.activation(css[:, 1, 1, :], css[:, 0, 1, :], ACT.Sqrt, scale=1.0 / MLA_KV_RANK, bias=eps)\
                    .then_inc(cstd_ready.sem, 1)
                for h in range(HEADS):
                    act.wait_ge(sc_out.sem, sc_out.at(l, h + 1))
                    nc.scalar.activation(zs[:, h, :], work[h][:, 0:BLK], ACT.Copy, scale=SCALE).then_inc(zs_ready.sem, 1)
                act.wait_ge(ff_ready.sem, ff_ready.at(l, 1))
                step(nc.scalar.activation(lf[:, 1, :, :], lf[:, 0, :, :], ACT.Abs))
                step(nc.scalar.activation(lf[:, 1, :, :], lf[:, 1, :, :], ACT.Exp, scale=-1.0))
                nc.scalar.activation(lf[:, 1, :, :], lf[:, 1, :, :], ACT.Ln, bias=1.0).then_inc(ffl_ready.sem, 1)
                act.wait_ge(c_turned.sem, c_turned.at(l, 1))
                for j in range(3):
                    ins = nc.scalar.activation(c_t[:, j, :], acc[2 + j // 2][:, (j % 2) * SEQ:(j % 2 + 1) * SEQ], ACT.Copy,
                                               scale=gain[:, G_CQ + j:G_CQ + j + 1])
                ins.then_inc(c_t_ready.sem, 1)
                act.wait_ge(zs_ready.sem, zs_ready.at(l, HEADS))
                step(nc.scalar.activation(za[:, :, :], zs[:, :, :], ACT.Abs))
                step(nc.scalar.activation(za[:, :, :], za[:, :, :], ACT.Exp, scale=-1.0))
                nc.scalar.activation(za[:, :, :], za[:, :, :], ACT.Ln, bias=1.0).then_inc(lc_ready.sem, 1)
                act.wait_ge(mla_out.sem, mla_out.at(l, 1))
                act.wait_ge(krot_ready.sem, krot_ready.at(l, 1))
                for t in range(T):
                    kv = acc[2 + t][:].rearrange("p (h n) -> p h n", h=HEADS)
                    nc.scalar.copy(mla_k[:, t, :, 0:HEAD_DIM], kv[:, :, 0:HEAD_DIM])
                    nc.scalar.copy(mla_v[:, t, :, :], kv[:, :, HEAD_DIM:])
                    ins = nc.scalar.copy(mla_k[:, t, :, HEAD_DIM:MLA_QK],
                                         krot[:, t:t + 1, :].to_broadcast([P, HEADS, MLA_ROPE]))
                ins.then_inc(mla_kv_ready.sem, 1)
                act.wait_ge(mla_turned.sem, mla_turned.at(l, 1))
                for a, dst in enumerate((qd_t, kd_t)):
                    for b in range(2):
                        ins = nc.scalar.copy(dst[0:MLA_QK, 2 * b:2 * b + 2, :],
                                             acc[2 * a + b][0:MLA_QK, :].rearrange("p (h s) -> p h s", s=SEQ))
                ins.then_inc(mla_t_ready.sem, 1)
                act.wait_ge(logw_ready.sem, logw_ready.at(l, HEADS))
                nc.scalar.activation(za[:, :, :], zs[:, :, :], ACT.Exp).then_inc(ew_ready.sem, 1)
                weights_exp(l, 0, 0, SCALE)
                weights_t(l, 0, wt[1])
                weights_exp(l, HEADS, 1, SCALE_MLA)
                weights_t(l, HEADS, wt[3])
                act.wait_ge(hss_ready.sem, hss_ready.at(l, 1))
                nc.scalar.activation(hss[:, 1, :], hss[:, 0, :], ACT.Sqrt, scale=1.0 / HEAD_DIM, bias=eps)\
                    .then_inc(hstd_ready.sem, 1)
                act_heads(l, 1, G_HEAD)
                ahead(l, C_OUT, 8)

                act.wait_ge(x_mid.sem, x_mid.at(l, 1))
                std(l, 1, step)
                act_heads(l, 2, G_FFN)
                with act.Fori(0, 4) as k:
                    for b in range(2):
                        ahead(l, C_QUERY + k * 4, 2, 2 * b)
                        act.wait_ge(chunk_done.sem, chunk_done.at(l, C_QUERY + k * 4 + (2 * b + 2)))
                        nc.scalar.copy(query_t[:, bass.ds(k * 4 + 2 * b, 2), :],
                                       work[b][:].rearrange("p (j s) -> p j s", s=SEQ)).then_inc(bank_free.sem, 1)
                for t in range(T):
                    for m4 in range(4):
                        act.wait_ge(score_out.sem, score_out.at(l, 4 * t + m4 + 1))
                        at = (SCORE_SLOT + t * PEER_HEADS + 2 * m4) * SEQ
                        nc.scalar.copy(arena[:, at:at + 512], work[m4][:]).then_inc(score_in.sem, 1)
                nc.scalar.preload_act_table(ACT.Gelu)

                def activations(i0):
                    for b in range(2):
                        ahead(l, C_U + i0, 2, 2 * b)
                        act.wait_ge(chunk_done.sem, chunk_done.at(l, C_U + i0 + (2 * b + 2)))
                        nc.scalar.activation(acts[:, bass.ds(i0 + 2 * b, 2), :],
                                             work[b][:].rearrange("p (j s) -> p j s", s=SEQ), ACT.Gelu)\
                            .then_inc(bank_free.sem, 1)

                with act.Fori(0, UNITS) as u:
                    act.wait_ge(unit_done.sem, unit_done.at(l, u))
                    nc.scalar.copy(stage[:, :, :], scores(u).rearrange("p (a n) -> p a n", a=2)).then_inc(staged.sem, 1)
                    activations(u * 4)
                act.wait_ge(unit_done.sem, unit_done.at(l, UNITS))
                nc.scalar.activation(picked[:, 2, :, :], picked[:, 2, :, :], ACT.Exp).then_inc(gate_exp.sem, 1)
                nc.scalar.preload_act_table(ACT.Gelu)
                with act.Fori(0, HALF // 4) as u:
                    activations(HALF + u * 4)

                def weight_head(i, slot):
                    act.wait_ge(chunk_done.sem, chunk_done.at(l, C_V + i - 1))
                    act.wait_ge(w_rest_in.sem, w_rest_in.at(l, i - 1))
                    nc.scalar.copy(w_head[:, slot, :], acts[:, i, :]).then_inc(w_head_in.sem, 1)

                def v_block(i0, last):
                    for j in range(4):
                        if isinstance(i0, int) and i0 + j + 1 == HALF:
                            act.wait_ge(gate_used.sem, gate_used.at(l, GROUPS))
                        if not (last and j == 3):
                            weight_head(i0 + (j + 1), (j + 1) % 2)
                        if not (last and j >= 2):
                            split_head(l, C_V + i0 + (j + 2), j % 2, (j + 2) % 4)

                act.wait_ge(gate_used.sem, gate_used.at(l, GROUPS // 2))
                weight_head(0, 0)
                v_block(0, False)
                with act.Fori(1, HALF // 4 - 1) as v:
                    v_block(4 * v, False)
                v_block(HALF - 4, False)
                with act.Fori(HALF // 4, E_TILES // 4 - 1) as v:
                    v_block(4 * v, False)
                v_block(E_TILES - 4, True)
                assert step.n == ACT_STEPS, step.n
            act.wait_ge(x_ready.sem, DEPTH + 1)
            for t in range(T):
                nc.scalar.activation(arena[:, (2 + t) * D_MODEL:(3 + t) * D_MODEL], xs[:, t, :], ACT.Square,
                                     accum_out=ss[:, 0, t:t + 1]).then_inc(act_step.sem, 1)
            act.wait_ge(act_step.sem, DEPTH * ACT_STEPS + 2)
            nc.scalar.activation(ss[:, 1, :], ss[:, 0, :], ACT.Sqrt, scale=1.0 / D_MODEL, bias=eps)\
                .then_inc(std_ready.sem, 1)
            act.wait_ge(rot_ready.sem, DEPTH + 1)
            act.dma_start(out, xs[:]).then_inc(out_done.sem, 16)
            act.wait_ge(out_done.sem, 16)

        @block.vector
        def _(dve):
            tt, ts = nc.vector.tensor_tensor, nc.vector.tensor_scalar
            dve.sem_inc(rest_in.sem, 2)
            dve.sem_inc(unit_done.sem, 1)
            dve.sem_inc(gate_used.sem, 2)
            dve.sem_inc(w_rest_in.sem, 2)
            dve.wait_ge(x_in.sem, 16)
            dve.sem_inc(x_ready.sem, 1)

            def split_rest(l, cj, slot, raw_slot):
                dve.wait_ge(head_in.sem, head_in.at(l, cj + 1))
                dve.wait_ge(chunk_done.sem, chunk_done.at(l, cj - 1))
                tt(rest[:, slot, :], raw[:, raw_slot, :], head[:, slot, :].bitcast(F32), ALU.subtract)\
                    .then_inc(rest_in.sem, 1)

            def ahead(l, c0, n, j0=0):
                for j in range(j0, j0 + n):
                    split_rest(l, c0 + (j + 1), (j + 1) % 2, (j + 1) % 4)

            def norm_tokens(l, use, step):
                dve.wait_ge(std_ready.sem, std_ready.at(l, use + 1))
                step(nc.vector.reciprocal(ss[:, 1, :], ss[:, 1, :]))
                for t in range(T):
                    ins = ts(xn[:, t, :], xs[:, t, :], ss[:, 1, t:t + 1], None, ALU.mult)
                ins.then_inc(xn_ready.sem, 1)

            def act_rests(l, use, g0):
                for b in range(4):
                    dve.wait_ge(act_head_in.sem, act_head_in.at(l, 4 * use + b + 1))
                    for kt in (2 * b, 2 * b + 1):
                        ins = nc.vector.scalar_tensor_tensor(
                            out=act_rest[:, kt, :], in0=work[b][:, (kt % 2) * SEQ:(kt % 2 + 1) * SEQ],
                            scalar=gain[:, g0 + kt:g0 + kt + 1], in1=act_head[:, kt, :].bitcast(F32),
                            op0=ALU.mult, op1=ALU.subtract)
                    ins.then_inc(act_rest_in.sem, 1)

            def rope(dst, src, table, heads, half, tmp, step):
                n = 2 * half
                cos, sin = table
                a = tmp[:, 0:heads * n].rearrange("p (h n) -> p h n", h=heads)
                b = tmp[:, 512:512 + heads * n].rearrange("p (h n) -> p h n", h=heads)
                tt(a, src, cos[:, None, :].to_broadcast([P, heads, n]), ALU.mult)
                tt(b[:, :, 0:half], src[:, :, half:n], sin[:, None, 0:half].to_broadcast([P, heads, half]), ALU.mult)
                step(tt(b[:, :, half:n], src[:, :, 0:half], sin[:, None, half:n].to_broadcast([P, heads, half]), ALU.mult))
                ins = tt(dst, a, b, ALU.add)
                return ins

            def table(name, dim, t):
                v = c[name].rearrange("p (a t n) -> p a t n", a=2, t=T)
                return v[:, 0, t, :], v[:, 1, t, :]

            def weights_max(l, base, n, scale, step):
                for h in range(HEADS):
                    dve.wait_ge(soft_out.sem, soft_out.at(l, base + h + 1))
                    if base:
                        dve.wait_ge(soft_turned.sem, soft_turned.at(l, h + 1))
                    step(tt(soft[:, h, :], work[h][:, 0:BLK], c["causal"], ALU.add))
                    nc.vector.reduce_max(mx[:, 2 * n, 0, h:h + 1], soft[:, h, 0:P], AX_X)
                    step(nc.vector.reduce_max(mx[:, 2 * n, 1, h:h + 1], soft[:, h, P:BLK], AX_X))
                    ts(mx[:, 2 * n + 1, :, h], mx[:, 2 * n, :, h], -scale, None, ALU.mult).then_inc(soft_max.sem, 1)

            with dve.Fori(0, DEPTH) as l:
                step = Steps(dve, dve_step, l)
                norm_tokens(l, 0, step)
                split_rest(l, 0, 0, 0)
                act_rests(l, 0, G_MIX)
                ahead(l, C_WIDE1, 8)
                dve.wait_ge(chunk_done.sem, chunk_done.at(l, C_TALL))
                dve.wait_ge(small_in.sem, small_in.at(l, 48))
                for t in range(T):
                    ahead(l, C_TALL, 2, 2 * t)
                    src = acc[2 * t][:].rearrange("p (h n) -> p h n", n=HEAD_DIM)
                    dst = rot[:, t, :].rearrange("p (h n) -> p h n", n=HEAD_DIM)
                    ins = rope(dst, src, table("rope64", HEAD_DIM, t), 8, HEAD_DIM // 2, spare, step)
                    if t == 0:
                        step(ins)
                ins.then_inc(rot_ready.sem, 1)
                ahead(l, C_TALL, 4, 4)
                ahead(l, C_WIDE2, 8)
                dve.wait_ge(chunk_done.sem, chunk_done.at(l, C_OUT))
                for n in range(2):
                    ins = nc.vector.tensor_copy(g2[:, 1, n * 512:(n + 1) * 512], acc[2 + n][:])
                ins.then_inc(g2_dve.sem, 1)
                dve.wait_ge(g2_dve.sem, g2_dve.at(l, 1))
                dve.wait_ge(g2_act.sem, g2_act.at(l, 1))
                tt(lf[:, 0, :, :], g2[:, :, FF:FF + HEADS],
                   gain[:, None, G_BF:G_BF + HEADS].to_broadcast([P, T, HEADS]), ALU.add).then_inc(ff_ready.sem, 1)
                for t in range(T):
                    src = g2[:, t, None, KR:KR + MLA_ROPE]
                    ins = rope(krot[:, t, None, :], src, table("rope32", MLA_ROPE, t), 1, MLA_ROPE // 2, spare, step)
                    if t == 0:
                        step(ins)
                ins.then_inc(krot_ready.sem, 1)
                decay = c["decay"].rearrange("p (h n) -> p h n", h=HEADS)
                for h in range(HEADS):
                    dve.wait_ge(sa_out.sem, sa_out.at(l, h + 1))
                    tt(wt[0][:, h, :], work[h][:, 0:BLK], decay[:, h, :], ALU.mult).then_inc(wa_ready.sem, 1)
                dve.wait_ge(cstd_ready.sem, cstd_ready.at(l, 1))
                step(nc.vector.reciprocal(css[:, 1, :, :], css[:, 1, :, :]))
                for t in range(T):
                    ts(cn[:, t, 0:256], g2[:, t, CQ:CKV], css[:, 1, 0, t:t + 1], None, ALU.mult)
                    ins = ts(cn[:, t, 256:384], g2[:, t, CKV:KR], css[:, 1, 1, t:t + 1], None, ALU.mult)
                ins.then_inc(cn_ready.sem, 1)
                dve.wait_ge(ffl_ready.sem, ffl_ready.at(l, 1))
                nc.vector.scalar_tensor_tensor(out=lf[:, 0, :, :], in0=lf[:, 0, :, :], scalar=0.0, in1=lf[:, 1, :, :],
                                               op0=ALU.min, op1=ALU.subtract).then_inc(ls_ready.sem, 1)
                step(nc.vector.memset(fc[:, :, :], 1.0))
                dve.wait_ge(fcum_out.sem, fcum_out.at(l, 1))
                cum = acc[0][:, 0:2 * HEADS].rearrange("p (t h) -> p t h", t=T)
                ts(fc[:, :, 0:HEADS], cum, 1.0 / SCALE, None, ALU.mult)
                ts(fc[:, :, 8 + HEADS:16], cum, -1.0 / SCALE, None, ALU.mult).then_inc(fc_ready.sem, 1)
                dve.wait_ge(fc_turned.sem, fc_turned.at(l, 1))
                step(nc.vector.tensor_copy(fc_t[0:8, :], work[0][0:8, :]))
                for h in range(HEADS):
                    ins = ts(fc_h[0:8, h, :], fc_t[0:8, 0:SEQ], c["pick"][0:8, h:h + 1], None, ALU.mult)
                ins.then_inc(fc_t_ready.sem, 1)
                dve.wait_ge(lc_ready.sem, lc_ready.at(l, 1))
                step(nc.vector.scalar_tensor_tensor(out=za[:, :, :], in0=zs[:, :, :], scalar=0.0, in1=za[:, :, :],
                                                    op0=ALU.max, op1=ALU.add))
                strict = c["strict"][:, None, :].to_broadcast([P, HEADS, BLK])
                tt(za[:, :, :], za[:, :, :], strict, ALU.mult).then_inc(sp_ready.sem, 1)
                dve.wait_ge(mla_out.sem, mla_out.at(l, 1))
                for t in range(T):
                    src = acc[t][:, 0:HEADS * MLA_QK].rearrange("p (h n) -> p h n", h=HEADS)
                    nc.vector.tensor_copy(mla_q[:, t, :, 0:HEAD_DIM], src[:, :, 0:HEAD_DIM])
                    ins = rope(mla_q[:, t, :, HEAD_DIM:MLA_QK], src[:, :, HEAD_DIM:MLA_QK],
                               table("rope32", MLA_ROPE, t), HEADS, MLA_ROPE // 2, spare, step)
                    if t == 0:
                        step(ins)
                ins.then_inc(mla_q_ready.sem, 1)
                for h in range(HEADS):
                    dve.wait_ge(cum_out.sem, cum_out.at(l, h + 1))
                    tt(zs[:, h, :], zs[:, h, :], work[h][:, 0:BLK], ALU.subtract).then_inc(logw_ready.sem, 1)
                weights_max(l, 0, 0, SCALE, step)
                dve.wait_ge(ew_ready.sem, ew_ready.at(l, 1))
                tt(wt[2][:, :, :], za[:, :, :], strict, ALU.mult).then_inc(wc_ready.sem, 1)
                weights_max(l, HEADS, 1, SCALE_MLA, step)

                def heads(v):
                    return v.rearrange("p (n d) -> p n d", d=HEAD_DIM)

                def each(v):
                    return v[:, :, None].to_broadcast([P, T * HEADS, HEAD_DIM])

                dve.wait_ge(o_out.sem, o_out.at(l, 1))
                step(nc.vector.reduce_sum(mean[:, 0, :], heads(acc[0][:]), AX_X))
                step(ts(mean[:, 1, :], mean[:, 0, :], 1.0 / HEAD_DIM, None, ALU.mult))
                tt(heads(ya[:, 0, :]), heads(acc[0][:]), each(mean[:, 1, :]), ALU.subtract)
                dve.wait_ge(o_out.sem, o_out.at(l, 2))
                nc.vector.tensor_copy(ya[:, 2, :], acc[2][:])
                for n, g in enumerate((1, 3)):
                    dve.wait_ge(o_out.sem, o_out.at(l, 3 + n))
                    step(nc.vector.reciprocal(dn[:, 2 * n + 1, :, :], dn[:, 2 * n, :, :]))
                    ins = tt(heads(ya[:, g, :]), heads(acc[g][:]),
                             each(dn[:, 2 * n + 1, :, :].rearrange("p t h -> p (t h)")), ALU.mult)
                step(ins)
                step(tt(ysq[:, :, :], ya[:, :, :], ya[:, :, :], ALU.mult))
                nc.vector.reduce_sum(hss[:, 0, :], heads(ysq.rearrange("p g n -> p (g n)")), AX_X)\
                    .then_inc(hss_ready.sem, 1)
                dve.wait_ge(hstd_ready.sem, hstd_ready.at(l, 1))
                step(nc.vector.reciprocal(hss[:, 1, :], hss[:, 1, :]))
                for g in range(4):
                    ins = tt(xn[:, :, g * GROUP_WIDTH:(g + 1) * GROUP_WIDTH].rearrange("p t (h d) -> p t h d", d=HEAD_DIM),
                             ya[:, g, :].rearrange("p (t h d) -> p t h d", t=T, d=HEAD_DIM),
                             hss[:, 1, 8 * g:8 * g + 8].rearrange("p (t h) -> p t h", t=T)[:, :, :, None]
                             .to_broadcast([P, T, HEADS, HEAD_DIM]), ALU.mult)
                step(ins)
                tt(xn[:, :, 0:GROUP_WIDTH], xn[:, :, 0:GROUP_WIDTH], rg[:, :, :], ALU.mult).then_inc(xn_ready.sem, 1)

                act_rests(l, 1, G_HEAD)
                ahead(l, C_OUT, 8)

                def add_residual(done):
                    dve.wait_ge(chunk_done.sem, chunk_done.at(l, done))
                    for t in range(T):
                        for n in range(2):
                            x_part = xs[:, t, n * 512:(n + 1) * 512]
                            ins = tt(x_part, x_part, acc[2 * t + n][:], ALU.add)
                    return ins

                add_residual(C_QUERY).then_inc(x_mid.sem, 1)

                dve.wait_ge(x_mid.sem, x_mid.at(l, 1))
                norm_tokens(l, 1, step)
                act_rests(l, 2, G_FFN)
                with dve.Fori(0, 4) as k:
                    ahead(l, C_QUERY + k * 4, 4)
                dve.wait_ge(score_in.sem, score_in.at(l, 8))
                after_register_wait(dve)
                with dve.Fori(0, UNITS) as u:
                    marks = [0]

                    def mark(ins):
                        ins.then_inc(route_step.sem, 1)
                        marks[0] += 1
                        return marks[0]

                    def seen(n):
                        dve.wait_ge(route_step.sem, l * route_step.per + u * ROUTE_STEPS + n)
                        after_register_wait(dve)

                    vec = nc.vector
                    first_s, second_s = stage[:, 0, :], stage[:, 1, :]
                    ahead(l, C_U + u * 4, 1)
                    dve.wait_ge(staged.sem, staged.at(l, u + 1))
                    after_register_wait(dve)
                    a = mark(vec.max(top_v[:, 0, 0:8], first_s))
                    b = mark(vec.max(top_v[:, 1, 0:8], second_s))
                    seen(a)
                    vec.max_index(top_i[:, 0, 0:8], top_v[:, 0, 0:8], first_s)
                    a = mark(vec.match_replace(left[:, 0, :], top_v[:, 0, 0:8], first_s, NEG_OUT))
                    seen(b)
                    vec.max_index(top_i[:, 1, 0:8], top_v[:, 1, 0:8], second_s)
                    b = mark(vec.match_replace(left[:, 1, :], top_v[:, 1, 0:8], second_s, NEG_OUT))
                    seen(a)
                    a = mark(vec.max(top_v[:, 0, 8:16], left[:, 0, :]))
                    seen(b)
                    b = mark(vec.max(top_v[:, 1, 8:16], left[:, 1, :]))
                    ahead(l, C_U + u * 4, 1, 1)
                    seen(b)
                    vec.max_index(top_i[:, 0, 8:16], top_v[:, 0, 8:16], left[:, 0, :])
                    a = mark(vec.max_index(top_i[:, 1, 8:16], top_v[:, 1, 8:16], left[:, 1, :]))
                    b = mark(tt(cand[:, :].rearrange("p (a b) -> p a b", a=TOPK),
                                top_v[:, 0, :, None].to_broadcast([P, TOPK, TOPK]),
                                top_v[:, 1, None, :].to_broadcast([P, TOPK, TOPK]), ALU.add))
                    seen(a)
                    vec.tensor_copy(top_f[:, :, :], top_i[:, :, :])
                    seen(b)
                    a = mark(vec.max(best_v[:, 0:8], cand[:, :]))
                    seen(a)
                    vec.max_index(best_i[:, 0:8], best_v[:, 0:8], cand[:, :])
                    left_c = left[:, :, :].rearrange("p a n -> p (a n)")
                    a = mark(vec.match_replace(left_c, best_v[:, 0:8], cand[:, :], NEG_OUT))
                    ahead(l, C_U + u * 4, 1, 2)
                    seen(a)
                    seen(mark(vec.max(best_v[:, 8:16], left_c)))
                    seen(mark(vec.max_index(best_i[:, 8:16], best_v[:, 8:16], left_c)))
                    ts(rank_i[:, 0, :], best_i[:, :], 4, None, ALU.logical_shift_right)
                    a = mark(ts(rank_i[:, 1, :], best_i[:, :], 15, None, ALU.bitwise_and))
                    flat = picked[:, :, :, :].rearrange("p a t n -> p a (t n)")[:, :, bass.ds(u * TOPK, TOPK)]
                    ts(flat[:, 2, :], best_v[:, :], best_v[:, 0:1], None, ALU.subtract)
                    seen(a)
                    seen(mark(vec.tensor_copy(rank_f[:, :, :], rank_i[:, :, :])))
                    m = match[:, :, :].rearrange("p a (k r) -> p (a k) r", k=TOPK)
                    seen(mark(tt(m, rank_f[:, :, :].rearrange("p a k -> p (a k)")[:, :, None]
                                 .to_broadcast([P, 2 * TOPK, TOPK]),
                                 iota[:, None, 0:TOPK].to_broadcast([P, 2 * TOPK, TOPK]), ALU.is_equal)))
                    m = match[:, :, :].rearrange("p a (k r) -> p a k r", k=TOPK)
                    a = mark(tt(m, m, top_f[:, :, None, :].to_broadcast([P, 2, TOPK, TOPK]), ALU.mult))
                    ahead(l, C_U + u * 4, 1, 3)
                    seen(a)
                    vec.reduce_sum(flat[:, 0:2, :], m, AX_X).then_inc(unit_done.sem, 1)
                    assert marks[0] == ROUTE_STEPS, marks[0]
                gate = picked[:, 2, :, :].rearrange("p t (h k) -> p (t h) k", k=TOPK)
                gsum = gs[:, :, :, :].rearrange("p a t h -> p a (t h)")
                dve.wait_ge(gate_exp.sem, gate_exp.at(l, 1))
                step(nc.vector.reduce_sum(gsum[:, 0, :], gate, AX_X))
                step(nc.vector.reciprocal(gsum[:, 1, :], gsum[:, 0, :]))
                tt(gate, gate, gsum[:, 1, :, None].to_broadcast([P, UNITS, TOPK]), ALU.mult).then_inc(gates_done.sem, 1)
                dve.wait_ge(picked_turned.sem, picked_turned.at(l, 1))
                nc.vector.tensor_copy(picked_t[:, 0:2, :], work[2][:].rearrange("p (a s) -> p a s", a=2))
                nc.vector.tensor_copy(picked_t[:, 2, :], work[3][:, 0:SEQ]).then_inc(picked_t_in.sem, 1)
                dve.wait_ge(picked_t_in.sem, picked_t_in.at(l, 1))
                after_register_wait(dve)

                def make_hot(half, g, b):
                    now = bass.ds(4 * g, 4) if not isinstance(g, int) else slice(4 * g, 4 * g + 4)
                    tt(hot1[:, b, :, :], iota[:, None, half * HALF:(half + 1) * HALF].to_broadcast([P, 4, HALF]),
                       picked_t[:, 0, now, None].to_broadcast([P, 4, HALF]), ALU.is_equal)
                    for q in range(4):
                        tok = bass.ds(4 * g + q, 1) if not isinstance(g, int) else slice(4 * g + q, 4 * g + q + 1)
                        ins = ts(hot2[:, b, q, :], iota, picked_t[:, 1, tok], picked_t[:, 2, tok],
                                 ALU.is_equal, ALU.mult)
                    ins.then_inc(hot_ready.sem, 1)

                def apply_gates(half, g, b):
                    dve.wait_ge(gate_out.sem, gate_out.at(l, half * (GROUPS // 2) + g + 1))
                    now = bass.ds(4 * g, 4) if not isinstance(g, int) else slice(4 * g, 4 * g + 4)
                    a = acts[:, half * HALF:(half + 1) * HALF, now]
                    tt(a, a, work[2 + b][:, 0:4 * HALF].rearrange("p (q i) -> p i q", q=4), ALU.mult)\
                        .then_inc(gate_used.sem, 1)

                with dve.Fori(0, HALF // 4) as u:
                    for j in range(4):
                        make_hot(0, 4 * u + j, j % 2)
                        ahead(l, C_U + HALF + u * 4, 1, j)
                        apply_gates(0, 4 * u + j, j % 2)

                def weight_rest(i, slot):
                    dve.wait_ge(w_head_in.sem, w_head_in.at(l, i + 1))
                    dve.wait_ge(chunk_done.sem, chunk_done.at(l, C_V + i - 1))
                    tt(w_rest[:, slot, :], acts[:, i, :], w_head[:, slot, :].bitcast(F32), ALU.subtract)\
                        .then_inc(w_rest_in.sem, 1)

                def v_block(i0, last, with_gates):
                    for j in range(4):
                        if with_gates:
                            make_hot(1, i0 + j, j % 2)
                        if not (last and j == 3):
                            ahead(l, C_V + i0, 1, j)
                            if not (with_gates and j == 3):
                                weight_rest(i0 + (j + 1), (j + 1) % 2)
                        if with_gates:
                            apply_gates(1, i0 + j, j % 2)
                            if j == 3:
                                weight_rest(i0 + (j + 1), (j + 1) % 2)

                weight_rest(0, 0)
                v_block(0, False, True)
                with dve.Fori(1, HALF // 4) as v:
                    v_block(4 * v, False, True)
                with dve.Fori(HALF // 4, E_TILES // 4 - 1) as v:
                    v_block(4 * v, False, False)
                v_block(E_TILES - 4, True, False)
                add_residual(CHUNKS).then_inc(x_ready.sem, 1)
                assert step.n == DVE_STEPS, step.n
            dve.wait_ge(std_ready.sem, DEPTH * 2 + 1)
            nc.vector.reciprocal(ss[:, 1, :], ss[:, 1, :]).then_inc(dve_step.sem, 1)
            dve.wait_ge(dve_step.sem, DEPTH * DVE_STEPS + 1)
            dve.wait_ge(fixed_in.sem, 32)
            for t in range(T):
                ins = nc.vector.scalar_tensor_tensor(out=xs[:, t, :], in0=xs[:, t, :], scalar=ss[:, 1, t:t + 1],
                                                     in1=arena[:, 0:D_MODEL], op0=ALU.mult, op1=ALU.mult)
            ins.then_inc(rot_ready.sem, 1)


def stream_layout(w_in, w_out, w_query, expert_u, expert_v):
    w = GROUP_WIDTH
    cols = np.cumsum([0] + [w] * 7 + [HEADS] + [w] * 3 + [MLA_Q_RANK, MLA_KV_RANK, MLA_ROPE])
    rq, rk, rv, rg, fq, fk, fv, ff, sq, sk, sv, cq, ckv, kr = (
        w_in[:, a:b] for a, b in zip(cols[:-1], cols[1:]))

    def wide(m):
        return m.reshape(-1, P, CHUNK)

    def tall(m):
        return m.reshape(KT, P, -1, P).transpose(2, 1, 0, 3).reshape(-1, P, CHUNK)

    second = np.concatenate([fv, sv, cq, ckv, kr, ff], 1)
    second = np.pad(second, ((0, 0), (0, D_MODEL - second.shape[1])))
    experts = expert_u.reshape(E_TILES, P, KT, P).transpose(0, 3, 2, 1).reshape(-1, P, CHUNK)
    chunks = np.concatenate([
        wide(np.concatenate([rq, rk, rv, rg], 1)), tall(np.concatenate([fq, fk, sq, sk], 1)),
        wide(second), wide(w_out), tall(w_query), experts, wide(expert_v)])
    return chunks.reshape(PAIRS, 2, P, CHUNK).transpose(0, 2, 1, 3)


def kernel(x, norm_mix, w_in, b_forget, norm_cq, norm_ckv, w_uq, w_ukv, head_gain, w_out,
           norm_ffn, w_query, sub_keys, expert_u, expert_v, norm_final):
    import concourse.bacc as bacc
    from concourse.bass_utils import run_bass_kernel_spmd

    def a(v):
        return np.asarray(v)

    def per_partition(v):
        return a(v).reshape(DEPTH, -1, P).transpose(0, 2, 1)

    stream = np.concatenate([stream_layout(a(w_in)[l], a(w_out)[l], a(w_query)[l], a(expert_u)[l], a(expert_v)[l])
                             for l in range(DEPTH)])
    gains = np.concatenate([
        per_partition(norm_mix), per_partition(head_gain), per_partition(norm_ffn), per_partition(norm_cq),
        per_partition(norm_ckv), np.broadcast_to(a(b_forget)[:, None, :], (DEPTH, P, HEADS))], 2)
    small = np.concatenate([
        a(w_uq).reshape(DEPTH, 2, P, -1).transpose(0, 2, 1, 3).reshape(DEPTH, P, -1), a(w_ukv),
        a(sub_keys).transpose(0, 4, 1, 2, 3).reshape(DEPTH, P, -1)], 2)
    tables = constants()
    arrays = {
        "x": a(x).reshape(T, P, D_MODEL).transpose(1, 0, 2),
        "stream": stream,
        "gains": gains,
        "small": small,
        "mixer_consts": np.concatenate([tables[n] for n, _ in MIXER_CONSTS], 1),
        "fixed_consts": np.concatenate([np.eye(P), np.tile(np.arange(P), (P, 1))], 1),
        "gain_final": a(norm_final).reshape(1, D_MODEL),
    }
    arrays = {n: np.ascontiguousarray(v, dtype=np.float32) for n, v in arrays.items()}
    nc = bacc.Bacc("TRN2", target_bir_lowering=False, num_devices=1)
    args = {n: nc.dram_tensor(n, v.shape, F32, kind="ExternalInput").ap() for n, v in arrays.items()}
    out = nc.dram_tensor("out", (P, T, D_MODEL), F32, kind="ExternalOutput").ap()
    hybrid_ret_fox_sb_mla_peer(nc, **args, out=out)
    r = run_bass_kernel_spmd(nc, [arrays], core_ids=[0])
    return r.results[0]["out"].transpose(1, 0, 2).reshape(1, SEQ, D_MODEL)
```

```python
from contextlib import ExitStack

import numpy as np

import concourse.bass as bass
from concourse import mybir

F32 = mybir.dt.float32
F32R = mybir.dt.float32r
U32 = mybir.dt.uint32
ACT = mybir.ActivationFunctionType
ALU = mybir.AluOpType
AX_X = mybir.AxisListType.X

P = 128
D_MODEL = 1024
SEQ = 256
DEPTH = 2
HEADS = 4
HEAD_DIM = 64
GROUP_WIDTH = HEADS * HEAD_DIM
MLA_Q_RANK = 256
MLA_KV_RANK = 128
MLA_ROPE = 32
MLA_QK = HEAD_DIM + MLA_ROPE
PEER_HEADS = 8
PEER_KEYS = 128
TOPK = 16
EPS = 1e-6
ROPE_BASE = 10000.0
SCALE = HEAD_DIM ** -0.5
SCALE_MLA = MLA_QK ** -0.5

T = SEQ // P
KT = D_MODEL // P
CHUNK = KT * P
E_TILES = PEER_KEYS
STRIDE = 6
C_WIDE1, C_TALL, C_WIDE2, C_OUT, C_QUERY, C_U = 0, 8, 16, 24, 32, 48
C_V = C_U + E_TILES
CHUNKS = C_V + E_TILES
PAIRS = CHUNKS // 2

BLK = 3 * P

FV, SV, CQ, CKV, KR, FF = 0, 256, 512, 768, 896, 928
NEG_BIG = -1e30
NEG_OUT = -3.0e38

ACT_STEPS, DVE_STEPS, ROUTE_STEPS = 12, 49, 16

G_MIX, G_HEAD, G_FFN, G_CQ, G_CKV, G_BF, GAINS = 0, 8, 16, 24, 26, 27, 31
W_UQ, W_UKV, W_KEYS, SMALL = 0, 768, 1280, 1280 + 16 * PEER_KEYS


def constants():
    i = np.arange(P, dtype=np.float32)
    k, q = i[:, None], i[None, :]
    tri_ge = (k >= q).astype(np.float32)
    tri_le = (k <= q).astype(np.float32)
    ones = np.ones((P, P), np.float32)
    gamma = np.log1p(-(2.0 ** (-5.0 - np.arange(HEADS, dtype=np.float32))))
    decay = np.zeros((P, HEADS, BLK), np.float32)
    for h in range(HEADS):
        near = np.where(q >= k, np.exp(gamma[h] * np.maximum(q - k, 0.0)), 0.0)
        far = np.exp(gamma[h] * (q + P - k))
        decay[:, h] = np.concatenate([near, far, near], 1) * SCALE
    late = np.where(k >= q, 0.0, NEG_BIG)
    causal = np.concatenate([late, 0 * late, late], 1)
    strict = np.concatenate([(k < q), np.ones((P, P), bool), (k < q)], 1)
    pos = np.arange(SEQ, dtype=np.float32)

    def rope(dim):
        inv = ROPE_BASE ** (-np.arange(0, dim, 2, dtype=np.float32) / dim)
        ang = (pos[:, None] * inv[None, :]).astype(np.float32)
        cos, sin = np.cos(ang), np.sin(ang)
        table = np.stack([np.concatenate([cos, cos], 1), np.concatenate([-sin, sin], 1)])
        return table.reshape(2, T, P, dim).transpose(2, 0, 1, 3).reshape(P, -1)

    pick = np.zeros((P, HEADS), np.float32)
    for h in range(HEADS):
        pick[h, h] = pick[HEADS + h, h] = 1.0
    return {
        "tri_ge": tri_ge, "tri_le": tri_le, "ones": ones, "decay": decay.reshape(P, -1),
        "causal": causal, "strict": strict, "rope64": rope(HEAD_DIM), "rope32": rope(MLA_ROPE),
        "pick": pick,
    }


MIXER_CONSTS = [("tri_ge", P), ("tri_le", P), ("ones", P), ("decay", HEADS * BLK), ("causal", BLK),
                ("strict", BLK), ("rope64", 2 * T * HEAD_DIM), ("rope32", 2 * T * MLA_ROPE), ("pick", HEADS)]
MIXER_CONST_COLS = sum(n for _, n in MIXER_CONSTS)


def hybrid_ret_fox_sb_mla_peer(nc, x, stream, gains, small, mixer_consts, fixed_consts, gain_final, out):
    with ExitStack() as ctx:
        def sb(name, shape, dt=F32):
            return ctx.enter_context(nc.sbuf_tensor(name, shape, dt))

        class Count:
            def __init__(self, name, per, first=0):
                self.sem, self.per, self.first = ctx.enter_context(nc.semaphore(name)), per, first

            def at(self, l, n):
                return l * self.per + (self.first + n)

        raw = sb("raw", [P, 4, CHUNK])
        head = sb("head", [P, 2, CHUNK], F32R)
        rest = sb("rest", [P, 2, CHUNK], F32R)
        xs = sb("xs", [P, T, D_MODEL])
        arena = sb("arena", [P, E_TILES * SEQ])
        gain = sb("gain", [P, GAINS])
        fixed = sb("fixed", [P, 2 * P])
        ident, iota = fixed[:, 0:P], fixed[:, P:2 * P]
        picked = sb("picked", [P, 3, T, PEER_HEADS * TOPK])
        ss = sb("ss", [P, 2, T])
        css = sb("css", [P, 2, 2, T])
        hss = sb("hss", [P, 2, 32])
        gs = sb("gs", [P, 2, T, PEER_HEADS])
        picked_t = sb("picked_t", [P, 4, SEQ])
        top_v = sb("top_v", [P, 2, TOPK])
        top_i = sb("top_i", [P, 2, TOPK], U32)
        top_f = sb("top_f", [P, 2, TOPK])
        left = sb("left", [P, 2, P])
        cand = sb("cand", [P, TOPK * TOPK])
        stage = sb("stage", [P, 2, P])
        best_v = sb("best_v", [P, TOPK])
        best_i = sb("best_i", [P, TOPK], U32)
        rank_i = sb("rank_i", [P, 2, TOPK], U32)
        rank_f = sb("rank_f", [P, 2, TOPK])
        match = sb("match", [P, 2, TOPK * TOPK])

        with nc.sbuf_tensor("act_head", [P, KT, SEQ], F32R) as act_head, \
                nc.sbuf_tensor("act_rest", [P, KT, SEQ], F32R) as act_rest:
            pass
        hot1 = sb("hot1", [P, 2, 4, P])
        hot2 = sb("hot2", [P, 2, 4, P])
        hot_gap = sb("hot_gap", [P, 4, 2, P])
        w_head = sb("w_head", [P, 2, SEQ], F32R)
        w_rest = sb("w_rest", [P, 2, SEQ], F32R)

        gain_row = hot1[:, :, :, :].rearrange("p b q n -> p (b q n)")
        assert 8 * P == D_MODEL

        used = [0]

        def carve(n):
            used[0] += n
            assert used[0] <= E_TILES * SEQ, used[0]
            return arena[:, used[0] - n:used[0]]

        xn = carve(T * D_MODEL).rearrange("p (t d) -> p t d", t=T)
        wt = [carve(HEADS * BLK).rearrange("p (h n) -> p h n", h=HEADS) for _ in range(4)]
        consts = carve(MIXER_CONST_COLS)
        at, c = 0, {}
        for name, n in MIXER_CONSTS:
            c[name] = consts[:, at:at + n]
            at += n
        smalls = carve(SMALL)
        w_uq = smalls[:, W_UQ:W_UKV].rearrange("p (r n) -> p r n", r=2)
        w_ukv = smalls[:, W_UKV:W_KEYS]
        keys_t = smalls[:, W_KEYS:SMALL].rearrange("p (m n) -> p m n", n=PEER_KEYS)
        rot = carve(T * 512).rearrange("p (t n) -> p t n", t=T)
        ret_t = carve(4 * SEQ).rearrange("p (j s) -> p j s", s=SEQ)
        rv = carve(T * GROUP_WIDTH).rearrange("p (t n) -> p t n", t=T)
        rg = carve(T * GROUP_WIDTH).rearrange("p (t n) -> p t n", t=T)
        fs_t = carve(8 * SEQ).rearrange("p (j s) -> p j s", s=SEQ)
        g2 = carve(T * D_MODEL).rearrange("p (t n) -> p t n", t=T)
        lf = carve(2 * T * HEADS).rearrange("p (a t h) -> p a t h", a=2, t=T)
        fc = carve(T * 16).rearrange("p (t n) -> p t n", t=T)
        fc_t = carve(2 * SEQ)
        fc_h = carve(HEADS * SEQ).rearrange("p (h s) -> p h s", h=HEADS)
        cn = carve(T * 384).rearrange("p (t n) -> p t n", t=T)
        c_t = carve(3 * SEQ).rearrange("p (j s) -> p j s", s=SEQ)
        mla_q = carve(T * HEADS * MLA_QK).rearrange("p (t h n) -> p t h n", t=T, h=HEADS)
        mla_k = carve(T * HEADS * MLA_QK).rearrange("p (t h n) -> p t h n", t=T, h=HEADS)
        mla_v = carve(T * GROUP_WIDTH).rearrange("p (t h n) -> p t h n", t=T, h=HEADS)
        krot = carve(T * MLA_ROPE).rearrange("p (t n) -> p t n", t=T)
        spare = carve(2 * 512)
        zs = carve(HEADS * BLK).rearrange("p (h n) -> p h n", h=HEADS)
        za = carve(HEADS * BLK).rearrange("p (h n) -> p h n", h=HEADS)
        soft = carve(HEADS * BLK).rearrange("p (h n) -> p h n", h=HEADS)
        mx = carve(4 * HEADS * T).rearrange("p (a t h) -> p a t h", a=4, t=T)
        dn = carve(4 * HEADS * T).rearrange("p (a t h) -> p a t h", a=4, t=T)
        mean = carve(2 * HEADS * T).rearrange("p (a n) -> p a n", a=2)
        scratch = wt[1].rearrange("p h n -> p (h n)")[:, 0:D_MODEL]
        qd_t = rot.rearrange("p t n -> p (t n)").rearrange("p (h s) -> p h s", h=HEADS)
        kd_t = ret_t
        soft_l = wt[3]
        ysq = fs_t.rearrange("p j s -> p (j s)").rearrange("p (g n) -> p g n", g=4)
        query_t = arena[:, T * D_MODEL:T * D_MODEL + 16 * SEQ].rearrange("p (m s) -> p m s", s=SEQ)
        assert 16 * SEQ <= 4 * HEADS * BLK

        acts = arena[:, 0:E_TILES * SEQ].rearrange("p (i s) -> p i s", s=SEQ)
        SCORE_SLOT = E_TILES - T * PEER_HEADS

        def scores(unit):
            return arena[:, bass.ds((unit + SCORE_SLOT) * SEQ, SEQ)]

        acc = [ctx.enter_context(nc.psum_tensor(f"acc{i}", [P, 512], F32)) for i in range(4)]
        work = [ctx.enter_context(nc.psum_tensor(f"work{i}", [P, 512], F32)) for i in range(4)]

        raw_in = [Count(f"raw_in{i}", 16 * PAIRS // 2) for i in range(2)]
        head_in = Count("head_in", CHUNKS)
        rest_in = Count("rest_in", CHUNKS, 2)
        head_free = Count("head_free", CHUNKS, 2)
        chunk_done = Count("chunk_done", CHUNKS, 2)
        TALLS = 4 + 8 + E_TILES // 2
        bank_free = Count("bank_free", TALLS, 2)
        fixed_in = Count("fixed_in", 0)
        x_in = [Count(f"x_in{t}", 0) for t in range(T)]
        gain_in = Count("gain_in", 16)
        small_in = Count("small_in", 32)
        x_ready = Count("x_ready", T, T)
        x_mid = Count("x_mid", T)
        std_ready = Count("std_ready", 2 * T)
        xn_ready = Count("xn_ready", 2 * T)
        heads_ready = Count("heads_ready", 2)
        turned = Count("turned", 12)
        act_head_in = Count("act_head_in", 12)
        act_rest_in = Count("act_rest_in", 12)
        rot_ready = Count("rot_ready", 1)
        rv_ready = Count("rv_ready", 1)
        ret_turned = Count("ret_turned", 1)
        ret_t_ready = Count("ret_t_ready", 1)
        g2_act = Count("g2_act", 1)
        g2_dve = Count("g2_dve", 1)
        cstd_ready = Count("cstd_ready", 1)
        cn_ready = Count("cn_ready", 1)
        c_turned = Count("c_turned", 1)
        c_t_ready = Count("c_t_ready", 1)
        mla_out = Count("mla_out", 2)
        krot_ready = Count("krot_ready", 1)
        mla_q_ready = Count("mla_q_ready", 1)
        mla_kv_ready = Count("mla_kv_ready", 1)
        mla_turned = Count("mla_turned", 1)
        mla_t_ready = Count("mla_t_ready", 1)
        ff_ready = Count("ff_ready", 1)
        ffl_ready = Count("ffl_ready", 1)
        ls_ready = Count("ls_ready", 1)
        fcum_out = Count("fcum_out", 1)
        fc_ready = Count("fc_ready", 1)
        fc_turned = Count("fc_turned", 1)
        fc_t_ready = Count("fc_t_ready", 1)
        sa_out = Count("sa_out", HEADS)
        wa_ready = Count("wa_ready", HEADS)
        sc_out = Count("sc_out", HEADS)
        zs_ready = Count("zs_ready", HEADS)
        lc_ready = Count("lc_ready", 1)
        sp_ready = Count("sp_ready", 1)
        cum_out = Count("cum_out", HEADS)
        logw_ready = Count("logw_ready", HEADS)
        ew_ready = Count("ew_ready", 1)
        wc_ready = Count("wc_ready", 1)
        soft_out = Count("soft_out", 2 * HEADS)
        soft_max = Count("soft_max", 2 * HEADS)
        soft_exp = Count("soft_exp", 2 * HEADS)
        soft_turned = Count("soft_turned", 2 * HEADS)
        soft_t_ready = Count("soft_t_ready", 2 * HEADS)
        o_out = Count("o_out", 4)
        o_read = Count("o_read", 1)
        hss_ready = Count("hss_ready", 2)
        hstd_ready = Count("hstd_ready", 2)
        score_out = Count("score_out", 8)
        score_in = Count("score_in", 8)
        UNITS = T * PEER_HEADS
        TURN_AT = E_TILES - 16
        unit_done = Count("unit_done", UNITS, 1)
        gate_exp = Count("gate_exp", 1)
        gates_done = Count("gates_done", 1)
        picked_turned = Count("picked_turned", 1)
        picked_t_in = Count("picked_t_in", 1)
        staged = Count("staged", UNITS)
        GROUPS = SEQ // 4
        hot_ready = Count("hot_ready", GROUPS)
        hot_act = Count("hot_act", GROUPS, 2)
        gap_ready = Count("gap_ready", GROUPS)
        gate_out = Count("gate_out", GROUPS)
        gate_used = Count("gate_used", GROUPS, 2)
        w_head_in = Count("w_head_in", E_TILES)
        w_rest_in = Count("w_rest_in", E_TILES, 2)
        final_ready = Count("final_ready", 0)
        out_done = [Count(f"out_done{t}", 0) for t in range(T)]
        act_step = Count("act_step", ACT_STEPS)
        dve_step = Count("dve_step", DVE_STEPS)
        route_step = Count("route_step", UNITS * ROUTE_STEPS)

        class Steps:

            def __init__(self, eng, count, l):
                self.eng, self.count, self.l, self.n = eng, count, l, 0

            def __call__(self, ins):
                ins.then_inc(self.count.sem, 1)
                self.n += 1
                self.eng.wait_ge(self.count.sem, self.count.at(self.l, self.n))

        passed = ctx.enter_context(nc.semaphore("passed"))

        def after_register_wait(eng):
            eng.sem_inc(passed, 1)

        block = ctx.enter_context(nc.Block())

        @block.sync
        def _(sp):
            def load(pair, slot):
                sp.dma_start(raw[:, 2 * slot:2 * slot + 2, :], stream[pair]).then_inc(raw_in[slot].sem, 16)

            load(0, 0)
            load(1, 1)
            with sp.Fori(1, DEPTH * PAIRS // 2) as k:
                for slot in range(2):
                    sp.wait_ge(rest_in.sem, 4 * k + (2 * slot + rest_in.first - 2))
                    load(2 * k + slot, slot)
            for slot in range(2):
                sp.wait_ge(raw_in[slot].sem, 16 * DEPTH * PAIRS // 2)

        @block.gpsimd
        def _(pool):
            pool.dma_start(fixed[:], fixed_consts).then_inc(fixed_in.sem, 16)
            pool.dma_start(gain[:], gains[0]).then_inc(gain_in.sem, 16)
            pool.dma_start(smalls, small[0]).then_inc(small_in.sem, 16)
            pool.dma_start(consts, mixer_consts).then_inc(small_in.sem, 16)
            with pool.Fori(1, DEPTH) as l:
                pool.wait_ge(act_rest_in.sem, act_rest_in.at(l, 0))
                pool.dma_start(gain[:], gains[l]).then_inc(gain_in.sem, 16)
                pool.wait_ge(x_ready.sem, x_ready.at(l, 0))
                pool.dma_start(smalls, small[l]).then_inc(small_in.sem, 16)
                pool.dma_start(consts, mixer_consts).then_inc(small_in.sem, 16)
            pool.wait_ge(gate_used.sem, gate_used.at(DEPTH - 1, GROUPS))
            pool.dma_start(gain_row, gain_final.to_broadcast([P, D_MODEL])).then_inc(fixed_in.sem, 16)

        @block.tensor
        def _(pe):
            mm = nc.tensor.matmul
            pe.sem_inc(head_free.sem, 2)
            pe.sem_inc(chunk_done.sem, 2)
            pe.wait_ge(fixed_in.sem, 16)

            def tall_block(l, c0, pair0, use=None):
                for j in range(4):
                    s, bank = j % 2, work[j // 2]
                    o = bank[:, (j % 2) * SEQ:(j % 2 + 1) * SEQ]
                    if j % 2 == 0:
                        pe.wait_ge(bank_free.sem, bank_free.at(l, pair0 + (j // 2 - 1)))
                    pe.wait_ge(head_in.sem, head_in.at(l, c0 + (j + 1)))
                    for kt in range(KT):
                        if use is not None and j == 0 and kt % 2 == 0:
                            pe.wait_ge(act_rest_in.sem, act_rest_in.at(l, 4 * use + kt // 2 + 1))
                        w = head[:, s, kt * P:(kt + 1) * P]
                        mm(o, w, act_head[:, kt, :], start=(kt == 0), stop=False)
                        ins = mm(o, w, act_rest[:, kt, :], start=False, stop=False)
                    ins.then_inc(head_free.sem, 1)
                    pe.wait_ge(rest_in.sem, rest_in.at(l, c0 + (j + 1)))
                    for kt in range(KT):
                        ins = mm(o, rest[:, s, kt * P:(kt + 1) * P], act_head[:, kt, :],
                                 start=False, stop=(kt == KT - 1))
                    ins.then_inc(chunk_done.sem, 1)

            def gates_of(l, n, b):
                pe.wait_ge(hot_ready.sem, hot_ready.at(l, n + 1))
                pe.wait_ge(hot_act.sem, hot_act.at(l, n + 1))
                pe.wait_ge(gate_used.sem, gate_used.at(l, n - 1))
                for q in range(4):
                    ins = mm(work[2 + b][:, q * P:(q + 1) * P], hot2[:, b, q, :], hot1[:, b, q, :],
                             start=True, stop=True)
                ins.then_inc(gate_out.sem, 1)

            def wide_chunk(l, cj, s, a_head, a_rest, first, last, between=None):
                pe.wait_ge(head_in.sem, head_in.at(l, cj + 1))
                for t in range(T):
                    for n in range(2):
                        mm(acc[2 * t + n][:], a_head(t), head[:, s, n * 512:(n + 1) * 512], start=first, stop=False)
                for t in range(T):
                    for n in range(2):
                        ins = mm(acc[2 * t + n][:], a_rest(t), head[:, s, n * 512:(n + 1) * 512], start=False, stop=False)
                ins.then_inc(head_free.sem, 1)
                if between:
                    between()
                pe.wait_ge(rest_in.sem, rest_in.at(l, cj + 1))
                for t in range(T):
                    for n in range(2):
                        ins = mm(acc[2 * t + n][:], a_head(t), rest[:, s, n * 512:(n + 1) * 512], start=False, stop=last)
                ins.then_inc(chunk_done.sem, 1)

            def wide(l, c0, use, between={}):
                for kt in range(KT):
                    if kt % 2 == 0:
                        pe.wait_ge(act_rest_in.sem, act_rest_in.at(l, 4 * use + kt // 2 + 1))
                    wide_chunk(l, c0 + kt, kt % 2, lambda t: act_head[:, kt, t * P:(t + 1) * P],
                               lambda t: act_rest[:, kt, t * P:(t + 1) * P], kt == 0, kt == KT - 1, between.get(kt))

            def keep_clock(count):
                for _ in range(count):
                    mm(work[3][:, 0:P], ident, ident, start=True, stop=True)

            def turn(l, use):
                for t in range(T):
                    pe.wait_ge(xn_ready.sem, xn_ready.at(l, T * (use // 2) + t + 1))
                    for kt in range(KT):
                        ins = turn_tile(t, kt)
                        if t == T - 1 and kt % 2:
                            ins.then_inc(turned.sem, 1)

            def turn_tile(t, kt):
                return pe.transpose(work[kt // 2][:, (kt % 2) * SEQ + t * P:(kt % 2) * SEQ + (t + 1) * P],
                                    xn[:, t, kt * P:(kt + 1) * P], ident)

            def keys_by_queries(o, k_t, q_t):
                mm(o[:, 0:SEQ], k_t[:, 0:P], q_t, start=True, stop=True)
                return mm(o[:, SEQ:BLK], k_t[:, P:SEQ], q_t[:, P:SEQ], start=True, stop=True)

            def weighted(g, w, v):
                for h in range(HEADS):
                    o = acc[g][:, h * HEAD_DIM:(h + 1) * HEAD_DIM]
                    mm(o, w[:, h, 0:P], v(0, h), start=True, stop=True)
                    o = acc[g][:, GROUP_WIDTH + h * HEAD_DIM:GROUP_WIDTH + (h + 1) * HEAD_DIM]
                    mm(o, w[:, h, P:SEQ], v(0, h), start=True, stop=False)
                    ins = mm(o, w[:, h, SEQ:BLK], v(1, h), start=False, stop=True)
                ins.then_inc(o_out.sem, 1)

            def rows(h):
                return slice((h % 2) * HEAD_DIM, (h % 2 + 1) * HEAD_DIM)

            with pe.Fori(0, DEPTH) as l:
                keep_clock(16)
                turn(l, 0)
                wide(l, C_WIDE1, 0)
                tall_block(l, C_TALL, 0)
                tall_block(l, C_TALL + 4, 2)
                pe.wait_ge(rot_ready.sem, rot_ready.at(l, 1))
                pe.wait_ge(rv_ready.sem, rv_ready.at(l, 1))

                def turn_rotated():
                    pe.wait_ge(zs_ready.sem, zs_ready.at(l, 2))
                    for j in range(4):
                        for t in range(T):
                            ins = pe.transpose(work[j // 2][:, (j % 2) * SEQ + t * P:(j % 2) * SEQ + (t + 1) * P],
                                               rot[:, t, j * P:(j + 1) * P], ident)
                    ins.then_inc(ret_turned.sem, 1)

                def retention_logits():
                    pe.wait_ge(ret_t_ready.sem, ret_t_ready.at(l, 1))
                    pe.wait_ge(zs_ready.sem, zs_ready.at(l, HEADS))
                    for h in range(HEADS):
                        keys_by_queries(work[h], ret_t[rows(h), 2 + h // 2, :], ret_t[rows(h), h // 2, :])\
                            .then_inc(sa_out.sem, 1)

                def stick_logits():
                    pe.wait_ge(bank_free.sem, bank_free.at(l, 4))
                    for h in range(HEADS):
                        keys_by_queries(work[h], fs_t[rows(h), 6 + h // 2, :], fs_t[rows(h), 4 + h // 2, :])\
                            .then_inc(sc_out.sem, 1)

                wide(l, C_WIDE2, 0, {0: stick_logits, 1: turn_rotated, 3: retention_logits})

                pe.wait_ge(sp_ready.sem, sp_ready.at(l, 1))
                for h in range(HEADS):
                    pe.wait_ge(wa_ready.sem, wa_ready.at(l, h + 1))
                    mm(work[h][:, 0:BLK], c["tri_ge"], za[:, h, :], start=True, stop=False)
                    mm(work[h][:, P:SEQ], c["ones"], za[:, h, SEQ:BLK], start=False, stop=True).then_inc(cum_out.sem, 1)

                pe.wait_ge(cn_ready.sem, cn_ready.at(l, 1))
                for j in range(3):
                    for t in range(T):
                        ins = pe.transpose(acc[2 + j // 2][:, (j % 2) * SEQ + t * P:(j % 2) * SEQ + (t + 1) * P],
                                           cn[:, t, j * P:(j + 1) * P], ident)
                ins.then_inc(c_turned.sem, 1)

                pe.wait_ge(ls_ready.sem, ls_ready.at(l, 1))
                pe.wait_ge(g2_act.sem, g2_act.at(l, 1))
                pe.wait_ge(g2_dve.sem, g2_dve.at(l, 1))
                mm(acc[0][:, 0:HEADS], c["tri_le"], lf[:, 0, 0, :], start=True, stop=True)
                mm(acc[0][:, HEADS:2 * HEADS], c["tri_le"], lf[:, 0, 1, :], start=True, stop=False)
                mm(acc[0][:, HEADS:2 * HEADS], c["ones"], lf[:, 0, 0, :], start=False, stop=True).then_inc(fcum_out.sem, 1)

                pe.wait_ge(fc_ready.sem, fc_ready.at(l, 1))
                for a in range(2):
                    for t in range(T):
                        ins = pe.transpose(acc[1][0:8, a * SEQ + t * P:a * SEQ + (t + 1) * P],
                                           fc[:, t, 8 * a:8 * a + 8], ident)
                ins.then_inc(fc_turned.sem, 1)

                pe.wait_ge(c_t_ready.sem, c_t_ready.at(l, 1))
                for t in range(T):
                    ins = mm(acc[2 + t][:], c_t[:, 2, t * P:(t + 1) * P], w_ukv, start=True, stop=True)
                ins.then_inc(mla_out.sem, 1)
                pe.wait_ge(fc_t_ready.sem, fc_t_ready.at(l, 1))
                for t in range(T):
                    mm(acc[t][:, 0:384], c_t[:, 0, t * P:(t + 1) * P], w_uq[:, 0, :], start=True, stop=False)
                    ins = mm(acc[t][:, 0:384], c_t[:, 1, t * P:(t + 1) * P], w_uq[:, 1, :], start=False, stop=True)
                ins.then_inc(mla_out.sem, 1)

                for h in range(HEADS):
                    q_t, k_t, o = fs_t[rows(h), h // 2, :], fs_t[rows(h), 2 + h // 2, :], work[h]
                    pe.wait_ge(logw_ready.sem, logw_ready.at(l, h + 1))
                    mm(o[:, 0:P], q_t[:, 0:P], k_t[:, 0:P], start=True, stop=False)
                    mm(o[:, P:BLK], q_t[:, P:SEQ], k_t, start=False, stop=False)
                for h in range(HEADS):
                    mm(work[h][:, 0:P], fc_h[0:8, h, 0:P], fc_t[0:8, SEQ:SEQ + P], start=False, stop=False)
                    mm(work[h][:, P:BLK], fc_h[0:8, h, P:SEQ], fc_t[0:8, SEQ:2 * SEQ], start=False, stop=True)\
                        .then_inc(soft_out.sem, 1)

                pe.wait_ge(mla_q_ready.sem, mla_q_ready.at(l, 1))
                pe.wait_ge(mla_kv_ready.sem, mla_kv_ready.at(l, 1))
                for a, src in enumerate((mla_q, mla_k)):
                    for h in range(HEADS):
                        for t in range(T):
                            ins = pe.transpose(
                                acc[2 * a + h // 2][0:MLA_QK, (h % 2) * SEQ + t * P:(h % 2) * SEQ + (t + 1) * P],
                                src[:, t, h, :], ident)
                ins.then_inc(mla_turned.sem, 1)

                def turn_weights(base, weights):
                    for h in range(HEADS):
                        pe.wait_ge(soft_exp.sem, soft_exp.at(l, base + h + 1))
                        for j in range(3):
                            ins = pe.transpose(work[h][:, j * P:(j + 1) * P], weights[:, h, j * P:(j + 1) * P], ident)
                        ins.then_inc(soft_turned.sem, 1)

                turn_weights(0, soft)
                pe.wait_ge(mla_t_ready.sem, mla_t_ready.at(l, 1))
                for h in range(HEADS):
                    mm(acc[h][:, 0:P], qd_t[0:MLA_QK, h, 0:P], kd_t[0:MLA_QK, h, 0:P], start=True, stop=True)
                    mm(acc[h][:, P:BLK], qd_t[0:MLA_QK, h, P:SEQ], kd_t[0:MLA_QK, h, :], start=True, stop=True)\
                        .then_inc(soft_out.sem, 1)
                pe.wait_ge(soft_max.sem, soft_max.at(l, HEADS + 1))
                weighted(0, wt[0], lambda t, h: rv[:, t, h * HEAD_DIM:(h + 1) * HEAD_DIM])
                pe.wait_ge(wc_ready.sem, wc_ready.at(l, 1))
                pe.wait_ge(soft_max.sem, soft_max.at(l, HEADS + 3))
                weighted(2, wt[2], lambda t, h: g2[:, t, SV + h * HEAD_DIM:SV + (h + 1) * HEAD_DIM])
                pe.wait_ge(soft_t_ready.sem, soft_t_ready.at(l, HEADS))
                turn_weights(HEADS, soft_l)
                weighted(1, wt[1], lambda t, h: g2[:, t, FV + h * HEAD_DIM:FV + (h + 1) * HEAD_DIM])
                pe.wait_ge(soft_max.sem, soft_max.at(l, 2 * HEADS))
                pe.wait_ge(soft_t_ready.sem, soft_t_ready.at(l, 2 * HEADS))
                weighted(3, wt[3], lambda t, h: mla_v[:, t, h, :])

                def turn_heads(part, tiles):
                    pe.wait_ge(heads_ready.sem, heads_ready.at(l, part))
                    for kt in tiles:
                        for t in range(T):
                            ins = turn_tile(t, kt)
                        if kt % 2:
                            ins.then_inc(turned.sem, 1)

                keep_clock(12)
                turn_heads(1, range(0, 6))
                pe.wait_ge(o_read.sem, o_read.at(l, 1))
                wide(l, C_OUT, 1, {2: lambda: turn_heads(2, range(6, KT))})

                keep_clock(16)
                turn(l, 2)
                after_register_wait(pe)
                with pe.Fori(0, 4) as k:
                    tall_block(l, C_QUERY + k * 4, 4 + k * 2, 2)
                pe.wait_ge(bank_free.sem, bank_free.at(l, 4 + 8))
                for t in range(T):
                    for m4 in range(4):
                        if t:
                            pe.wait_ge(score_in.sem, score_in.at(l, m4 + 1))
                        for m in range(4):
                            ins = mm(work[m4][:, m * P:(m + 1) * P], query_t[:, 4 * m4 + m, t * P:(t + 1) * P],
                                     keys_t[:, 4 * m4 + m, :], start=True, stop=True)
                        ins.then_inc(score_out.sem, 1)
                pe.wait_ge(score_in.sem, score_in.at(l, 8))
                after_register_wait(pe)

                with pe.Fori(0, TURN_AT // 4) as u:
                    tall_block(l, C_U + u * 4, 12 + u * 2)

                pe.wait_ge(gates_done.sem, gates_done.at(l, 1))
                for a in range(3):
                    for t in range(T):
                        ins = pe.transpose(work[2 + a // 2][:, (a % 2) * SEQ + t * P:(a % 2) * SEQ + (t + 1) * P],
                                           picked[:, a, t, :], ident)
                ins.then_inc(picked_turned.sem, 1)

                after_register_wait(pe)
                with pe.Fori(TURN_AT // 4, E_TILES // 4) as u:
                    tall_block(l, C_U + u * 4, 12 + u * 2)

                with pe.Fori(0, GROUPS // 4) as u:
                    for j in range(4):
                        gates_of(l, 4 * u + j, j % 2)

                def v_block(i0, first, last):
                    for j in range(4):
                        pe.wait_ge(w_head_in.sem, w_head_in.at(l, i0 + (j + 1)))
                        pe.wait_ge(w_rest_in.sem, w_rest_in.at(l, i0 + (j + 1)))
                        wide_chunk(l, C_V + i0 + j, j % 2, lambda t: w_head[:, j % 2, t * P:(t + 1) * P],
                                   lambda t: w_rest[:, j % 2, t * P:(t + 1) * P], first and j == 0, last and j == 3)

                v_block(0, True, False)
                with pe.Fori(1, E_TILES // 4 - 1) as v:
                    v_block(4 * v, False, False)
                v_block(E_TILES - 4, False, True)

        @block.scalar
        def _(act):
            for t in range(T):
                act.dma_start(xs[:, t, :], x[:, t, :]).then_inc(x_in[t].sem, 16)
            act.sem_inc(bank_free.sem, 2)
            act.sem_inc(hot_act.sem, 2)

            def split_head(l, cj, slot, raw_slot):
                act.wait_ge(raw_in[raw_slot // 2].sem, raw_in[raw_slot // 2].at(l, 4 * (cj + (4 - raw_slot))))
                act.wait_ge(head_free.sem, head_free.at(l, cj - 1))
                act.wait_ge(rest_in.sem, rest_in.at(l, cj - 1))
                nc.scalar.copy(head[:, slot, :], raw[:, raw_slot, :]).then_inc(head_in.sem, 1)

            def ahead(l, c0, n, j0=0):
                for j in range(j0, j0 + n):
                    split_head(l, c0 + (j + 2), j % 2, (j + 2) % 4)

            def std(l, use, x_in_place, step):
                nc.scalar.preload_act_table(ACT.Sqrt)
                for t in range(T):
                    act.wait_ge(x_in_place.sem, x_in_place.at(l, t + 1 - x_in_place.first))
                    step(nc.scalar.activation(scratch, xs[:, t, :], ACT.Square, accum_out=ss[:, 0, t:t + 1]))
                    nc.scalar.activation(ss[:, 1, t:t + 1], ss[:, 0, t:t + 1], ACT.Sqrt, scale=1.0 / D_MODEL, bias=eps)\
                        .then_inc(std_ready.sem, 1)

            def act_heads(l, use, g0, banks=range(4)):
                for b in banks:
                    act.wait_ge(turned.sem, turned.at(l, 4 * use + b + 1))
                    for kt in (2 * b, 2 * b + 1):
                        ins = nc.scalar.activation(act_head[:, kt, :], work[b][:, (kt % 2) * SEQ:(kt % 2 + 1) * SEQ],
                                                   ACT.Copy, scale=gain[:, g0 + kt:g0 + kt + 1])
                    ins.then_inc(act_head_in.sem, 1)

            def weights_exp(l, base, n, scale, weights):
                for h in range(HEADS):
                    act.wait_ge(soft_max.sem, soft_max.at(l, base + h + 1))
                    nc.scalar.activation(weights[:, h, 0:P], weights[:, h, 0:P], ACT.Exp, scale=scale,
                                         bias=mx[:, 2 * n + 1, 0, h:h + 1], accum_out=dn[:, 2 * n, 0, h:h + 1])
                    nc.scalar.activation(weights[:, h, P:BLK], weights[:, h, P:BLK], ACT.Exp, scale=scale,
                                         bias=mx[:, 2 * n + 1, 1, h:h + 1], accum_out=dn[:, 2 * n, 1, h:h + 1])\
                        .then_inc(soft_exp.sem, 1)

            def weights_t(l, base, dst):
                for h in range(HEADS):
                    act.wait_ge(soft_turned.sem, soft_turned.at(l, base + h + 1))
                    nc.scalar.copy(dst[:, h, :], work[h][:, 0:BLK]).then_inc(soft_t_ready.sem, 1)

            eps = EPS
            with act.Fori(0, DEPTH) as l:
                step = Steps(act, act_step, l)
                std(l, 0, x_ready, step)
                for j in range(2):
                    split_head(l, j, j, j)
                act.wait_ge(gain_in.sem, gain_in.at(l, 16))
                act_heads(l, 0, G_MIX)
                ahead(l, C_WIDE1, 8)
                act.wait_ge(small_in.sem, small_in.at(l, 32))
                act.wait_ge(chunk_done.sem, chunk_done.at(l, C_TALL))
                for t in range(T):
                    nc.scalar.copy(rv[:, t, :], acc[2 * t + 1][:, 0:GROUP_WIDTH])
                for t in range(T):
                    ins = nc.scalar.activation(rg[:, t, :], acc[2 * t + 1][:, GROUP_WIDTH:512], ACT.Silu)
                ins.then_inc(rv_ready.sem, 1)
                for b in range(4):
                    ahead(l, C_TALL, 2, 2 * b)
                    act.wait_ge(chunk_done.sem, chunk_done.at(l, C_TALL + 2 * b + 2))
                    nc.scalar.copy(fs_t[:, 2 * b:2 * b + 2, :], work[b % 2][:].rearrange("p (j s) -> p j s", s=SEQ))\
                        .then_inc(bank_free.sem, 1)
                ahead(l, C_WIDE2, 1)
                for h in range(HEADS):
                    act.wait_ge(sc_out.sem, sc_out.at(l, h + 1))
                    nc.scalar.activation(zs[:, h, :], work[h][:, 0:BLK], ACT.Copy, scale=SCALE).then_inc(zs_ready.sem, 1)
                ahead(l, C_WIDE2, 1, 1)
                act.wait_ge(zs_ready.sem, zs_ready.at(l, HEADS))
                step(nc.scalar.activation(za[:, :, :], zs[:, :, :], ACT.Abs))
                act.wait_ge(ret_turned.sem, ret_turned.at(l, 1))
                for b in range(2):
                    ins = nc.scalar.copy(ret_t[:, 2 * b:2 * b + 2, :], work[b][:].rearrange("p (j s) -> p j s", s=SEQ))
                ins.then_inc(ret_t_ready.sem, 1)
                ahead(l, C_WIDE2, 1, 2)
                step(nc.scalar.activation(za[:, :, :], za[:, :, :], ACT.Exp, scale=-1.0))
                ahead(l, C_WIDE2, 1, 3)
                nc.scalar.activation(za[:, :, :], za[:, :, :], ACT.Ln, bias=1.0).then_inc(lc_ready.sem, 1)
                ahead(l, C_WIDE2, 4, 4)
                nc.scalar.preload_act_table(ACT.Sqrt)

                act.wait_ge(chunk_done.sem, chunk_done.at(l, C_OUT))
                for n in range(2):
                    ins = nc.scalar.copy(g2[:, 0, n * 512:(n + 1) * 512], acc[n][:])
                ins.then_inc(g2_act.sem, 1)
                act.wait_ge(g2_dve.sem, g2_dve.at(l, 1))
                act.wait_ge(g2_act.sem, g2_act.at(l, 1))
                for a, (c0, n) in enumerate(((CQ, MLA_Q_RANK), (CKV, MLA_KV_RANK))):
                    for t in range(T):
                        step(nc.scalar.activation(scratch[:, 0:n], g2[:, t, c0:c0 + n], ACT.Square,
                                                  accum_out=css[:, 0, a, t:t + 1]))
                nc.scalar.activation(css[:, 1, 0, :], css[:, 0, 0, :], ACT.Sqrt, scale=1.0 / MLA_Q_RANK, bias=eps)
                nc.scalar.activation(css[:, 1, 1, :], css[:, 0, 1, :], ACT.Sqrt, scale=1.0 / MLA_KV_RANK, bias=eps)\
                    .then_inc(cstd_ready.sem, 1)
                act.wait_ge(ff_ready.sem, ff_ready.at(l, 1))
                step(nc.scalar.activation(lf[:, 1, :, :], lf[:, 0, :, :], ACT.Abs))
                step(nc.scalar.activation(lf[:, 1, :, :], lf[:, 1, :, :], ACT.Exp, scale=-1.0))
                nc.scalar.activation(lf[:, 1, :, :], lf[:, 1, :, :], ACT.Ln, bias=1.0).then_inc(ffl_ready.sem, 1)
                act.wait_ge(c_turned.sem, c_turned.at(l, 1))
                for j in range(3):
                    ins = nc.scalar.activation(c_t[:, j, :], acc[2 + j // 2][:, (j % 2) * SEQ:(j % 2 + 1) * SEQ], ACT.Copy,
                                               scale=gain[:, G_CQ + j:G_CQ + j + 1])
                ins.then_inc(c_t_ready.sem, 1)
                act.wait_ge(logw_ready.sem, logw_ready.at(l, HEADS))
                nc.scalar.activation(za[:, :, :], zs[:, :, :], ACT.Exp).then_inc(ew_ready.sem, 1)
                act.wait_ge(mla_out.sem, mla_out.at(l, 1))
                act.wait_ge(krot_ready.sem, krot_ready.at(l, 1))
                for t in range(T):
                    kv = acc[2 + t][:].rearrange("p (h n) -> p h n", h=HEADS)
                    nc.scalar.copy(mla_k[:, t, :, 0:HEAD_DIM], kv[:, :, 0:HEAD_DIM])
                    nc.scalar.copy(mla_v[:, t, :, :], kv[:, :, HEAD_DIM:])
                    ins = nc.scalar.copy(mla_k[:, t, :, HEAD_DIM:MLA_QK],
                                         krot[:, t:t + 1, :].to_broadcast([P, HEADS, MLA_ROPE]))
                ins.then_inc(mla_kv_ready.sem, 1)
                weights_exp(l, 0, 0, SCALE, soft)
                act.wait_ge(mla_turned.sem, mla_turned.at(l, 1))
                for a, dst in enumerate((qd_t, kd_t)):
                    for b in range(2):
                        ins = nc.scalar.copy(dst[0:MLA_QK, 2 * b:2 * b + 2, :],
                                             acc[2 * a + b][0:MLA_QK, :].rearrange("p (h s) -> p h s", s=SEQ))
                ins.then_inc(mla_t_ready.sem, 1)
                weights_t(l, 0, wt[1])
                weights_exp(l, HEADS, 1, SCALE_MLA, soft_l)
                weights_t(l, HEADS, wt[3])
                def heads_std(part, n):
                    act.wait_ge(hss_ready.sem, hss_ready.at(l, part))
                    nc.scalar.activation(hss[:, 1, n], hss[:, 0, n], ACT.Sqrt, scale=1.0 / HEAD_DIM, bias=eps)\
                        .then_inc(hstd_ready.sem, 1)

                nc.scalar.preload_act_table(ACT.Sqrt)
                heads_std(1, slice(0, 24))
                act_heads(l, 1, G_HEAD, range(3))
                heads_std(2, slice(24, 32))
                ahead(l, C_OUT, 2)
                act_heads(l, 1, G_HEAD, range(3, 4))
                ahead(l, C_OUT, 6, 2)

                std(l, 1, x_mid, step)
                act_heads(l, 2, G_FFN)
                with act.Fori(0, 4) as k:
                    for b in range(2):
                        ahead(l, C_QUERY + k * 4, 2, 2 * b)
                        act.wait_ge(chunk_done.sem, chunk_done.at(l, C_QUERY + k * 4 + (2 * b + 2)))
                        nc.scalar.copy(query_t[:, bass.ds(k * 4 + 2 * b, 2), :],
                                       work[b][:].rearrange("p (j s) -> p j s", s=SEQ)).then_inc(bank_free.sem, 1)
                for t in range(T):
                    for m4 in range(4):
                        act.wait_ge(score_out.sem, score_out.at(l, 4 * t + m4 + 1))
                        at = (SCORE_SLOT + t * PEER_HEADS + 2 * m4) * SEQ
                        nc.scalar.copy(arena[:, at:at + 512], work[m4][:]).then_inc(score_in.sem, 1)
                nc.scalar.preload_act_table(ACT.Gelu)

                def activations(i0, b):
                    ahead(l, C_U + i0, 2, 2 * b)
                    act.wait_ge(chunk_done.sem, chunk_done.at(l, C_U + i0 + (2 * b + 2)))
                    nc.scalar.activation(acts[:, bass.ds(i0 + 2 * b, 2), :],
                                         work[b % 2][:].rearrange("p (j s) -> p j s", s=SEQ), ACT.Gelu)\
                        .then_inc(bank_free.sem, 1)

                with act.Fori(0, UNITS // 2) as w:
                    for b in range(STRIDE):
                        if b % (STRIDE // 2) == 0:
                            u = 2 * w + b // (STRIDE // 2)
                            act.wait_ge(unit_done.sem, unit_done.at(l, u))
                            nc.scalar.copy(stage[:, :, :], scores(u).rearrange("p (a n) -> p a n", a=2))\
                                .then_inc(staged.sem, 1)
                        activations(2 * STRIDE * w, b)
                for b in range(2):
                    activations(UNITS * STRIDE, b)
                act.wait_ge(unit_done.sem, unit_done.at(l, UNITS))
                nc.scalar.activation(picked[:, 2, :, :], picked[:, 2, :, :], ACT.Exp).then_inc(gate_exp.sem, 1)
                nc.scalar.preload_act_table(ACT.Gelu)
                with act.Fori(UNITS * STRIDE // 4 + 1, E_TILES // 4) as u:
                    for b in range(2):
                        activations(4 * u, b)

                def gaps(g, slot):
                    act.wait_ge(hot_act.sem, hot_act.at(l, g - 2))
                    for q in range(2):
                        ins = nc.scalar.activation(hot_gap[:, slot, q, :], iota, ACT.Square, scale=-1.0,
                                                   bias=picked_t[:, 1, bass.ds(4 * g + (2 + q), 1)])
                    ins.then_inc(gap_ready.sem, 1)

                def hot_second(g, slot):
                    act.wait_ge(gap_ready.sem, gap_ready.at(l, g + 1))
                    act.wait_ge(gate_used.sem, gate_used.at(l, g - 1))
                    for q in range(2):
                        tok = bass.ds(4 * g + (2 + q), 1)
                        ins = nc.scalar.activation(hot2[:, slot % 2, 2 + q, :], hot_gap[:, slot, q, :], ACT.Relu,
                                                   scale=picked_t[:, 3, tok], bias=picked_t[:, 2, tok])
                    ins.then_inc(hot_act.sem, 1)

                act.wait_ge(picked_t_in.sem, picked_t_in.at(l, 1))
                gaps(0, 0)
                with act.Fori(0, GROUPS // 4 - 1) as u:
                    for j in range(4):
                        gaps(4 * u + (j + 1), (j + 1) % 4)
                        hot_second(4 * u + j, j)
                for j in range(4):
                    if j < 3:
                        gaps(GROUPS - 3 + j, j + 1)
                    hot_second(GROUPS - 4 + j, j)

                def weight_head(i, slot):
                    act.wait_ge(chunk_done.sem, chunk_done.at(l, C_V + i - 1))
                    act.wait_ge(w_rest_in.sem, w_rest_in.at(l, i - 1))
                    nc.scalar.copy(w_head[:, slot, :], acts[:, i, :]).then_inc(w_head_in.sem, 1)

                def v_block(i0, last):
                    for j in range(4):
                        if not (last and j == 3):
                            weight_head(i0 + (j + 1), (j + 1) % 2)
                        if not (last and j >= 2):
                            split_head(l, C_V + i0 + (j + 2), j % 2, (j + 2) % 4)

                act.wait_ge(gate_used.sem, gate_used.at(l, GROUPS))
                weight_head(0, 0)
                with act.Fori(0, E_TILES // 4 - 1) as v:
                    v_block(4 * v, False)
                v_block(E_TILES - 4, True)
                assert step.n == ACT_STEPS, step.n
            nc.scalar.preload_act_table(ACT.Sqrt)
            for t in range(T):
                act.wait_ge(x_ready.sem, x_ready.at(DEPTH, t + 1 - T))
                nc.scalar.activation(arena[:, (2 + t) * D_MODEL:(3 + t) * D_MODEL], xs[:, t, :], ACT.Square,
                                     accum_out=ss[:, 0, t:t + 1]).then_inc(act_step.sem, 1)
                act.wait_ge(act_step.sem, act_step.at(DEPTH, t + 1))
                nc.scalar.activation(ss[:, 1, t:t + 1], ss[:, 0, t:t + 1], ACT.Sqrt, scale=1.0 / D_MODEL, bias=eps)\
                    .then_inc(std_ready.sem, 1)
            for t in range(T):
                act.wait_ge(final_ready.sem, final_ready.at(0, t + 1))
                act.dma_start(out[:, t, :], xs[:, t, :]).then_inc(out_done[t].sem, 16)
            for t in range(T):
                act.wait_ge(out_done[t].sem, 16)

        @block.vector
        def _(dve):
            tt, ts = nc.vector.tensor_tensor, nc.vector.tensor_scalar
            dve.sem_inc(rest_in.sem, 2)
            dve.sem_inc(unit_done.sem, 1)
            dve.sem_inc(gate_used.sem, 2)
            dve.sem_inc(w_rest_in.sem, 2)
            for t in range(T):
                dve.wait_ge(x_in[t].sem, 16)
                dve.sem_inc(x_ready.sem, 1)

            def split_rest(l, cj, slot, raw_slot):
                dve.wait_ge(head_in.sem, head_in.at(l, cj + 1))
                dve.wait_ge(chunk_done.sem, chunk_done.at(l, cj - 1))
                tt(rest[:, slot, :], raw[:, raw_slot, :], head[:, slot, :].bitcast(F32), ALU.subtract)\
                    .then_inc(rest_in.sem, 1)

            def ahead(l, c0, n, j0=0):
                for j in range(j0, j0 + n):
                    split_rest(l, c0 + (j + 1), (j + 1) % 2, (j + 1) % 4)

            def norm_tokens(l, use, step):
                for t in range(T):
                    dve.wait_ge(std_ready.sem, std_ready.at(l, T * use + t + 1))
                    step(nc.vector.reciprocal(ss[:, 1, t:t + 1], ss[:, 1, t:t + 1]))
                    ts(xn[:, t, :], xs[:, t, :], ss[:, 1, t:t + 1], None, ALU.mult).then_inc(xn_ready.sem, 1)

            def act_rests(l, use, g0, banks=range(4)):
                for b in banks:
                    dve.wait_ge(act_head_in.sem, act_head_in.at(l, 4 * use + b + 1))
                    for kt in (2 * b, 2 * b + 1):
                        ins = nc.vector.scalar_tensor_tensor(
                            out=act_rest[:, kt, :], in0=work[b][:, (kt % 2) * SEQ:(kt % 2 + 1) * SEQ],
                            scalar=gain[:, g0 + kt:g0 + kt + 1], in1=act_head[:, kt, :].bitcast(F32),
                            op0=ALU.mult, op1=ALU.subtract)
                    ins.then_inc(act_rest_in.sem, 1)

            def rope(dst, src, table, heads, half, tmp, step):
                n = 2 * half
                cos, sin = table
                a = tmp[:, 0:heads * n].rearrange("p (h n) -> p h n", h=heads)
                b = tmp[:, 512:512 + heads * n].rearrange("p (h n) -> p h n", h=heads)
                tt(a, src, cos[:, None, :].to_broadcast([P, heads, n]), ALU.mult)
                tt(b[:, :, 0:half], src[:, :, half:n], sin[:, None, 0:half].to_broadcast([P, heads, half]), ALU.mult)
                step(tt(b[:, :, half:n], src[:, :, 0:half], sin[:, None, half:n].to_broadcast([P, heads, half]), ALU.mult))
                ins = tt(dst, a, b, ALU.add)
                return ins

            def table(name, dim, t):
                v = c[name].rearrange("p (a t n) -> p a t n", a=2, t=T)
                return v[:, 0, t, :], v[:, 1, t, :]

            def weights_max(l, base, n, scale, weights, banks, step):
                for h in range(HEADS):
                    dve.wait_ge(soft_out.sem, soft_out.at(l, base + h + 1))
                    step(tt(weights[:, h, :], banks[h][:, 0:BLK], c["causal"], ALU.add))
                    nc.vector.reduce_max(mx[:, 2 * n, 0, h:h + 1], weights[:, h, 0:P], AX_X)
                    step(nc.vector.reduce_max(mx[:, 2 * n, 1, h:h + 1], weights[:, h, P:BLK], AX_X))
                    ts(mx[:, 2 * n + 1, :, h], mx[:, 2 * n, :, h], -scale, None, ALU.mult).then_inc(soft_max.sem, 1)

            with dve.Fori(0, DEPTH) as l:
                step = Steps(dve, dve_step, l)
                norm_tokens(l, 0, step)
                split_rest(l, 0, 0, 0)
                act_rests(l, 0, G_MIX)
                ahead(l, C_WIDE1, 8)
                dve.wait_ge(chunk_done.sem, chunk_done.at(l, C_TALL))
                dve.wait_ge(small_in.sem, small_in.at(l, 32))
                for t in range(T):
                    ahead(l, C_TALL, 2, 2 * t)
                    src = acc[2 * t][:].rearrange("p (h n) -> p h n", n=HEAD_DIM)
                    dst = rot[:, t, :].rearrange("p (h n) -> p h n", n=HEAD_DIM)
                    ins = rope(dst, src, table("rope64", HEAD_DIM, t), 8, HEAD_DIM // 2, spare, step)
                    if t == 0:
                        step(ins)
                ins.then_inc(rot_ready.sem, 1)
                ahead(l, C_TALL, 4, 4)
                ahead(l, C_WIDE2, 4)
                decay = c["decay"].rearrange("p (h n) -> p h n", h=HEADS)
                for h in range(HEADS):
                    dve.wait_ge(sa_out.sem, sa_out.at(l, h + 1))
                    tt(wt[0][:, h, :], work[h][:, 0:BLK], decay[:, h, :], ALU.mult).then_inc(wa_ready.sem, 1)
                ahead(l, C_WIDE2, 1, 4)
                dve.wait_ge(lc_ready.sem, lc_ready.at(l, 1))
                step(nc.vector.scalar_tensor_tensor(out=za[:, :, :], in0=zs[:, :, :], scalar=0.0, in1=za[:, :, :],
                                                    op0=ALU.max, op1=ALU.add))
                strict = c["strict"][:, None, :].to_broadcast([P, HEADS, BLK])
                tt(za[:, :, :], za[:, :, :], strict, ALU.mult).then_inc(sp_ready.sem, 1)
                ahead(l, C_WIDE2, 3, 5)
                dve.wait_ge(chunk_done.sem, chunk_done.at(l, C_OUT))
                for n in range(2):
                    ins = nc.vector.tensor_copy(g2[:, 1, n * 512:(n + 1) * 512], acc[2 + n][:])
                ins.then_inc(g2_dve.sem, 1)
                dve.wait_ge(g2_dve.sem, g2_dve.at(l, 1))
                dve.wait_ge(g2_act.sem, g2_act.at(l, 1))
                tt(lf[:, 0, :, :], g2[:, :, FF:FF + HEADS],
                   gain[:, None, G_BF:G_BF + HEADS].to_broadcast([P, T, HEADS]), ALU.add).then_inc(ff_ready.sem, 1)
                for t in range(T):
                    src = g2[:, t, None, KR:KR + MLA_ROPE]
                    ins = rope(krot[:, t, None, :], src, table("rope32", MLA_ROPE, t), 1, MLA_ROPE // 2, spare, step)
                    if t == 0:
                        step(ins)
                ins.then_inc(krot_ready.sem, 1)
                dve.wait_ge(cstd_ready.sem, cstd_ready.at(l, 1))
                step(nc.vector.reciprocal(css[:, 1, :, :], css[:, 1, :, :]))
                for t in range(T):
                    ts(cn[:, t, 0:256], g2[:, t, CQ:CKV], css[:, 1, 0, t:t + 1], None, ALU.mult)
                    ins = ts(cn[:, t, 256:384], g2[:, t, CKV:KR], css[:, 1, 1, t:t + 1], None, ALU.mult)
                ins.then_inc(cn_ready.sem, 1)
                for h in range(HEADS):
                    dve.wait_ge(cum_out.sem, cum_out.at(l, h + 1))
                    tt(zs[:, h, :], zs[:, h, :], work[h][:, 0:BLK], ALU.subtract).then_inc(logw_ready.sem, 1)
                dve.wait_ge(ffl_ready.sem, ffl_ready.at(l, 1))
                nc.vector.scalar_tensor_tensor(out=lf[:, 0, :, :], in0=lf[:, 0, :, :], scalar=0.0, in1=lf[:, 1, :, :],
                                               op0=ALU.min, op1=ALU.subtract).then_inc(ls_ready.sem, 1)
                step(nc.vector.memset(fc[:, :, :], 1.0))
                dve.wait_ge(fcum_out.sem, fcum_out.at(l, 1))
                cum = acc[0][:, 0:2 * HEADS].rearrange("p (t h) -> p t h", t=T)
                ts(fc[:, :, 0:HEADS], cum, 1.0 / SCALE, None, ALU.mult)
                ts(fc[:, :, 8 + HEADS:16], cum, -1.0 / SCALE, None, ALU.mult).then_inc(fc_ready.sem, 1)
                dve.wait_ge(fc_turned.sem, fc_turned.at(l, 1))
                step(nc.vector.tensor_copy(fc_t[0:8, :], acc[1][0:8, :]))
                for h in range(HEADS):
                    ins = ts(fc_h[0:8, h, :], fc_t[0:8, 0:SEQ], c["pick"][0:8, h:h + 1], None, ALU.mult)
                ins.then_inc(fc_t_ready.sem, 1)
                dve.wait_ge(ew_ready.sem, ew_ready.at(l, 1))
                tt(wt[2][:, :, :], za[:, :, :], strict, ALU.mult).then_inc(wc_ready.sem, 1)
                dve.wait_ge(mla_out.sem, mla_out.at(l, 2))
                for t in range(T):
                    src = acc[t][:, 0:HEADS * MLA_QK].rearrange("p (h n) -> p h n", h=HEADS)
                    nc.vector.tensor_copy(mla_q[:, t, :, 0:HEAD_DIM], src[:, :, 0:HEAD_DIM])
                    ins = rope(mla_q[:, t, :, HEAD_DIM:MLA_QK], src[:, :, HEAD_DIM:MLA_QK],
                               table("rope32", MLA_ROPE, t), HEADS, MLA_ROPE // 2, spare, step)
                    if t == 0:
                        step(ins)
                ins.then_inc(mla_q_ready.sem, 1)
                weights_max(l, 0, 0, SCALE, soft, work, step)
                weights_max(l, HEADS, 1, SCALE_MLA, soft_l, acc, step)

                def heads(v):
                    return v.rearrange("p (t h d) -> p t h d", t=T, d=HEAD_DIM)

                def each(v):
                    return v.rearrange("p (t h) -> p t h", t=T)[:, :, :, None].to_broadcast([P, T, HEADS, HEAD_DIM])

                def output(g):
                    return xn[:, :, g * GROUP_WIDTH:(g + 1) * GROUP_WIDTH].rearrange("p t (h d) -> p t h d", d=HEAD_DIM)

                def sum_squares(g):
                    step(tt(heads(ysq[:, g, :]), output(g), output(g), ALU.mult))
                    return nc.vector.reduce_sum(hss[:, 0, 8 * g:8 * g + 8],
                                                ysq[:, g, :].rearrange("p (n d) -> p n d", d=HEAD_DIM), AX_X)

                def over_sum(g, n):
                    step(nc.vector.reciprocal(dn[:, 2 * n + 1, :, :], dn[:, 2 * n, :, :]))
                    return tt(output(g), heads(acc[g][:]), each(dn[:, 2 * n + 1, :, :].rearrange("p t h -> p (t h)")),
                              ALU.mult)

                def over_rms(g):
                    return tt(output(g), output(g), each(hss[:, 1, 8 * g:8 * g + 8]), ALU.mult)

                dve.wait_ge(o_out.sem, o_out.at(l, 1))
                step(nc.vector.reduce_sum(mean[:, 0, :], acc[0][:].rearrange("p (n d) -> p n d", d=HEAD_DIM), AX_X))
                step(ts(mean[:, 1, :], mean[:, 0, :], 1.0 / HEAD_DIM, None, ALU.mult))
                step(tt(output(0), heads(acc[0][:]), each(mean[:, 1, :]), ALU.subtract))
                sum_squares(0)
                dve.wait_ge(o_out.sem, o_out.at(l, 2))
                step(nc.vector.tensor_copy(output(2), heads(acc[2][:])))
                sum_squares(2)
                dve.wait_ge(o_out.sem, o_out.at(l, 3))
                step(over_sum(1, 0))
                sum_squares(1).then_inc(hss_ready.sem, 1)
                dve.wait_ge(hstd_ready.sem, hstd_ready.at(l, 1))
                step(nc.vector.reciprocal(hss[:, 1, 0:24], hss[:, 1, 0:24]))
                step(over_rms(0))
                tt(xn[:, :, 0:GROUP_WIDTH], xn[:, :, 0:GROUP_WIDTH], rg[:, :, :], ALU.mult)
                over_rms(1)
                over_rms(2).then_inc(heads_ready.sem, 1)
                dve.wait_ge(o_out.sem, o_out.at(l, 4))
                over_sum(3, 1).then_inc(o_read.sem, 1)
                act_rests(l, 1, G_HEAD, range(3))
                dve.wait_ge(o_read.sem, o_read.at(l, 1))
                sum_squares(3).then_inc(hss_ready.sem, 1)
                dve.wait_ge(hstd_ready.sem, hstd_ready.at(l, 2))
                step(nc.vector.reciprocal(hss[:, 1, 24:32], hss[:, 1, 24:32]))
                over_rms(3).then_inc(heads_ready.sem, 1)

                ahead(l, C_OUT, 2)
                act_rests(l, 1, G_HEAD, range(3, 4))
                ahead(l, C_OUT, 6, 2)

                def add_residual(done, added):
                    dve.wait_ge(chunk_done.sem, chunk_done.at(l, done))
                    for t in range(T):
                        for n in range(2):
                            x_part = xs[:, t, n * 512:(n + 1) * 512]
                            ins = tt(x_part, x_part, acc[2 * t + n][:], ALU.add)
                        ins.then_inc(added.sem, 1)

                add_residual(C_QUERY, x_mid)

                dve.wait_ge(x_mid.sem, x_mid.at(l, T))
                norm_tokens(l, 1, step)
                act_rests(l, 2, G_FFN)
                with dve.Fori(0, 4) as k:
                    ahead(l, C_QUERY + k * 4, 4)
                dve.wait_ge(score_in.sem, score_in.at(l, 8))
                after_register_wait(dve)
                def route(u, c0, j0):
                    marks = [0]

                    def mark(ins):
                        ins.then_inc(route_step.sem, 1)
                        marks[0] += 1
                        return marks[0]

                    def seen(n):
                        dve.wait_ge(route_step.sem, l * route_step.per + u * ROUTE_STEPS + n)
                        after_register_wait(dve)

                    vec = nc.vector
                    first_s, second_s = stage[:, 0, :], stage[:, 1, :]
                    ahead(l, c0, 1, j0)
                    dve.wait_ge(staged.sem, staged.at(l, u + 1))
                    after_register_wait(dve)
                    a = mark(vec.max(top_v[:, 0, 0:8], first_s))
                    b = mark(vec.max(top_v[:, 1, 0:8], second_s))
                    seen(a)
                    vec.max_index(top_i[:, 0, 0:8], top_v[:, 0, 0:8], first_s)
                    a = mark(vec.match_replace(left[:, 0, :], top_v[:, 0, 0:8], first_s, NEG_OUT))
                    seen(b)
                    vec.max_index(top_i[:, 1, 0:8], top_v[:, 1, 0:8], second_s)
                    b = mark(vec.match_replace(left[:, 1, :], top_v[:, 1, 0:8], second_s, NEG_OUT))
                    seen(a)
                    a = mark(vec.max(top_v[:, 0, 8:16], left[:, 0, :]))
                    seen(b)
                    b = mark(vec.max(top_v[:, 1, 8:16], left[:, 1, :]))
                    ahead(l, c0, 1, j0 + 1)
                    seen(b)
                    vec.max_index(top_i[:, 0, 8:16], top_v[:, 0, 8:16], left[:, 0, :])
                    a = mark(vec.max_index(top_i[:, 1, 8:16], top_v[:, 1, 8:16], left[:, 1, :]))
                    b = mark(tt(cand[:, :].rearrange("p (a b) -> p a b", a=TOPK),
                                top_v[:, 0, :, None].to_broadcast([P, TOPK, TOPK]),
                                top_v[:, 1, None, :].to_broadcast([P, TOPK, TOPK]), ALU.add))
                    ahead(l, c0, 1, j0 + 2)
                    seen(a)
                    vec.tensor_copy(top_f[:, :, :], top_i[:, :, :])
                    seen(b)
                    a = mark(vec.max(best_v[:, 0:8], cand[:, :]))
                    seen(a)
                    vec.max_index(best_i[:, 0:8], best_v[:, 0:8], cand[:, :])
                    left_c = left[:, :, :].rearrange("p a n -> p (a n)")
                    a = mark(vec.match_replace(left_c, best_v[:, 0:8], cand[:, :], NEG_OUT))
                    ahead(l, c0, 1, j0 + 3)
                    seen(a)
                    a = mark(vec.max(best_v[:, 8:16], left_c))
                    seen(a)
                    seen(mark(vec.max_index(best_i[:, 8:16], best_v[:, 8:16], left_c)))
                    ts(rank_i[:, 0, :], best_i[:, :], 4, None, ALU.logical_shift_right)
                    a = mark(ts(rank_i[:, 1, :], best_i[:, :], 15, None, ALU.bitwise_and))
                    flat = picked[:, :, :, :].rearrange("p a t n -> p a (t n)")[:, :, bass.ds(u * TOPK, TOPK)]
                    ts(flat[:, 2, :], best_v[:, :], best_v[:, 0:1], None, ALU.subtract)
                    ahead(l, c0, 1, j0 + 4)
                    seen(a)
                    seen(mark(vec.tensor_copy(rank_f[:, :, :], rank_i[:, :, :])))
                    m = match[:, :, :].rearrange("p a (k r) -> p (a k) r", k=TOPK)
                    seen(mark(tt(m, rank_f[:, :, :].rearrange("p a k -> p (a k)")[:, :, None]
                                 .to_broadcast([P, 2 * TOPK, TOPK]),
                                 iota[:, None, 0:TOPK].to_broadcast([P, 2 * TOPK, TOPK]), ALU.is_equal)))
                    m = match[:, :, :].rearrange("p a (k r) -> p a k r", k=TOPK)
                    a = mark(tt(m, m, top_f[:, :, None, :].to_broadcast([P, 2, TOPK, TOPK]), ALU.mult))
                    ahead(l, c0, 1, j0 + 5)
                    seen(a)
                    vec.reduce_sum(flat[:, 0:2, :], m, AX_X).then_inc(unit_done.sem, 1)
                    assert marks[0] == ROUTE_STEPS, marks[0]
                with dve.Fori(0, UNITS // 2) as w:
                    for k in range(2):
                        route(2 * w + k, C_U + 2 * STRIDE * w, k * STRIDE)
                ahead(l, C_U + UNITS * STRIDE, 4)
                gate = picked[:, 2, :, :].rearrange("p t (h k) -> p (t h) k", k=TOPK)
                gsum = gs[:, :, :, :].rearrange("p a t h -> p a (t h)")
                dve.wait_ge(gate_exp.sem, gate_exp.at(l, 1))
                step(nc.vector.reduce_sum(gsum[:, 0, :], gate, AX_X))
                step(nc.vector.reciprocal(gsum[:, 1, :], gsum[:, 0, :]))
                tt(gate, gate, gsum[:, 1, :, None].to_broadcast([P, UNITS, TOPK]), ALU.mult).then_inc(gates_done.sem, 1)
                with dve.Fori(UNITS * STRIDE // 4 + 1, TURN_AT // 4) as u:
                    ahead(l, C_U + u * 4, 4)
                dve.wait_ge(picked_turned.sem, picked_turned.at(l, 1))
                nc.vector.tensor_copy(picked_t[:, 0:2, :], work[2][:].rearrange("p (a s) -> p a s", a=2))
                ts(picked_t[:, 3, :], work[3][:, 0:SEQ], -1.0, None, ALU.mult)
                nc.vector.tensor_copy(picked_t[:, 2, :], work[3][:, 0:SEQ]).then_inc(picked_t_in.sem, 1)
                after_register_wait(dve)
                with dve.Fori(TURN_AT // 4, E_TILES // 4) as u:
                    ahead(l, C_U + u * 4, 4)
                dve.wait_ge(chunk_done.sem, chunk_done.at(l, C_V))
                dve.wait_ge(picked_t_in.sem, picked_t_in.at(l, 1))
                after_register_wait(dve)

                def make_hot(g, b):
                    tt(hot1[:, b, :, :], iota[:, None, :].to_broadcast([P, 4, P]),
                       picked_t[:, 0, bass.ds(4 * g, 4), None].to_broadcast([P, 4, P]), ALU.is_equal)
                    for q in range(2):
                        tok = bass.ds(4 * g + q, 1)
                        ins = ts(hot2[:, b, q, :], iota, picked_t[:, 1, tok], picked_t[:, 2, tok],
                                 ALU.is_equal, ALU.mult)
                    ins.then_inc(hot_ready.sem, 1)

                def apply_gates(g, b):
                    dve.wait_ge(gate_out.sem, gate_out.at(l, g + 1))
                    a = acts[:, :, bass.ds(4 * g, 4)]
                    tt(a, a, work[2 + b][:].rearrange("p (q i) -> p i q", q=4), ALU.mult).then_inc(gate_used.sem, 1)

                make_hot(0, 0)
                with dve.Fori(0, GROUPS // 2 - 1) as u:
                    for b in range(2):
                        make_hot(2 * u + (b + 1), 1 - b)
                        apply_gates(2 * u + b, b)
                make_hot(GROUPS - 1, 1)
                apply_gates(GROUPS - 2, 0)
                apply_gates(GROUPS - 1, 1)

                def weight_rest(i, slot):
                    dve.wait_ge(w_head_in.sem, w_head_in.at(l, i + 1))
                    dve.wait_ge(chunk_done.sem, chunk_done.at(l, C_V + i - 1))
                    tt(w_rest[:, slot, :], acts[:, i, :], w_head[:, slot, :].bitcast(F32), ALU.subtract)\
                        .then_inc(w_rest_in.sem, 1)

                def v_block(i0, last):
                    for j in range(3 if last else 4):
                        ahead(l, C_V + i0, 1, j)
                        weight_rest(i0 + (j + 1), (j + 1) % 2)

                weight_rest(0, 0)
                with dve.Fori(0, E_TILES // 4 - 1) as v:
                    v_block(4 * v, False)
                v_block(E_TILES - 4, True)
                add_residual(CHUNKS, x_ready)
                assert step.n == DVE_STEPS, step.n
            dve.wait_ge(fixed_in.sem, 32)
            for t in range(T):
                dve.wait_ge(std_ready.sem, std_ready.at(DEPTH, t + 1))
                nc.vector.reciprocal(ss[:, 1, t:t + 1], ss[:, 1, t:t + 1]).then_inc(dve_step.sem, 1)
                dve.wait_ge(dve_step.sem, dve_step.at(DEPTH, t + 1))
                nc.vector.scalar_tensor_tensor(out=xs[:, t, :], in0=xs[:, t, :], scalar=ss[:, 1, t:t + 1],
                                               in1=gain_row, op0=ALU.mult, op1=ALU.mult).then_inc(final_ready.sem, 1)


def stream_layout(w_in, w_out, w_query, expert_u, expert_v):
    w = GROUP_WIDTH
    cols = np.cumsum([0] + [w] * 7 + [HEADS] + [w] * 3 + [MLA_Q_RANK, MLA_KV_RANK, MLA_ROPE])
    rq, rk, rv, rg, fq, fk, fv, ff, sq, sk, sv, cq, ckv, kr = (
        w_in[:, a:b] for a, b in zip(cols[:-1], cols[1:]))

    def wide(m):
        return m.reshape(-1, P, CHUNK)

    def tall(m):
        return m.reshape(KT, P, -1, P).transpose(2, 1, 0, 3).reshape(-1, P, CHUNK)

    second = np.concatenate([fv, sv, cq, ckv, kr, ff], 1)
    second = np.pad(second, ((0, 0), (0, D_MODEL - second.shape[1])))
    experts = expert_u.reshape(E_TILES, P, KT, P).transpose(0, 3, 2, 1).reshape(-1, P, CHUNK)
    chunks = np.concatenate([
        wide(np.concatenate([rq, rk, rv, rg], 1)), tall(np.concatenate([fq, fk, sq, sk], 1)),
        wide(second), wide(w_out), tall(w_query), experts, wide(expert_v)])
    return chunks.reshape(PAIRS, 2, P, CHUNK).transpose(0, 2, 1, 3)


def kernel(x, norm_mix, w_in, b_forget, norm_cq, norm_ckv, w_uq, w_ukv, head_gain, w_out,
           norm_ffn, w_query, sub_keys, expert_u, expert_v, norm_final):
    import concourse.bacc as bacc
    from concourse.bass_utils import run_bass_kernel_spmd

    def a(v):
        return np.asarray(v)

    def per_partition(v):
        return a(v).reshape(DEPTH, -1, P).transpose(0, 2, 1)

    stream = np.concatenate([stream_layout(a(w_in)[l], a(w_out)[l], a(w_query)[l], a(expert_u)[l], a(expert_v)[l])
                             for l in range(DEPTH)])
    gains = np.concatenate([
        per_partition(norm_mix), per_partition(head_gain), per_partition(norm_ffn), per_partition(norm_cq),
        per_partition(norm_ckv), np.broadcast_to(a(b_forget)[:, None, :], (DEPTH, P, HEADS))], 2)
    small = np.concatenate([
        a(w_uq).reshape(DEPTH, 2, P, -1).transpose(0, 2, 1, 3).reshape(DEPTH, P, -1), a(w_ukv),
        a(sub_keys).transpose(0, 4, 1, 2, 3).reshape(DEPTH, P, -1)], 2)
    tables = constants()
    arrays = {
        "x": a(x).reshape(T, P, D_MODEL).transpose(1, 0, 2),
        "stream": stream,
        "gains": gains,
        "small": small,
        "mixer_consts": np.concatenate([tables[n] for n, _ in MIXER_CONSTS], 1),
        "fixed_consts": np.concatenate([np.eye(P), np.tile(np.arange(P), (P, 1))], 1),
        "gain_final": a(norm_final).reshape(1, D_MODEL),
    }
    arrays = {n: np.ascontiguousarray(v, dtype=np.float32) for n, v in arrays.items()}
    nc = bacc.Bacc("TRN2", target_bir_lowering=False, num_devices=1)
    args = {n: nc.dram_tensor(n, v.shape, F32, kind="ExternalInput").ap() for n, v in arrays.items()}
    out = nc.dram_tensor("out", (P, T, D_MODEL), F32, kind="ExternalOutput").ap()
    hybrid_ret_fox_sb_mla_peer(nc, **args, out=out)
    r = run_bass_kernel_spmd(nc, [arrays], core_ids=[0])
    return r.results[0]["out"].transpose(1, 0, 2).reshape(1, SEQ, D_MODEL)
```
